# Optimizing a Trainium2 kernel written in Bass

```python
import jax, jax.numpy as jnp
from jax import lax
import numpy as np
import math

D_MODEL = 1024
BATCH = 1
SEQ = 256
DEPTH = 2

N_HEADS = 16
HEAD_DIM = D_MODEL // N_HEADS
ROPE_THETA = 10000.0
NORM_EPS = 1e-6
PLE_DIM = 256
N_MIXERS = 2
N_MOBA_LAYERS = (DEPTH + 1) // 2
N_NSA_LAYERS = DEPTH // 2
NEG_INF = -1e30
FORCE_SCORE = 1e30

MOBA_BLOCK = 256
MOBA_TOPK = 3
MOBA_Q_CHUNK = 16
MOBA_IN = 4 * D_MODEL

NSA_KV_GROUPS = 4
NSA_HEADS_PER_GROUP = N_HEADS // NSA_KV_GROUPS
NSA_KV_DIM = NSA_KV_GROUPS * HEAD_DIM
NSA_N_BRANCH = 3
CMP_LEN = 32
CMP_STRIDE = 16
CMP_HIDDEN = 4 * HEAD_DIM
SEL_BLOCK = 64
SEL_TOPN = 16
WINDOW = 512
NSA_Q_CHUNK = 64
NSA_IN = D_MODEL + 2 * NSA_N_BRANCH * NSA_KV_DIM + NSA_N_BRANCH * N_HEADS + D_MODEL


def rms_norm(x, gain):
    xf = x.astype(jnp.float32)
    y = xf * lax.rsqrt(jnp.mean(xf * xf, axis=-1, keepdims=True) + NORM_EPS)
    return (y * gain.astype(jnp.float32)).astype(x.dtype)

def rope(x, pos):
    half = HEAD_DIM // 2
    inv_freq = ROPE_THETA ** (-jnp.arange(half, dtype=jnp.float32) / half)
    ang = pos.astype(jnp.float32)[..., None] * inv_freq
    cos, sin = jnp.cos(ang), jnp.sin(ang)
    xf = x.astype(jnp.float32)
    x1, x2 = xf[..., :half], xf[..., half:]
    return jnp.concatenate([x1 * cos - x2 * sin, x2 * cos + x1 * sin], axis=-1).astype(x.dtype)

def masked_softmax(s, mask):
    s = jnp.where(mask, s.astype(jnp.float32), NEG_INF)
    return jnp.where(mask, jax.nn.softmax(s, axis=-1), 0.0)

def split_heads(x, n):
    B, T, _ = x.shape
    return x.reshape(B, T, n, HEAD_DIM).transpose(0, 2, 1, 3)

def merge_heads(x):
    B, H, T, d = x.shape
    return x.transpose(0, 2, 1, 3).reshape(B, T, H * d)

def moba_attention(q, k, v):
    B, H, T, _ = q.shape
    nb = -(-T // MOBA_BLOCK)
    Tp = nb * MOBA_BLOCK
    pad = ((0, 0), (0, 0), (0, Tp - T), (0, 0))
    q, k, v = jnp.pad(q, pad), jnp.pad(k, pad), jnp.pad(v, pad)
    kb = k.reshape(B, H, nb, MOBA_BLOCK, HEAD_DIM)
    vb = v.reshape(B, H, nb, MOBA_BLOCK, HEAD_DIM)
    k_mean = kb.astype(jnp.float32).mean(axis=3).astype(k.dtype)
    q_blk = jnp.arange(Tp) // MOBA_BLOCK
    gate = jnp.einsum('bhtd,bhnd->bhtn', q, k_mean).astype(jnp.float32)
    past = jnp.arange(nb)[None, :] < q_blk[:, None]
    gate = jnp.where(past, gate, NEG_INF)
    topk = min(MOBA_TOPK, nb)
    g_val, g_idx = lax.top_k(gate, topk)
    g_valid = g_val > 0.5 * NEG_INF
    scale = HEAD_DIM ** -0.5
    C = MOBA_Q_CHUNK
    b_ix = jnp.arange(B)[:, None, None, None]
    h_ix = jnp.arange(H)[None, :, None, None]

    def chunk(c):
        s0 = c * C
        qc = lax.dynamic_slice_in_dim(q, s0, C, axis=2)
        idx = lax.dynamic_slice_in_dim(g_idx, s0, C, axis=2)
        valid = lax.dynamic_slice_in_dim(g_valid, s0, C, axis=2)
        k_sel = kb[b_ix, h_ix, idx]
        v_sel = vb[b_ix, h_ix, idx]
        s_sel = jnp.einsum('bhcd,bhcnkd->bhcnk', qc, k_sel).reshape(B, H, C, topk * MOBA_BLOCK)
        m_sel = jnp.broadcast_to(valid[..., None], (B, H, C, topk, MOBA_BLOCK)).reshape(B, H, C, topk * MOBA_BLOCK)
        blk0 = (s0 // MOBA_BLOCK) * MOBA_BLOCK
        k_own = lax.dynamic_slice_in_dim(k, blk0, MOBA_BLOCK, axis=2)
        v_own = lax.dynamic_slice_in_dim(v, blk0, MOBA_BLOCK, axis=2)
        s_own = jnp.einsum('bhcd,bhkd->bhck', qc, k_own)
        q_pos = s0 + jnp.arange(C)
        k_pos = blk0 + jnp.arange(MOBA_BLOCK)
        m_own = jnp.broadcast_to(k_pos[None, :] <= q_pos[:, None], (B, H, C, MOBA_BLOCK))
        s = jnp.concatenate([s_sel, s_own], axis=-1) * scale
        m = jnp.concatenate([m_sel, m_own], axis=-1)
        pr = masked_softmax(s, m).astype(v.dtype)
        p_sel = pr[..., :topk * MOBA_BLOCK].reshape(B, H, C, topk, MOBA_BLOCK)
        p_own = pr[..., topk * MOBA_BLOCK:]
        return (jnp.einsum('bhcnk,bhcnkd->bhcd', p_sel, v_sel)
                + jnp.einsum('bhck,bhkd->bhcd', p_own, v_own))

    out = lax.map(chunk, jnp.arange(Tp // C))
    out = out.transpose(1, 2, 0, 3, 4).reshape(B, H, Tp, HEAD_DIM)
    return out[:, :, :T]

def moba_layer(h, w_in, q_gain, k_gain, w_out, pos):
    q, k, v, z = jnp.split(h @ w_in, 4, axis=-1)
    q = rope(rms_norm(split_heads(q, N_HEADS), q_gain), pos)
    k = rope(rms_norm(split_heads(k, N_HEADS), k_gain), pos)
    v = split_heads(v, N_HEADS)
    o = merge_heads(moba_attention(q, k, v)) * jax.nn.silu(z)
    return o @ w_out

def compress(x, pe, w1, w2):
    B, G, T, _ = x.shape
    nc = (T - CMP_LEN) // CMP_STRIDE + 1
    idx = np.arange(nc)[:, None] * CMP_STRIDE + np.arange(CMP_LEN)[None, :]
    blocks = x[:, :, idx] + pe
    flat = blocks.reshape(B, G, nc, CMP_LEN * HEAD_DIM)
    return jax.nn.gelu(flat @ w1) @ w2

def selection_overlap(nc, ns):
    c_start = np.arange(nc) * CMP_STRIDE
    s_start = np.arange(ns) * SEL_BLOCK
    ovl = (c_start[:, None] < s_start[None, :] + SEL_BLOCK) & (c_start[:, None] + CMP_LEN > s_start[None, :])
    return jnp.asarray(ovl.astype(np.float32))

def nsa_attention(q, kc, vc, ks, vs, kw, vw, g):
    B, H, T, _ = q.shape
    G, R, C = NSA_KV_GROUPS, NSA_HEADS_PER_GROUP, NSA_Q_CHUNK
    q = q.reshape(B, G, R, T, HEAD_DIM)
    g = g.reshape(B, G, R, T, NSA_N_BRANCH)
    nc = kc.shape[2]
    ns = T // SEL_BLOCK
    topn = min(SEL_TOPN, ns)
    cmp_end = jnp.arange(nc) * CMP_STRIDE + CMP_LEN - 1
    ovl = selection_overlap(nc, ns)
    ksb = ks.reshape(B, G, ns, SEL_BLOCK, HEAD_DIM)
    vsb = vs.reshape(B, G, ns, SEL_BLOCK, HEAD_DIM)
    wpad = ((0, 0), (0, 0), (WINDOW, 0), (0, 0))
    kw_pad, vw_pad = jnp.pad(kw, wpad), jnp.pad(vw, wpad)
    scale = HEAD_DIM ** -0.5
    b_ix = jnp.arange(B)[:, None, None, None]
    g_ix = jnp.arange(G)[None, :, None, None]
    blk = jnp.arange(ns)

    def chunk(c):
        s0 = c * C
        qc = lax.dynamic_slice_in_dim(q, s0, C, axis=3)
        gc = lax.dynamic_slice_in_dim(g, s0, C, axis=3)
        q_pos = s0 + jnp.arange(C)
        s_c = jnp.einsum('bgrcd,bgnd->bgrcn', qc, kc) * scale
        p_c = masked_softmax(s_c, cmp_end[None, :] <= q_pos[:, None])
        o_c = jnp.einsum('bgrcn,bgnd->bgrcd', p_c.astype(vc.dtype), vc)
        imp = jnp.einsum('bgrcn,ns->bgcs', p_c, ovl)
        own = q_pos // SEL_BLOCK
        forced = (blk[None, :] == 0) | (blk[None, :] == own[:, None]) | (blk[None, :] == own[:, None] - 1)
        causal = blk[None, :] <= own[:, None]
        imp = jnp.where(forced, FORCE_SCORE, jnp.where(causal, imp, NEG_INF))
        val, idx = lax.top_k(imp, topn)
        valid = val > 0.5 * NEG_INF
        k_sel = ksb[b_ix, g_ix, idx]
        v_sel = vsb[b_ix, g_ix, idx]
        s_s = jnp.einsum('bgrcd,bgcnkd->bgrcnk', qc, k_sel).reshape(B, G, R, C, topn * SEL_BLOCK) * scale
        k_pos = idx[..., None] * SEL_BLOCK + jnp.arange(SEL_BLOCK)
        m_s = valid[..., None] & (k_pos <= q_pos[None, None, :, None, None])
        p_s = masked_softmax(s_s, m_s.reshape(B, G, 1, C, topn * SEL_BLOCK))
        p_s = p_s.reshape(B, G, R, C, topn, SEL_BLOCK).astype(v_sel.dtype)
        o_s = jnp.einsum('bgrcnk,bgcnkd->bgrcd', p_s, v_sel)
        k_w = lax.dynamic_slice_in_dim(kw_pad, s0, C + WINDOW, axis=2)
        v_w = lax.dynamic_slice_in_dim(vw_pad, s0, C + WINDOW, axis=2)
        s_w = jnp.einsum('bgrcd,bgkd->bgrck', qc, k_w) * scale
        k_pos_w = s0 - WINDOW + jnp.arange(C + WINDOW)
        diff = q_pos[:, None] - k_pos_w[None, :]
        m_w = (diff >= 0) & (diff < WINDOW) & (k_pos_w[None, :] >= 0)
        o_w = jnp.einsum('bgrck,bgkd->bgrcd', masked_softmax(s_w, m_w).astype(v_w.dtype), v_w)
        return gc[..., 0:1] * o_c + gc[..., 1:2] * o_s + gc[..., 2:3] * o_w

    out = lax.map(chunk, jnp.arange(T // C))
    return out.transpose(1, 2, 3, 0, 4, 5).reshape(B, H, T, HEAD_DIM)

def nsa_layer(h, w_in, q_gain, k_gain, cmp_pe, cmp_w1, cmp_w2, w_out, pos):
    B, T, _ = h.shape
    offs = np.cumsum([D_MODEL] + [NSA_KV_DIM] * 6 + [NSA_N_BRANCH * N_HEADS]).tolist()
    q, kc, vc, ks, vs, kw, vw, gl, z = jnp.split(h @ w_in, offs, axis=-1)
    q = rope(rms_norm(split_heads(q, N_HEADS), q_gain), pos)
    kc = compress(split_heads(kc, NSA_KV_GROUPS), cmp_pe[0], cmp_w1[0], cmp_w2[0])
    vc = compress(split_heads(vc, NSA_KV_GROUPS), cmp_pe[1], cmp_w1[1], cmp_w2[1])
    cmp_pos = jnp.arange(kc.shape[2]) * CMP_STRIDE + CMP_LEN - 1
    kc = rope(rms_norm(kc, k_gain[0]), cmp_pos)
    ks = rope(rms_norm(split_heads(ks, NSA_KV_GROUPS), k_gain[1]), pos)
    kw = rope(rms_norm(split_heads(kw, NSA_KV_GROUPS), k_gain[2]), pos)
    vs = split_heads(vs, NSA_KV_GROUPS)
    vw = split_heads(vw, NSA_KV_GROUPS)
    g = jax.nn.sigmoid(gl).reshape(B, T, N_HEADS, NSA_N_BRANCH).transpose(0, 2, 1, 3)
    o = merge_heads(nsa_attention(q, kc, vc, ks, vs, kw, vw, g)) * jax.nn.silu(z)
    return o @ w_out

def first_inputs(seed: int = 0) -> dict:
    key = jax.random.key(seed)
    ks = jax.random.split(key, 17)
    f32 = jnp.float32

    def nrm(k, shape, scale):
        return jax.random.normal(k, shape, f32) * scale

    def gain(k, shape):
        return 1.0 + 0.01 * jax.random.normal(k, shape, f32)

    return {
        "x": nrm(ks[0], (BATCH, SEQ, D_MODEL), 1.0),
        "p": nrm(ks[1], (DEPTH, BATCH, SEQ, PLE_DIM), 1.0),
        "norm_gain": gain(ks[2], (DEPTH, D_MODEL)),
        "moba_w_in": nrm(ks[3], (N_MOBA_LAYERS, D_MODEL, MOBA_IN), D_MODEL ** -0.5),
        "moba_q_gain": gain(ks[4], (N_MOBA_LAYERS, HEAD_DIM)),
        "moba_k_gain": gain(ks[5], (N_MOBA_LAYERS, HEAD_DIM)),
        "moba_w_out": nrm(ks[6], (N_MOBA_LAYERS, D_MODEL, D_MODEL), D_MODEL ** -0.5),
        "nsa_w_in": nrm(ks[7], (N_NSA_LAYERS, D_MODEL, NSA_IN), D_MODEL ** -0.5),
        "nsa_q_gain": gain(ks[8], (N_NSA_LAYERS, HEAD_DIM)),
        "nsa_k_gain": gain(ks[9], (N_NSA_LAYERS, NSA_N_BRANCH, HEAD_DIM)),
        "nsa_cmp_pe": nrm(ks[10], (N_NSA_LAYERS, 2, CMP_LEN, HEAD_DIM), 0.1),
        "nsa_cmp_w1": nrm(ks[11], (N_NSA_LAYERS, 2, CMP_LEN * HEAD_DIM, CMP_HIDDEN), (CMP_LEN * HEAD_DIM) ** -0.5),
        "nsa_cmp_w2": nrm(ks[12], (N_NSA_LAYERS, 2, CMP_HIDDEN, HEAD_DIM), CMP_HIDDEN ** -0.5),
        "nsa_w_out": nrm(ks[13], (N_NSA_LAYERS, D_MODEL, D_MODEL), D_MODEL ** -0.5),
        "ple_w_proj": nrm(ks[14], (DEPTH, PLE_DIM, D_MODEL), PLE_DIM ** -0.5),
        "ple_gate_gain": gain(ks[15], (DEPTH, D_MODEL)),
        "ple_w_gate": nrm(ks[16], (DEPTH, D_MODEL, D_MODEL), D_MODEL ** -0.5),
    }

def first_block(x, p, norm_gain, moba_w_in, moba_q_gain, moba_k_gain, moba_w_out,
              nsa_w_in, nsa_q_gain, nsa_k_gain, nsa_cmp_pe, nsa_cmp_w1, nsa_cmp_w2, nsa_w_out,
              ple_w_proj, ple_gate_gain, ple_w_gate):
    pos = jnp.arange(x.shape[1])
    for i in range(DEPTH):
        h = rms_norm(x, norm_gain[i])
        j = i // N_MIXERS
        if i % N_MIXERS == 0:
            x = x + moba_layer(h, moba_w_in[j], moba_q_gain[j], moba_k_gain[j], moba_w_out[j], pos)
        else:
            x = x + nsa_layer(h, nsa_w_in[j], nsa_q_gain[j], nsa_k_gain[j], nsa_cmp_pe[j],
                              nsa_cmp_w1[j], nsa_cmp_w2[j], nsa_w_out[j], pos)
        gate = jax.nn.sigmoid(rms_norm(x, ple_gate_gain[i]) @ ple_w_gate[i])
        x = x + gate * (p[i] @ ple_w_proj[i])
    return x


N_MEM = 256
RMS_EPS = 1e-6
MAX_POS_OFFSET = 1024
MASK_VALUE = -1e30

SSM_GROUPS = 32
SSM_GROUP_CH = 16
SSM_WIDTH = SSM_GROUPS * SSM_GROUP_CH
SSM_STATE = 64

MLA_HEADS = 8
MLA_Q_RANK = 512
MLA_KV_RANK = 256
MLA_NOPE = 64
MLA_ROPE = 32
MLA_V = 64
MLA_WIDTH = MLA_HEADS * MLA_V
Q_BLOCK = 128

HG_HEADS = 4
HG_DK = 128
HG_DV = 128
HG_WIDTH = HG_HEADS * HG_DK
HG_CHUNK = 64

X_HEADS = 4
X_HEAD_DIM = 128
X_WIDTH = X_HEADS * X_HEAD_DIM

D_FF = -(-(8 * D_MODEL) // (3 * 256)) * 256

N_BRANCH = 3
IN_SPLITS = [SSM_WIDTH, MLA_Q_RANK, MLA_KV_RANK, MLA_ROPE,
             HG_HEADS * HG_DK, HG_HEADS * HG_DK, HG_HEADS * HG_DV, HG_HEADS * HG_DV,
             N_BRANCH * D_MODEL]
D_IN = sum(IN_SPLITS)


def rmsnorm(x, g):
    xf = x.astype(jnp.float32)
    y = xf * lax.rsqrt(jnp.mean(xf * xf, axis=-1, keepdims=True) + RMS_EPS)
    return (y * g.astype(jnp.float32)).astype(x.dtype)

def rope_tables(positions):
    half = MLA_ROPE // 2
    inv_freq = ROPE_THETA ** (-jnp.arange(half, dtype=jnp.float32) / half)
    ang = positions.astype(jnp.float32)[..., None] * inv_freq
    return jnp.cos(ang), jnp.sin(ang)

def apply_rope(x, cos, sin):
    xf = x.astype(jnp.float32)
    x1, x2 = jnp.split(xf, 2, axis=-1)
    return jnp.concatenate([x1 * cos - x2 * sin, x2 * cos + x1 * sin], axis=-1).astype(x.dtype)

def s5_mixer(u, lam_re, lam_im, b_re, b_im, c_re, c_im, d_skip, log_step, w_glu):
    bsz, s, _ = u.shape
    uf = u.astype(jnp.float32).reshape(bsz, s, SSM_GROUPS, SSM_GROUP_CH)
    lam = lax.complex(lam_re.astype(jnp.float32), lam_im.astype(jnp.float32))
    step = jnp.exp(log_step.astype(jnp.float32))[:, None]
    lam_bar = jnp.exp(lam * step)
    b_mat = lax.complex(b_re.astype(jnp.float32), b_im.astype(jnp.float32))
    b_bar = ((lam_bar - 1.0) / lam)[..., None] * b_mat
    bu = jnp.einsum('bsgh,gph->bsgp', uf.astype(jnp.complex64), b_bar)
    a = jnp.broadcast_to(lam_bar, bu.shape)

    def combine(left, right):
        a_l, b_l = left
        a_r, b_r = right
        return a_r * a_l, a_r * b_l + b_r

    _, states = lax.associative_scan(combine, (a, bu), axis=1)
    c_mat = lax.complex(c_re.astype(jnp.float32), c_im.astype(jnp.float32))
    y = jnp.real(jnp.einsum('bsgp,ghp->bsgh', states, c_mat)) + d_skip.astype(jnp.float32) * uf
    y = jax.nn.gelu(y.reshape(bsz, s, SSM_WIDTH)).astype(u.dtype)
    z_out, z_gate = jnp.split(y @ w_glu, 2, axis=-1)
    return z_out * jax.nn.sigmoid(z_gate)

def blocked_causal_attention(q, k, v, scale):
    bsz, s, h, dqk = q.shape
    nb = s // Q_BLOCK
    qb = q.reshape(bsz, nb, Q_BLOCK, h, dqk).transpose(1, 0, 2, 3, 4)
    kpos = jnp.arange(s)

    def one_block(args):
        q_blk, start = args
        sc = jnp.einsum('bqhd,bkhd->bhqk', q_blk, k, preferred_element_type=jnp.float32) * scale
        qpos = start + jnp.arange(Q_BLOCK)
        sc = jnp.where(kpos[None, :] <= qpos[:, None], sc, MASK_VALUE)
        p = jax.nn.softmax(sc, axis=-1).astype(v.dtype)
        return jnp.einsum('bhqk,bkhd->bqhd', p, v)

    ob = lax.map(one_block, (qb, jnp.arange(nb) * Q_BLOCK))
    return ob.transpose(1, 0, 2, 3, 4).reshape(bsz, s, h, v.shape[-1])

def mla_mixer(q_lat, kv_lat, k_rope, cos, sin, q_norm, kv_norm, w_uq, w_ukv, w_o):
    bsz, s, _ = q_lat.shape
    q = (rmsnorm(q_lat, q_norm) @ w_uq).reshape(bsz, s, MLA_HEADS, MLA_NOPE + MLA_ROPE)
    q_nope, q_pe = q[..., :MLA_NOPE], q[..., MLA_NOPE:]
    q_pe = apply_rope(q_pe, cos[:, :, None, :], sin[:, :, None, :])
    kv = (rmsnorm(kv_lat, kv_norm) @ w_ukv).reshape(bsz, s, MLA_HEADS, MLA_NOPE + MLA_V)
    k_nope, v = kv[..., :MLA_NOPE], kv[..., MLA_NOPE:]
    k_pe = apply_rope(k_rope, cos, sin)
    k = jnp.concatenate([k_nope, jnp.broadcast_to(k_pe[:, :, None, :], (bsz, s, MLA_HEADS, MLA_ROPE))], axis=-1)
    q = jnp.concatenate([q_nope, q_pe], axis=-1)
    o = blocked_causal_attention(q, k, v, 1.0 / math.sqrt(MLA_NOPE + MLA_ROPE))
    return o.reshape(bsz, s, MLA_WIDTH) @ w_o

def hgrn2_mixer(q, f_logit, i_in, g, lb, g_norm, w_o):
    bsz, s, _ = q.shape
    n_chunks = s // HG_CHUNK

    def to_chunks(t):
        return t.reshape(bsz, n_chunks, HG_CHUNK, HG_HEADS, -1).transpose(1, 0, 3, 2, 4)

    lbf = lb.astype(jnp.float32)
    sig = jax.nn.sigmoid(f_logit.astype(jnp.float32))
    f = lbf + (1.0 - lbf) * sig
    log_f = jnp.log(f)
    k = 1.0 - f
    xs = (to_chunks(jax.nn.silu(q.astype(jnp.float32))), to_chunks(k),
          to_chunks(i_in.astype(jnp.float32)), to_chunks(log_f))
    causal = jnp.tril(jnp.ones((HG_CHUNK, HG_CHUNK), dtype=bool))[:, :, None]

    def chunk_step(state, chunk):
        q_n, k_n, v_n, lf_n = chunk
        b = jnp.cumsum(lf_n, axis=2)
        diff = b[:, :, :, None, :] - b[:, :, None, :, :]
        decay = jnp.where(causal, jnp.exp(jnp.where(causal, diff, 0.0)), 0.0)
        attn = jnp.einsum('bhtd,bhsd,bhtsd->bhts', q_n, k_n, decay)
        o_n = jnp.einsum('bhts,bhse->bhte', attn, v_n) + jnp.einsum('bhtd,bhde->bhte', q_n * jnp.exp(b), state)
        b_last = b[:, :, -1, :]
        k_dec = k_n * jnp.exp(b_last[:, :, None, :] - b)
        state = jnp.exp(b_last)[..., None] * state + jnp.einsum('bhsd,bhse->bhde', k_dec, v_n)
        return state, o_n

    s0 = jnp.zeros((bsz, HG_HEADS, HG_DK, HG_DV), jnp.float32)
    _, o = lax.scan(chunk_step, s0, xs)
    o = o.transpose(1, 0, 3, 2, 4).reshape(bsz, s, HG_HEADS, HG_DV)
    gate = g.astype(jnp.float32).reshape(bsz, s, HG_HEADS, HG_DV)
    o = rmsnorm(o, g_norm) * jax.nn.silu(gate)
    return o.reshape(bsz, s, HG_HEADS * HG_DV).astype(g.dtype) @ w_o

def memory_cross_attention(h, mem_n, w_q, w_kv, w_o):
    bsz, s, _ = h.shape
    m = mem_n.shape[1]
    q = (h @ w_q).reshape(bsz, s, X_HEADS, X_HEAD_DIM)
    k, v = jnp.split(mem_n @ w_kv, 2, axis=-1)
    k = k.reshape(bsz, m, X_HEADS, X_HEAD_DIM)
    v = v.reshape(bsz, m, X_HEADS, X_HEAD_DIM)
    sc = jnp.einsum('bqhd,bkhd->bhqk', q, k, preferred_element_type=jnp.float32) / math.sqrt(X_HEAD_DIM)
    p = jax.nn.softmax(sc, axis=-1).astype(v.dtype)
    o = jnp.einsum('bhqk,bkhd->bqhd', p, v)
    return o.reshape(bsz, s, X_WIDTH) @ w_o

def swiglu_ffn(h, w_gate_up, w_down):
    gt, up = jnp.split(h @ w_gate_up, 2, axis=-1)
    return (jax.nn.silu(gt) * up) @ w_down

def second_inputs(seed: int = 0) -> dict:
    key = jax.random.key(seed)
    keys = list(jax.random.split(key, 48))
    L = DEPTH

    def nrm(shape, scale):
        return scale * jax.random.normal(keys.pop(), shape, jnp.float32)

    def gain(shape):
        return 1.0 + 0.05 * jax.random.normal(keys.pop(), shape, jnp.float32)

    x = nrm((BATCH, SEQ, D_MODEL), 1.0)
    mem = nrm((BATCH, N_MEM, D_MODEL), 1.0)
    offsets = jax.random.randint(keys.pop(), (BATCH, 1), 0, MAX_POS_OFFSET, dtype=jnp.int32)
    positions = (offsets + jnp.arange(SEQ, dtype=jnp.int32)[None, :]).astype(jnp.int32)
    state_idx = jnp.arange(SSM_STATE, dtype=jnp.float32)
    return {
        "x": x,
        "mem": mem,
        "positions": positions,
        "norm_mix": gain((L, D_MODEL)),
        "w_in": nrm((L, D_MODEL, D_IN), D_MODEL ** -0.5),
        "ssm_lam_re": -0.5 + nrm((L, SSM_GROUPS, SSM_STATE), 0.01),
        "ssm_lam_im": math.pi * state_idx + nrm((L, SSM_GROUPS, SSM_STATE), 0.01),
        "ssm_b_re": nrm((L, SSM_GROUPS, SSM_STATE, SSM_GROUP_CH), (2.0 * SSM_GROUP_CH) ** -0.5),
        "ssm_b_im": nrm((L, SSM_GROUPS, SSM_STATE, SSM_GROUP_CH), (2.0 * SSM_GROUP_CH) ** -0.5),
        "ssm_c_re": nrm((L, SSM_GROUPS, SSM_GROUP_CH, SSM_STATE), (2.0 * SSM_STATE) ** -0.5),
        "ssm_c_im": nrm((L, SSM_GROUPS, SSM_GROUP_CH, SSM_STATE), (2.0 * SSM_STATE) ** -0.5),
        "ssm_d": nrm((L, SSM_GROUPS, SSM_GROUP_CH), 1.0),
        "ssm_log_step": jax.random.uniform(keys.pop(), (L, SSM_GROUPS), jnp.float32, math.log(1e-3), math.log(1e-1)),
        "ssm_w_glu": nrm((L, SSM_WIDTH, 2 * D_MODEL), SSM_WIDTH ** -0.5),
        "mla_q_norm": gain((L, MLA_Q_RANK)),
        "mla_kv_norm": gain((L, MLA_KV_RANK)),
        "mla_w_uq": nrm((L, MLA_Q_RANK, MLA_HEADS * (MLA_NOPE + MLA_ROPE)), MLA_Q_RANK ** -0.5),
        "mla_w_ukv": nrm((L, MLA_KV_RANK, MLA_HEADS * (MLA_NOPE + MLA_V)), MLA_KV_RANK ** -0.5),
        "mla_w_o": nrm((L, MLA_WIDTH, D_MODEL), MLA_WIDTH ** -0.5),
        "hg_lb": nrm((L, HG_HEADS * HG_DK), 1.0),
        "hg_g_norm": gain((L, HG_DV)),
        "hg_w_o": nrm((L, HG_HEADS * HG_DV, D_MODEL), (HG_HEADS * HG_DV) ** -0.5),
        "w_out": nrm((L, D_MODEL, D_MODEL), D_MODEL ** -0.5),
        "norm_cross": gain((L, D_MODEL)),
        "norm_mem": gain((L, D_MODEL)),
        "x_w_q": nrm((L, D_MODEL, X_WIDTH), D_MODEL ** -0.5),
        "x_w_kv": nrm((L, D_MODEL, 2 * X_WIDTH), D_MODEL ** -0.5),
        "x_w_o": nrm((L, X_WIDTH, D_MODEL), X_WIDTH ** -0.5),
        "norm_ffn": gain((L, D_MODEL)),
        "ffn_w_gate_up": nrm((L, D_MODEL, 2 * D_FF), D_MODEL ** -0.5),
        "ffn_w_down": nrm((L, D_FF, D_MODEL), D_FF ** -0.5),
        "norm_final": gain((D_MODEL,)),
    }

def second_block(x, mem, positions, norm_mix, w_in, ssm_lam_re, ssm_lam_im, ssm_b_re, ssm_b_im,
              ssm_c_re, ssm_c_im, ssm_d, ssm_log_step, ssm_w_glu, mla_q_norm, mla_kv_norm,
              mla_w_uq, mla_w_ukv, mla_w_o, hg_lb, hg_g_norm, hg_w_o, w_out, norm_cross, norm_mem,
              x_w_q, x_w_kv, x_w_o, norm_ffn, ffn_w_gate_up, ffn_w_down, norm_final):
    bsz, s, _ = x.shape
    cos, sin = rope_tables(positions)
    lb_p = jax.nn.softmax(hg_lb.astype(jnp.float32), axis=0)
    lower_bounds = jnp.cumsum(lb_p, axis=0) - lb_p[0:1]
    split_at = np.cumsum(IN_SPLITS)[:-1].tolist()

    for l in range(DEPTH):
        h = rmsnorm(x, norm_mix[l])
        (u_ssm, q_lat, kv_lat, k_rope, hg_q, hg_f, hg_i, hg_g, gate_logits) = jnp.split(h @ w_in[l], split_at, axis=-1)
        y_ssm = s5_mixer(u_ssm, ssm_lam_re[l], ssm_lam_im[l], ssm_b_re[l], ssm_b_im[l],
                         ssm_c_re[l], ssm_c_im[l], ssm_d[l], ssm_log_step[l], ssm_w_glu[l])
        y_mla = mla_mixer(q_lat, kv_lat, k_rope, cos, sin, mla_q_norm[l], mla_kv_norm[l],
                          mla_w_uq[l], mla_w_ukv[l], mla_w_o[l])
        y_hg = hgrn2_mixer(hg_q, hg_f, hg_i, hg_g, lower_bounds[l], hg_g_norm[l], hg_w_o[l])
        gates = jax.nn.sigmoid(gate_logits.astype(jnp.float32)).reshape(bsz, s, N_BRANCH, D_MODEL)
        merged = (gates[:, :, 0] * y_ssm.astype(jnp.float32)
                  + gates[:, :, 1] * y_mla.astype(jnp.float32)
                  + gates[:, :, 2] * y_hg.astype(jnp.float32)).astype(x.dtype)
        x = x + merged @ w_out[l]
        x = x + memory_cross_attention(rmsnorm(x, norm_cross[l]), rmsnorm(mem, norm_mem[l]),
                                       x_w_q[l], x_w_kv[l], x_w_o[l])
        x = x + swiglu_ffn(rmsnorm(x, norm_ffn[l]), ffn_w_gate_up[l], ffn_w_down[l])
    return rmsnorm(x, norm_final)


def setup_inputs(seed=0):
    out = dict(first_inputs(seed))
    for name, value in second_inputs(seed + 1).items():
        if name != "x":
            out[name + "_2"] = value
    return out


def reference(
    x, p, norm_gain, moba_w_in, moba_q_gain, moba_k_gain, moba_w_out, nsa_w_in, nsa_q_gain,
    nsa_k_gain, nsa_cmp_pe, nsa_cmp_w1, nsa_cmp_w2, nsa_w_out, ple_w_proj, ple_gate_gain,
    ple_w_gate, mem_2, positions_2, norm_mix_2, w_in_2, ssm_lam_re_2, ssm_lam_im_2, ssm_b_re_2,
    ssm_b_im_2, ssm_c_re_2, ssm_c_im_2, ssm_d_2, ssm_log_step_2, ssm_w_glu_2, mla_q_norm_2,
    mla_kv_norm_2, mla_w_uq_2, mla_w_ukv_2, mla_w_o_2, hg_lb_2, hg_g_norm_2, hg_w_o_2, w_out_2,
    norm_cross_2, norm_mem_2, x_w_q_2, x_w_kv_2, x_w_o_2, norm_ffn_2, ffn_w_gate_up_2,
    ffn_w_down_2, norm_final_2,
):
    x = first_block(
        x, p, norm_gain, moba_w_in, moba_q_gain, moba_k_gain, moba_w_out, nsa_w_in, nsa_q_gain,
        nsa_k_gain, nsa_cmp_pe, nsa_cmp_w1, nsa_cmp_w2, nsa_w_out, ple_w_proj, ple_gate_gain,
        ple_w_gate,
    )
    return second_block(
        x, mem_2, positions_2, norm_mix_2, w_in_2, ssm_lam_re_2, ssm_lam_im_2, ssm_b_re_2,
        ssm_b_im_2, ssm_c_re_2, ssm_c_im_2, ssm_d_2, ssm_log_step_2, ssm_w_glu_2, mla_q_norm_2,
        mla_kv_norm_2, mla_w_uq_2, mla_w_ukv_2, mla_w_o_2, hg_lb_2, hg_g_norm_2, hg_w_o_2,
        w_out_2, norm_cross_2, norm_mem_2, x_w_q_2, x_w_kv_2, x_w_o_2, norm_ffn_2,
        ffn_w_gate_up_2, ffn_w_down_2, norm_final_2,
    )


_drawn_inputs = setup_inputs


def setup_inputs(seed=0):
    import zlib

    import numpy as np

    out = dict(_drawn_inputs(seed))
    spreads = {}
    factors = {'norm_gain': 8.0,
     'moba_q_gain': 8.0,
     'moba_k_gain': 8.0,
     'nsa_q_gain': 8.0,
     'nsa_k_gain': 8.0,
     'nsa_cmp_pe': 3.075,
     'ple_gate_gain': 64.0,
     'ssm_lam_re_2': 64.0,
     'ssm_lam_im_2': 32.344,
     'ssm_b_re_2': 44.424,
     'ssm_b_im_2': 44.496,
     'ssm_c_re_2': 45.224,
     'ssm_c_im_2': 45.072,
     'ssm_log_step_2': 33.856,
     'mla_q_norm_2': 8.0,
     'mla_kv_norm_2': 6.324,
     'hg_lb_2': 21.792,
     'hg_g_norm_2': 22.144,
     'norm_cross_2': 8.0,
     'norm_mem_2': 6.224,
     'ssm_d_2': 8.0,
     'ssm_w_glu_2': 8.0,
     'norm_ffn_2': 8.0,
     'ffn_w_gate_up_2': 3.691,
     'ffn_w_down_2': 3.707}
    for name, (base, spread) in spreads.items():
        noise = np.random.default_rng([zlib.crc32(name.encode()), seed]).standard_normal(out[name].shape)
        drawn = base * np.exp(spread * noise) if base else spread * noise
        out[name] = __import__('jax').numpy.asarray(drawn.astype(out[name].dtype))
    for name, factor in factors.items():
        out[name] = (out[name] * factor).astype(out[name].dtype)
    return out
```

```python
from contextlib import ExitStack

import numpy as np
import concourse.bass as bass
from concourse import mybir
from concourse.alu_op_type import AluOpType as ALU

F32 = mybir.dt.float32
I32 = mybir.dt.int32
I8 = mybir.dt.int8
ACT = mybir.ActivationFunctionType
AX = mybir.AxisListType

P = 128
D = 1024
T = 256
TT = T // P
KD = D // P
DEPTH = 2
EPS = 1e-6
NEG = -1e30
RING = 6
UNIT = 2048
BANKS = 8
PI = 3.1415925
ROUND = 12582912.0
TWO_PI = (6.28125, 0.0019340515136718750, 1.2556659146435e-06)

H, HD = 16, 64
KV = 4
NCMP = 15
NCP = 16
CL, CS = 32, 16

SG, SC, SN = 32, 16, 64
SB = SG * SN // P
QR, KR, NOPE, ROPE, MV, MH = 512, 256, 64, 32, 64, 8
QK = NOPE + ROPE
HH, HK = 4, 128
XH, XK = 4, 128
FF = 2816
LEVELS = [1, 2, 4, 8, 16, 32, 64, 128]

V1 = dict(norm0=0, norm1=8, ple0=16, ple1=24, pe=32)
V2 = dict(mix=0, cross=8, mem=16, ffn=24, q=32, kv=36, lb0=38, lb1=42, hgn=46, skip=47,
          lam_re=51, lam_im=67, step=96)


class Line:

    def __init__(self, known):
        self.known = known
        self.count, self.base, self.marks = 0, None, {}
        self.layer = known["layer"] if known else 0

    def mark(self, name, in_layer):
        self.marks[name] = (self.count, in_layer)

    def at(self, name, l):
        if not self.known:
            return 1
        value, in_layer = self.known["marks"][name]
        return value + l * self.layer if in_layer else value


class Program:

    def __init__(self, known):
        self.known = known
        self.lines, self.groups, self.evacs = {}, {}, {}
        self.in_layer = False
        self.bank_layer = known["bank_layer"] if known else [0] * BANKS


class Hand:

    def __init__(self, prog, name, bank_evac):
        self.p, self.line, self.bank_evac = prog, prog.lines[name], bank_evac
        self.l = 0

    def step(self, ins, mark=None):
        self.line.count += 1
        if mark is not None:
            self.line.mark(mark, self.p.in_layer)

    def last(self):
        return self.line.count + self.l * self.line.layer if self.p.in_layer else self.line.count

    def at(self, who, mark):
        return self.p.lines[who].at(mark, self.l)

    def bank(self, key):
        return self.p.groups[key][0]

    def evac_value(self, key):
        bank, value, in_layer = self.p.groups[key]
        return value + self.l * self.p.bank_layer[bank] if in_layer else value

    def evacuations(self, *keys):
        last = {}
        for key in keys:
            bank, value, _ = self.p.groups[key]
            if bank not in last or value > self.p.groups[last[bank]][1]:
                last[bank] = key
        return [(self.bank_evac[bank], self.evac_value(key)) for bank, key in last.items()]

    def evacuated(self, key, ins):
        self.p.evacs[key] = self.p.evacs.get(key, 0) + 1


def kview(w, k0, nk, c0, nc):
    return w[k0 * P:(k0 + nk) * P, c0:c0 + nc].rearrange("(k p) n -> p k n", p=P)


def weight_plan_first(A):
    out = []

    def cols(name, w, c0, n):
        for c in range(0, n, 256):
            out.append((name, (8, 256), kview(w, 0, 8, c0 + c, 256)))

    def ple(i):
        out.append(("proj", (2, 1024), kview(A["ple_w_proj"][i], 0, 2, 0, 1024)))
        cols("gate", A["ple_w_gate"][i], 0, 1024)

    w = A["moba_w_in"][0]
    for name, c0 in (("q", 0), ("k", D), ("v", 2 * D), ("z", 3 * D)):
        cols(name, w, c0, D)
    cols("out", A["moba_w_out"][0], 0, D)
    ple(0)
    w = A["nsa_w_in"][0]
    cols("q", w, 0, D)
    cols("kv", w, D, 6 * 256)
    out.append(("gl", (8, 48), kview(w, 0, 8, D + 6 * 256, 48)))
    cols("z", w, D + 6 * 256 + 48, D)
    for s in range(2):
        for c in range(2):
            out.append(("cmp", (8, 256), kview(A["nsa_cmp_w1"][0, s], 8 * c, 8, 0, 256)))
    cols("out", A["nsa_w_out"][0], 0, D)
    ple(1)
    while len(out) % RING:
        out.append(None)
    return out


def weight_plan_layer(A, l):
    out = []

    def cols(name, w, c0, n):
        for c in range(0, n, 256):
            out.append((name, (8, 256), kview(w, 0, 8, c0 + c, 256)))

    w = A["w_in_2"][l]
    cols("u", w, 0, 512)
    cols("gates", w, 3360, 3 * D)
    cols("ql", w, 512, 512)
    cols("kvl", w, 1024, 256)
    out.append(("kr", (8, 32), kview(w, 0, 8, 1280, 32)))
    for c in (2, 3, 0, 1):
        out.append(("glu", (4, 512), kview(A["ssm_w_glu_2"][l], 0, 4, 512 * c, 512)))
    for c in range(2):
        out.append(("uq", (4, 384), kview(A["mla_w_uq_2"][l], 0, 4, 384 * c, 384)))
    out.append(("ukv", (2, 1024), kview(A["mla_w_ukv_2"][l], 0, 2, 0, 1024)))
    cols("hq", w, 1312, 512)
    cols("hf", w, 1824, 512)
    cols("hi", w, 2336, 512)
    cols("hg", w, 2848, 512)
    for c in range(2):
        out.append(("mo", (4, 512), kview(A["mla_w_o_2"][l], 0, 4, 512 * c, 512)))
    for c in range(2):
        out.append(("ho", (4, 512), kview(A["hg_w_o_2"][l], 0, 4, 512 * c, 512)))
    cols("xk", A["x_w_kv_2"][l], 0, 512)
    cols("xv", A["x_w_kv_2"][l], 512, 512)
    cols("wout", A["w_out_2"][l], 0, D)
    cols("xq", A["x_w_q_2"][l], 0, 512)
    for c in range(2):
        out.append(("xo", (4, 512), kview(A["x_w_o_2"][l], 0, 4, 512 * c, 512)))
    for c in range(0, FF, 256):
        out.append(("fg", (8, 256), kview(A["ffn_w_gate_up_2"][l], 0, 8, c, 256)))
        out.append(("fu", (8, 256), kview(A["ffn_w_gate_up_2"][l], 0, 8, FF + c, 256)))
    for c in range(FF // P // 2):
        out.append(("fd", (2, 1024), kview(A["ffn_w_down_2"][l], 2 * c, 2, 0, 1024)))
    while len(out) % RING:
        out.append(None)
    return out


def slot_loads(plan, i):
    return sum(1 for j in range(i % RING, i + 1, RING) if plan[j] is not None)


START_LOADS = 13
GATES_EARLY = 7
BETWEEN_LEVELS = [("hi", 0), ("hi", 1), ("hg", 0), ("hg", 1), ("mo2", 0), ("mo2", 1), ("mo2", 2), ("mo2", 3)]
PARAM_LOADS = 17


def used(mark, plan):
    kind, first, n = mark
    while plan[n] is None:
        n -= RING
    return kind, first, n


def build(nc, A, out, known, looped):
    plan1 = weight_plan_first(A)
    plan2 = [weight_plan_layer(A, l) for l in range(DEPTH)]
    prog = Program(known)

    with ExitStack() as ctx:
        def sb(name, shape, dt=F32):
            return ctx.enter_context(nc.sbuf_tensor(name, shape, dt))

        def sem(name):
            return ctx.enter_context(nc.semaphore(name))

        banks = [ctx.enter_context(nc.psum_tensor(f"bank{i}", [P, 512], F32)) for i in range(BANKS)]
        bank_evac = [sem(f"bank_evac{i}") for i in range(BANKS)]
        unit_ready = [sem(f"unit_ready{i}") for i in range(RING)]
        params_ready = sem("params_ready")
        start_ready = sem("start_ready")
        out_stored = sem("out_stored")
        pe_done = sem("pe_done")
        act_done = sem("act_done")
        dve_done = sem("dve_done")
        pool_done = sem("pool_done")
        for name in ("pe", "dve", "act", "pool", "sp"):
            prog.lines[name] = Line(known["lines"][name] if known else None)

        ring = sb("ring", [P, RING, UNIT])
        x = sb("x", [P, TT, D])
        xn = sb("xn", [P, TT, D])
        hT = sb("hT", [P, KD, T])
        ident = sb("ident", [P, P])
        causal3 = sb("causal3", [P, 3, P])
        level_mask = sb("level_mask", [P, 8, P], I8)
        ones = sb("ones", [P, T])
        angles = sb("angles", [P, P])
        cos_t = sb("cos_t", [P, P])
        sin_t = sb("sin_t", [P, P])
        tr_a = sb("tr_a", [P, P])
        tr_b = sb("tr_b", [P, P])
        freqs = sb("freqs", [P, 48])
        pos_i = sb("pos_i", [P, 6], I32)
        pos_f = sb("pos_f", [P, 6])
        rows = sb("rows", [P, P])
        vt = sb("vt", [P, P])
        lsr = sb("lsr", [P, 2])
        st_a = sb("st_a", [P, 2, 2])
        st_b = sb("st_b", [P, 2])
        st_c = sb("st_c", [P, 2])
        hs_a = sb("hs_a", [P, 64])
        hs_b = sb("hs_b", [P, 64])
        hs_c = sb("hs_c", [P, 64])
        a_max = sb("a_max", [P, 3, 6])
        a_sum = sb("a_sum", [P, 3, 6])
        a_rec = sb("a_rec", [P, 3, 6])
        a_nrm = sb("a_nrm", [P, 3, 6])
        memn = sb("memn", [P, KD, T])
        chm = sb("chm", [P, 2, 2])
        chm_i = sb("chm_i", [P, 2], I32)
        low = sb("low", [P, HH])
        lbt = sb("lbt", [P, 4, HH])
        mst = sb("mst", [P, 3, 4])
        ARENA = 30050
        arena = sb("arena", [P, ARENA])
        top = {"at": 0, "most": 0}

        def take(*shape, at=None):
            n = int(np.prod(shape))
            a = top["at"] if at is None else at
            if at is None:
                top["at"] += n
            assert a + n <= ARENA, (a + n, ARENA)
            v = arena[:, a:a + n]
            if len(shape) == 2:
                v = v.rearrange("p (a b) -> p a b", a=shape[0])
            if len(shape) == 3:
                v = v.rearrange("p (a b c) -> p a b c", a=shape[0], b=shape[1])
            if len(shape) == 4:
                v = v.rearrange("p (a b c d) -> p a b c d", a=shape[0], b=shape[1], c=shape[2])
            return v

        qk = take(2, TT, H, HD)
        raw = qk[:, 1, :, :, :].rearrange("p t h d -> p (t h d)")
        vf = take(TT, H, HD)
        tmp = take(4, TT * H * HD // 2)
        qT = take(KD, T)
        kT = take(KD, T)
        zs = take(KD, T)
        sc = take(3, 832)
        pT = take(3, 1024)
        gains = take(6, HD)
        gl_s = take(TT, H, 3)
        w2s = take(2, 2, HD)
        cmp_neg = take(TT, NCP)
        cmp_on = take(TT, NCP)
        kvr = take(6, TT * KV, HD)
        kcT = take(KV, NCP)
        vcf = take(KV, HD)
        kcf = take(KV, HD)
        hid = take(2, 2, 60)
        kcd = tmp[:, 3, 512:512 + KV * 2 * HD].rearrange("p (a b c) -> p a b c", a=KV, b=2)
        p_in = take(2, TT, 256)
        dup = take(2, TT * KV, 2, HD)
        x2 = vf.rearrange("p t h d -> p (t h d)").rearrange("p (s g t) -> p s g t", s=2, g=KV)
        flat_v = [sc.rearrange("p a b -> p (a b)")[:, 960 * i:960 * (i + 1)].rearrange("p (j n) -> p j n", j=16)
                  for i in range(2)]
        mem_in = zs.rearrange("p k t -> p (k t)").rearrange("p (t d) -> p t d", t=TT)
        top["most"] = top["at"]
        oT1 = qk[:, 0, :, :, :].rearrange("p t h d -> p (t h d)").rearrange("p (k t) -> p k t", k=KD)
        prj = qk[:, 1, :, :, :].rearrange("p t h d -> p t (h d)")
        g_tmp = tmp.rearrange("p a b -> p (a b)")[:, 0:4 * 512].rearrange("p (a t c) -> p a t c", a=4, t=TT)
        assert 4 * 512 <= 4 * TT * H * HD // 2

        top["at"] = 0
        gates = take(3 * KD, T)
        gu = gates[:, 0:FF // P, :]
        merged = take(KD, T)
        sgl = take(KD, T)
        sT = take(4, T)
        mT = take(4, T)
        work = top["at"]
        e_re = take(SB, T + 1)
        e_im = take(SB, T + 1)
        e_tmp = gates[:, 16:24, :].rearrange("p a b -> p (a b)").rearrange("p (a b) -> p a b", a=SB)
        b_raw = take(2, SB, SC)
        low_part = sgl.rearrange("p a b -> p (a b)")
        b_tmp = [low_part[:, 256 * i:256 * (i + 1)].rearrange("p (a b) -> p a b", a=SB) for i in range(4)]
        b_diag = low_part[:, 1024:2048].rearrange("p (s a b c) -> p s a b c", s=2, a=SB, b=2)
        b_T = take(2, 4, P)
        c_raw = take(2, 4, SN)
        c_diag = merged.rearrange("p a b -> p (a b)")[:, 0:1024].rearrange("p (s a b c) -> p s a b c", s=2, a=4, b=2)
        c_T = take(2, 4, P)
        s5v = take(20, SB)
        uT = take(4, T)
        z_in = take(2, 2, T)
        z_st = take(2, 2, T)
        z_tm = take(4, T)
        x_st = take(2, 2, T)
        x_tm = mT
        y_s = take(4, T)
        top["most"] = max(top["most"], top["at"])
        top["at"] = work
        ql = take(TT, QR)
        kvl = take(TT, KR)
        krp = take(TT, ROPE)
        qlT = take(4, T)
        kvT = take(2, T)
        m_q = take(TT, MH, QK)
        m_k = take(TT, MH, QK)
        m_v = take(TT, MH, MV)
        m_tmp = take(4, TT * MH, ROPE // 2)
        m_qT = take(MH, T)
        m_kT = take(MH, T)
        m_sc = take(3, 512)
        m_pT = take(3, 512)
        mlan = take(TT, QR)
        top["most"] = max(top["most"], top["at"])
        top["at"] = work
        hq = take(HH, T)
        hb = take(HH, T)
        hk = take(HH, T)
        hE = take(HH, T)
        hQ = take(2, HH, T)
        hKp = take(2, HH, T)
        hA = take(HH, 3, P)
        hv = take(TT, HH, HK)
        hg = take(TT, HH, HK)
        ho = take(TT, HH, HK)
        hsq = take(TT, HH, HK)
        top["most"] = max(top["most"], top["at"])
        top["at"] = work
        memT = take(KD, T)
        xkT = take(XH, T)
        xv = take(TT, XH * XK)
        xqT = take(XH, T)
        x_sc = take(3, 512)
        x_pT = take(3, 512)
        xoT = take(XH, T)
        f_tmp = take(4, 512)
        nfin = hT[:, 0:4, :].rearrange("p k t -> p (k t)")
        m_tmp2 = hsq.rearrange("p t h d -> p (t h d)").rearrange("p (a b) -> p a b", a=2)
        top["most"] = max(top["most"], top["at"])

        prog.lines["sp"].layer_now = 0

        def in_layers(e, eng, body, before=lambda: None):
            prog.in_layer = True
            base = e.line.count
            if looped:
                with eng.Fori(0, DEPTH) as l:
                    before()
                    body(l)
            else:
                for l in range(DEPTH):
                    before()
                    e.line.count = base
                    body(l)
            e.line.layer_now = e.line.count - base
            e.line.count = base + DEPTH * e.line.layer_now
            prog.in_layer = False
            e.l = DEPTH - 1

        def bc(ap, axis, shape):
            return ap.unsqueeze(axis).to_broadcast([ap.shape[0], *shape])

        block = ctx.enter_context(nc.Block())

        @block.tensor
        def _(pe):
            e = Hand(prog, "pe", bank_evac)
            total = [0] * BANKS
            turn = [0]
            unit_at = {"n": 0, "plan": plan1, "base": [0] * RING, "layer": [0] * RING}
            for s in range(RING):
                unit_at["layer"][s] = slot_loads(plan2[0], len(plan2[0]) - RING + s)

            def opened(key, evacs):
                b = turn[0] % BANKS
                turn[0] += 1
                if total[b] > 0 or prog.in_layer:
                    pe.wait_ge(bank_evac[b], total[b] + e.l * prog.bank_layer[b]
                               if prog.in_layer else total[b])
                total[b] += evacs
                prog.groups[key] = (b, total[b], prog.in_layer)
                assert key not in prog.evacs
                prog.evacs[("want", key)] = evacs
                return banks[b]

            def closed(key, ins):
                e.step(ins.then_inc(pe_done, 1), ("group", key))

            def unit(name):
                plan, n = unit_at["plan"], unit_at["n"]
                unit_at["n"] += 1
                s = n % RING
                got, (nk, ncol), _ = plan[n]
                assert got == name, (got, name, n)
                value = 16 * (unit_at["base"][s] + slot_loads(plan, n))
                pe.wait_ge(unit_ready[s], value + e.l * 16 * unit_at["layer"][s]
                           if prog.in_layer else value)
                return ring[:, s, 0:nk * ncol].rearrange("p (k n) -> p k n", k=nk)

            def unit_used():
                e.line.mark(("unit", unit_at["plan"] is plan1, unit_at["n"] - 1), prog.in_layer)

            def unit_skip():
                while unit_at["n"] % RING:
                    assert unit_at["plan"][unit_at["n"]] is None
                    unit_at["n"] += 1

            def feature_major(key, w, src, nk, m0, nm, evacs=1):
                b = opened(key, evacs)
                for m in range(nm):
                    for k in range(nk):
                        ins = pe.matmul(b[:, m * T:(m + 1) * T], w[:, k, (m0 + m) * P:(m0 + m + 1) * P],
                                        src[:, k, :], start=(k == 0), stop=(k == nk - 1))
                closed(key, ins)

            def token_major(key, w, src, nk, c0, n, tts, evacs=1):
                b = opened(key, evacs)
                for i, tt in enumerate(tts):
                    for k in range(nk):
                        ins = pe.matmul(b[:, i * n:(i + 1) * n], src[:, k, tt * P:(tt + 1) * P],
                                        w[:, k, c0:c0 + n], start=(k == 0), stop=(k == nk - 1))
                closed(key, ins)

            def transposes(key, pieces, evacs=1):
                b = opened(key, evacs)
                for c, src in pieces:
                    m, n = src.shape[0], src.shape[1]
                    ins = pe.transpose(b[0:n, c:c + m], src, ident[0:m, 0:m])
                closed(key, ins)

            def norm_pe(n, kd=KD, src=xn):
                pe.wait_ge(dve_done, e.at("dve", ("xn", n)))
                for j in range(kd // 2):
                    transposes(("nT", n, j), [(256 * i + P * tt, src[:, tt, (2 * j + i) * P:(2 * j + i + 1) * P])
                                              for i in range(2) for tt in range(TT)], evacs=2)

            def norm_ready(n, kd=KD):
                for s_, v_ in e.evacuations(*[("nT", n, j) for j in range(kd // 2)]):
                    pe.wait_ge(s_, v_)

            def units_fm(name, key, src, count):
                for i in range(count):
                    w = unit(name)
                    feature_major((key, i), w, src, 8, 0, 2)
                    unit_used()

            def units_tm(name, key, src, count):
                for i in range(count):
                    w = unit(name)
                    token_major((key, i), w, src, 8, 0, w.shape[2], (0, 1))
                    unit_used()

            def attention_pe(key, nh, scores, moved, values, lag=2):
                for i in range(nh + lag + 1):
                    if i < nh:
                        scores(i)
                    if 0 <= i - lag < nh:
                        pe.wait_ge(pool_done, e.at("pool", (key, "norm", i - lag)))
                        moved(i - lag)
                    if 0 <= i - lag - 1 < nh:
                        values(i - lag - 1)

            def causal_scores(key, q, k):
                b = opened(key, 1)
                pe.matmul(b[:, 0:P], q[:, 0:P], k[:, 0:P], start=True, stop=True)
                ins = pe.matmul(b[:, P:3 * P], q[:, P:T], k[:, 0:T], start=True, stop=True)
                closed(key, ins)

            def causal_moved(key, s):
                transposes(key, [(P * j, s[:, P * j:P * (j + 1)]) for j in range(3)])

            pe.wait_ge(start_ready, 16 * START_LOADS)
            pe.wait_ge(pool_done, e.at("pool", "constants"))
            transposes("vt1", [(0, rows[0:64, :])])

            norm_pe("mem")

            norm_pe("n0")
            norm_ready("n0")
            units_tm("q", "mq", hT, 4)
            units_tm("k", "mk", hT, 4)
            units_tm("v", "mv", hT, 4)
            units_fm("z", "mz", hT, 4)
            for a in range(2):
                pe.wait_ge(dve_done, e.at("dve", ("roped", "m", a)))
                src = qk[:, a, :, :, :].rearrange("p t h d -> p t (h d)")
                for j in range(4):
                    transposes(("mT", a, j), [(T * i + P * tt, src[:, tt, (2 * j + i) * P:(2 * j + i + 1) * P])
                                              for i in range(2) for tt in range(TT)])
            for a in range(2):
                for s_, v_ in e.evacuations(*[("mT", a, j) for j in range(4)]):
                    pe.wait_ge(s_, v_)
            for s_, v_ in e.evacuations(*[("mv", j) for j in range(4)]):
                pe.wait_ge(s_, v_)

            def m_scores(h):
                o, j = HD * (h % 2), h // 2
                causal_scores(("ms", h), qT[o:o + HD, j, :], kT[o:o + HD, j, :])

            def m_moved(h):
                causal_moved(("mp", h), sc[:, h % 3, 0:384])

            def pair_bank(key, h):
                if h % 2 == 0:
                    opened(key, 1)
                return banks[e.bank(key)]

            def causal_values(b, o, nv, v0, v1, p, first, last):
                pe.matmul(b[o:o + nv, 0:T], v0, p[:, 0:T], start=first, stop=False)
                return pe.matmul(b[o:o + nv, P:T], v1, p[:, T:T + P], start=False, stop=last)

            def m_values(h):
                for s_, v_ in e.evacuations(("mp", h)):
                    pe.wait_ge(s_, v_)
                key = ("mo", h // 2)
                b = pair_bank(key, h)
                ins = causal_values(b, HD * (h % 2), HD, vf[:, 0, h, :], vf[:, 1, h, :], pT[:, h % 3, :], True, True)
                if h % 2:
                    closed(key, ins)
                else:
                    e.step(ins.then_inc(pe_done, 1))

            attention_pe("ma", H, m_scores, m_moved, m_values)
            for s_, v_ in e.evacuations(*[("mo", j) for j in range(KD)]):
                pe.wait_ge(s_, v_)
            units_tm("out", "mw", oT1, 4)

            def ple_pe(i):
                transposes(("pT", i), [(T * k + P * tt, p_in[:, i, tt, P * k:P * (k + 1)])
                                       for k in range(2) for tt in range(TT)])
                for s_, v_ in e.evacuations(("pT", i)):
                    pe.wait_ge(s_, v_)
                w = unit("proj")
                for c in range(2):
                    for tt in range(TT):
                        token_major(("pj", i, c, tt), w, pT_in, 2, 512 * c, 512, (tt,))
                unit_used()
                norm_pe(("pl", i))
                norm_ready(("pl", i))
                units_tm("gate", ("pg", i), hT, 4)

            pT_in = pT.rearrange("p a b -> p (a b)")[:, 0:2 * T].rearrange("p (k t) -> p k t", k=2)
            ple_pe(0)

            norm_pe("n1")
            norm_ready("n1")
            units_tm("q", "nq", hT, 4)
            units_tm("kv", "nk", hT, 6)
            units_tm("gl", "ng", hT, 1)
            units_fm("z", "nz", hT, 4)
            for s in range(2):
                pe.wait_ge(pool_done, e.at("pool", ("dup", s)))
                for j in range(2):
                    transposes(("cx", s, j), [(T * i + P * tt, dup[:, s, tt * KV + 2 * j + i, :, :].rearrange("p c d -> p (c d)"))
                                              for i in range(2) for tt in range(TT)], evacs=2)
            for s in range(2):
                pe.wait_ge(dve_done, e.at("dve", ("flat", s)))
                b = opened(("ch", s), 1)
                ws = [unit("cmp"), unit("cmp")]
                for m in range(2):
                    for j in range(16):
                        ins = pe.matmul(b[:, m * 60:(m + 1) * 60], ws[j // 8][:, j % 8, m * P:(m + 1) * P],
                                        flat_v[s][:, j, :], start=(j == 0), stop=(j == 15))
                closed(("ch", s), ins)
                for back in (2, 1):
                    e.line.mark(("unit", True, unit_at["n"] - back), False)
            for s in range(2):
                for s_, v_ in e.evacuations(("ch", s)):
                    pe.wait_ge(s_, v_)
                b = opened(("cv", s), 1)
                for g in range(KV):
                    for k in range(2):
                        ins = pe.matmul(b[0:NCMP, g * HD:(g + 1) * HD], hid[:, s, k, g * NCMP:(g + 1) * NCMP],
                                        w2s[:, s, k, :], start=(k == 0), stop=(k == 1))
                closed(("cv", s), ins)
            for a in range(2):
                pe.wait_ge(pool_done, e.at("pool", ("dup", 2 + a)))
                for j in range(2):
                    transposes(("nkT", a, j), [(T * i + P * tt, dup[:, a, tt * KV + 2 * j + i, :, :].rearrange("p c d -> p (c d)"))
                                               for i in range(2) for tt in range(TT)])
            pe.wait_ge(dve_done, e.at("dve", "ckv"))
            transposes("ckT", [(NCP * g, kcd[0:NCMP, g, :, :].rearrange("p c d -> p (c d)")) for g in range(KV)])
            pe.wait_ge(dve_done, e.at("dve", ("roped", "n", 0)))
            src_q = qk[:, 0, :, :, :].rearrange("p t h d -> p t (h d)")
            for j in range(4):
                transposes(("nqT", j), [(T * i + P * tt, src_q[:, tt, (2 * j + i) * P:(2 * j + i + 1) * P])
                                        for i in range(2) for tt in range(TT)])
            for s_, v_ in e.evacuations("ckT", *[("nqT", j) for j in range(4)], *[("nkT", a, j) for a in range(2) for j in range(2)]):
                pe.wait_ge(s_, v_)
            for s_, v_ in e.evacuations(*[("nk", j) for j in range(6)]):
                pe.wait_ge(s_, v_)

            def n_scores(h):
                o, j, g = HD * (h % 2), h // 2, h // 4
                q = qT[o:o + HD, j, :]
                b = opened(("ns", h, 0), 1)
                for tt in range(TT):
                    ins = pe.matmul(b[:, NCP * tt:NCP * (tt + 1)], q[:, P * tt:P * (tt + 1)], kcT[o:o + HD, g, :],
                                    start=True, stop=True)
                closed(("ns", h, 0), ins)
                for a in range(2):
                    causal_scores(("ns", h, 1 + a), q, kT[o:o + HD, KV * a + g, :])

            def n_moved(h):
                s = sc[:, h % 3, :]
                transposes(("np", h, 0), [(P * tt, s[:, 768 + NCP * tt:768 + NCP * (tt + 1)]) for tt in range(TT)])
                for a in range(2):
                    causal_moved(("np", h, 1 + a), s[:, 384 * a:384 * (a + 1)])

            def n_values(h):
                g, o = h // 4, HD * (h % 2)
                for s_, v_ in e.evacuations(*[("np", h, a) for a in range(3)]):
                    pe.wait_ge(s_, v_)
                key = ("no", h // 2)
                b = pair_bank(key, h)
                p = pT[:, h % 3, :]
                pe.matmul(b[o:o + HD, 0:T], vcf[0:NCP, g, :], p[0:NCP, 768:768 + T], start=True, stop=False)
                for a in range(2):
                    v = kvr[:, 3 + 2 * a, :, :]
                    ins = causal_values(b, o, HD, v[:, g, :], v[:, KV + g, :], p[:, 384 * a:384 * (a + 1)], False, a == 1)
                if h % 2:
                    closed(key, ins)
                else:
                    e.step(ins.then_inc(pe_done, 1))

            attention_pe("na", H, n_scores, n_moved, n_values)
            for s_, v_ in e.evacuations(*[("no", j) for j in range(KD)]):
                pe.wait_ge(s_, v_)
            units_tm("out", "nw", oT1, 4)
            ple_pe(1)
            unit_skip()

            while turn[0] % BANKS:
                turn[0] += 1
            n_first = len(plan1)
            unit_at.update(plan=plan2[0], n=0, base=[slot_loads(plan1, n_first - RING + s) for s in range(RING)])
            group_base = list(total)

            def layer(l):
                e.l = l
                unit_at["n"] = 0
                pe.wait_ge(params_ready, 16 * PARAM_LOADS + l * 16 * PARAM_LOADS)
                pe.wait_ge(dve_done, e.at("dve", "log_steps"))
                transposes("vt2", [(0, rows[:, :])])
                norm_pe("n2")
                norm_ready("n2")
                units_fm("u", "u", hT, 2)

                def gate(i):
                    w = unit("gates")
                    feature_major(("ga", i), w, hT, 8, 0, 2)
                    unit_used()

                gate(0)
                gate(1)
                pe.wait_ge(dve_done, e.at("dve", "b_diag"))
                for s in range(2):
                    transposes(("bT", s), [(P * q, b_diag[:, s, 4 * q:4 * q + 4, :, :].rearrange("p a b c -> p (a b c)"))
                                           for q in range(4)])
                pe.wait_ge(dve_done, e.at("dve", "c_diag"))
                for s in range(2):
                    transposes(("cT", s), [(P * q, c_diag[:, s, q, :, :].rearrange("p a b -> p (a b)"))
                                           for q in range(4)])
                for i in range(2, GATES_EARLY):
                    gate(i)
                for s_, v_ in e.evacuations(("u", 0), ("u", 1), ("bT", 0), ("bT", 1), ("cT", 0), ("cT", 1)):
                    pe.wait_ge(s_, v_)

                def s5_in(b):
                    q, r = b // 4, 32 * (b % 4)
                    bank = opened(("bu", b), 4)
                    for s in range(2):
                        ins = pe.matmul(bank[:, T * s:T * (s + 1)], b_T[r:r + 32, s, q, :], uT[r:r + 32, q, :],
                                        start=True, stop=True)
                    closed(("bu", b), ins)

                def s5_out(b):
                    q, r = b // 4, 32 * (b % 4)
                    key = ("y", q)
                    bank = opened(key, 1) if b % 4 == 0 else banks[e.bank(key)]
                    pe.wait_ge(pool_done, e.at("pool", ("state", b)))
                    pe.matmul(bank[r:r + 32, 0:T], c_T[:, 0, q, r:r + 32], x_st[:, b % 2, 0, :], start=True, stop=False)
                    ins = pe.matmul(bank[r:r + 32, 0:T], c_T[:, 1, q, r:r + 32], x_st[:, b % 2, 1, :],
                                    start=False, stop=True)
                    if b % 4 == 3:
                        closed(key, ins)
                    else:
                        e.step(ins.then_inc(pe_done, 1))
                    e.line.mark(("s5_out", b), True)

                for i in range(SB + 2):
                    if i < SB:
                        s5_in(i)
                    if i >= 2:
                        s5_out(i - 2)
                    if i % 2 and i // 2 < 12 - GATES_EARLY:
                        gate(GATES_EARLY + i // 2)

                units_tm("ql", "ql", hT, 2)
                units_tm("kvl", "kvl", hT, 1)
                units_tm("kr", "kr", hT, 1)
                pe.wait_ge(act_done, e.at("act", "s5_gelu"))
                for u in range(4):
                    w = unit("glu")
                    for j in range(2):
                        feature_major(("gl", u, j), w, sT, 4, 2 * j, 2)
                    unit_used()
                pe.wait_ge(dve_done, e.at("dve", "mla_xn"))
                for j in range(2):
                    transposes(("qlT", j), [(T * i + P * tt, mlan[:, tt, (2 * j + i) * P:(2 * j + i + 1) * P])
                                            for i in range(2) for tt in range(TT)], evacs=2)
                pe.wait_ge(dve_done, e.at("dve", "mla_kn"))
                transposes("kvT", [(T * i + P * tt, kvl[:, tt, i * P:(i + 1) * P])
                                   for i in range(2) for tt in range(TT)], evacs=2)
                for s_, v_ in e.evacuations(("qlT", 0), ("qlT", 1), "kvT"):
                    pe.wait_ge(s_, v_)
                for u in range(2):
                    w = unit("uq")
                    for tt in range(TT):
                        token_major(("uq", u, tt), w, qlT, 4, 0, 384, (tt,))
                    unit_used()
                w = unit("ukv")
                for c in range(2):
                    for tt in range(TT):
                        token_major(("ukv", c, tt), w, kvT, 2, 512 * c, 512, (tt,), evacs=2)
                unit_used()
                pe.wait_ge(dve_done, e.at("dve", "mq_roped"))
                for j in range(4):
                    transposes(("mqT", j), [(T * i + P * tt, m_q[:, tt, 2 * j + i, :]) for i in range(2) for tt in range(TT)])
                pe.wait_ge(dve_done, e.at("dve", "mk_roped"))
                for j in range(4):
                    transposes(("mkT", j), [(T * i + P * tt, m_k[:, tt, 2 * j + i, :]) for i in range(2) for tt in range(TT)])
                for s_, v_ in e.evacuations(*[("mqT", j) for j in range(4)], *[("mkT", j) for j in range(4)]):
                    pe.wait_ge(s_, v_)

                def l_scores(h):
                    causal_scores(("ls", h), m_qT[0:QK, h, :], m_kT[0:QK, h, :])

                def l_moved(h):
                    causal_moved(("lp", h), m_sc[:, h % 3, 0:384])

                def l_values(h):
                    for s_, v_ in e.evacuations(("lp", h)):
                        pe.wait_ge(s_, v_)
                    key = ("lo", h // 2)
                    b = pair_bank(key, h)
                    ins = causal_values(b, MV * (h % 2), MV, m_v[:, 0, h, :], m_v[:, 1, h, :], m_pT[:, h % 3, :], True, True)
                    if h % 2:
                        closed(key, ins)
                    else:
                        e.step(ins.then_inc(pe_done, 1))

                attention_pe("la", MH, l_scores, l_moved, l_values)

                units_fm("hq", "hq", hT, 2)
                units_fm("hf", "hf", hT, 2)
                for s_, v_ in e.evacuations(*[("lo", j) for j in range(4)]):
                    pe.wait_ge(s_, v_)
                held = {}

                def between_levels(n):
                    name, i = BETWEEN_LEVELS[n]
                    if name == "mo2":
                        if i % 2 == 0:
                            held["mo"] = unit("mo")
                        feature_major((name, i // 2, i % 2), held["mo"], mT, 4, 2 * (i % 2), 2)
                        if i % 2:
                            unit_used()
                    else:
                        token_major((name, i), unit(name), hT, 8, 0, 256, (0, 1))
                        unit_used()

                between_levels(0)
                pe.wait_ge(dve_done, e.at("dve", "hk"))
                for s_, v_ in e.evacuations(("hq", 0), ("hq", 1)):
                    pe.wait_ge(s_, v_)
                for n, L in enumerate([0] + LEVELS):
                    q_, k_ = (hq, hk) if L == 0 else (hQ[:, n % 2], hKp[:, n % 2])
                    if L:
                        pe.wait_ge(dve_done, e.at("dve", ("level", L)))
                    if L < P:
                        for half in range(2):
                            b = opened(("hl", L, half), 1)
                            for i in range(2):
                                h = 2 * half + i
                                for tt in range(TT):
                                    c = (2 * i + tt) * P
                                    ins = pe.matmul(b[:, c:c + P], k_[:, h, tt * P:(tt + 1) * P],
                                                    q_[:, h, tt * P:(tt + 1) * P], start=True, stop=True)
                            closed(("hl", L, half), ins)
                    else:
                        b = opened(("hl", L), 1)
                        for h in range(HH):
                            ins = pe.matmul(b[:, h * P:(h + 1) * P], k_[:, h, 0:P], q_[:, h, P:T], start=True, stop=True)
                        closed(("hl", L), ins)
                    if n + 1 < len(BETWEEN_LEVELS):
                        between_levels(n + 1)
                for s_, v_ in e.evacuations(("hl", P), ("hl", 64, 0), ("hl", 64, 1), ("hi", 0), ("hi", 1)):
                    pe.wait_ge(s_, v_)
                for tt in range(TT):
                    b = opened(("ho", tt), 1)
                    for h in range(HH):
                        o = b[:, h * P:(h + 1) * P]
                        if tt == 0:
                            ins = pe.matmul(o, hA[:, h, 0, :], hv[:, 0, h, :], start=True, stop=True)
                        else:
                            pe.matmul(o, hA[:, h, 2, :], hv[:, 0, h, :], start=True, stop=False)
                            ins = pe.matmul(o, hA[:, h, 1, :], hv[:, 1, h, :], start=False, stop=True)
                    closed(("ho", tt), ins)
                pe.wait_ge(dve_done, e.at("dve", "hg_out"))
                for j in range(2):
                    transposes(("hoT", j), [(T * i + P * tt, ho[:, tt, 2 * j + i, :]) for i in range(2) for tt in range(TT)])
                for s_, v_ in e.evacuations(("hoT", 0), ("hoT", 1)):
                    pe.wait_ge(s_, v_)
                for u in range(2):
                    w = unit("ho")
                    for j in range(2):
                        feature_major(("ho2", u, j), w, sT, 4, 2 * j, 2)
                    unit_used()

                pe.wait_ge(pool_done, e.at("pool", "memT"))
                units_fm("xk", "xk", memT, 2)
                units_tm("xv", "xv", memT, 2)
                pe.wait_ge(pool_done, e.at("pool", ("mg", "ho2", 3)))
                units_tm("wout", "wout", merged, 4)
                norm_pe("n3")
                norm_ready("n3")
                units_fm("xq", "xq", hT, 2)
                for s_, v_ in e.evacuations(("xq", 0), ("xq", 1), ("xk", 0), ("xk", 1), ("xv", 0), ("xv", 1)):
                    pe.wait_ge(s_, v_)

                def x_scores(h):
                    b = opened(("xs", h), 2)
                    for tt in range(TT):
                        ins = pe.matmul(b[:, T * tt:T * (tt + 1)], xqT[:, h, P * tt:P * (tt + 1)], xkT[:, h, :],
                                        start=True, stop=True)
                    closed(("xs", h), ins)

                def x_moved(h):
                    s = x_sc[:, h % 3, :].rearrange("p (t k) -> p t k", t=TT)
                    transposes(("xp", h), [(T * k + P * tt, s[:, tt, P * k:P * (k + 1)])
                                           for k in range(2) for tt in range(TT)])

                def x_values(h):
                    for s_, v_ in e.evacuations(("xp", h)):
                        pe.wait_ge(s_, v_)
                    b = opened(("xo", h), 1)
                    for k in range(2):
                        ins = pe.matmul(b[:, 0:T], xv[:, k, XK * h:XK * (h + 1)], x_pT[:, h % 3, T * k:T * (k + 1)],
                                        start=(k == 0), stop=(k == 1))
                    closed(("xo", h), ins)

                attention_pe("xa", XH, x_scores, x_moved, x_values)
                for s_, v_ in e.evacuations(*[("xo", h) for h in range(XH)]):
                    pe.wait_ge(s_, v_)
                for u in range(2):
                    w = unit("xo")
                    for tt in range(TT):
                        token_major(("xw", u, tt), w, xoT, 4, 0, 512, (tt,))
                    unit_used()
                norm_pe("n4")
                norm_ready("n4")
                for i in range(FF // 256):
                    w = unit("fg")
                    feature_major(("fg", i), w, hT, 8, 0, 2)
                    unit_used()
                    w = unit("fu")
                    feature_major(("fu", i), w, hT, 8, 0, 2)
                    unit_used()
                out_b = {}
                for tt in range(TT):
                    for c in range(2):
                        out_b[tt, c] = opened(("fd", tt, c), 1)
                n_down = FF // 256
                for i in range(n_down):
                    w = unit("fd")
                    if i >= n_down - 3:
                        for s_, v_ in e.evacuations(("fu", i)):
                            pe.wait_ge(s_, v_)
                    for tt in range(TT):
                        for c in range(2):
                            for k in range(2):
                                ins = pe.matmul(out_b[tt, c][:, :], gu[:, 2 * i + k, P * tt:P * (tt + 1)],
                                                w[:, k, 512 * c:512 * (c + 1)], start=(i == 0 and k == 0),
                                                stop=(i == n_down - 1 and k == 1))
                            if i == n_down - 1:
                                closed(("fd", tt, c), ins)
                    if i < n_down - 1:
                        e.step(ins.then_inc(pe_done, 1))
                    unit_used()
                unit_skip()
                while turn[0] % BANKS:
                    turn[0] += 1

            in_layers(e, pe, layer, before=lambda: total.__setitem__(slice(None), group_base))
            prog.bank_now = [t - g for t, g in zip(total, group_base)]

        @block.scalar
        def _(act):
            e = Hand(prog, "act", bank_evac)

            before = [None]

            def norm_act(n, src, ready=()):
                for s_, v_ in e.evacuations(*ready):
                    act.wait_ge(s_, v_)
                if before[0] is not None:
                    act.wait_ge(pe_done, e.at("pe", ("group", ("nT", before[0], KD // 2 - 1))))
                before[0] = n
                for tt in range(TT):
                    ins = act.activation(xn[:, tt, :], src[:, tt, :], ACT.Square, accum_out=st_a[:, 0, tt:tt + 1])
                    e.step(ins.then_inc(act_done, 1), ("sq", n))
                act.wait_ge(dve_done, e.at("dve", ("ms", n)))
                e.step(act.activation(st_c[:, :], st_b[:, :], ACT.Sqrt).then_inc(act_done, 1), ("rt", n))

            def norm_evac_act(n, gain, dst=hT):
                for j in range(0, KD // 2, 2):
                    act.wait_ge(pe_done, e.at("pe", ("group", ("nT", n, j))))
                    b = banks[e.bank(("nT", n, j))]
                    for i in range(2):
                        k, src = 2 * j + i, b[:, T * i:T * (i + 1)]
                        if gain is None:
                            ins = act.activation(dst[:, k, :], src, ACT.Copy)
                        else:
                            ins = act.activation(dst[:, k, :], src, ACT.Copy, scale=vt[:, gain + k:gain + k + 1])
                        e.evacuated(("nT", n, j), ins.then_inc(bank_evac[e.bank(("nT", n, j))], 1))

            def evac(key, dst, cols, func=ACT.Copy, p=P, src=None):
                act.wait_ge(pe_done, e.at("pe", ("group", key)))
                b = banks[e.bank(key)]
                src = b[0:p, 0:cols] if src is None else src(b)
                if len(dst.shape) == 3 and len(src.shape) == 2:
                    src = src.rearrange("p (a b) -> p a b", a=dst.shape[1])
                if len(dst.shape) == 4 and len(src.shape) == 2:
                    src = src.rearrange("p (a b c) -> p a b c", a=dst.shape[1], b=dst.shape[2])
                e.evacuated(key, act.activation(dst, src, func).then_inc(bank_evac[e.bank(key)], 1))

            def attention_act(key, nh, exps, copies, lag=2):
                for i in range(nh + lag):
                    if i < nh:
                        exps(i)
                    if i >= lag:
                        copies(i - lag)

            def causal_exps(s, slot, c0):
                for tt, (a, b) in enumerate(((0, P), (P, 3 * P))):
                    ins = act.activation(s[:, a:b], s[:, a:b], ACT.Exp, bias=a_max[:, slot, c0 + tt:c0 + tt + 1],
                                         accum_out=a_sum[:, slot, c0 + tt:c0 + tt + 1])
                    yield ins

            act.wait_ge(start_ready, 16 * START_LOADS)
            act.wait_ge(dve_done, e.at("dve", "reduced"))
            e.step(act.activation(sin_t[:, :], tr_b[:, :], ACT.Sin).then_inc(act_done, 1))
            e.step(act.activation(cos_t[:, :], tr_b[:, :], ACT.Sin, scale=0.5).then_inc(act_done, 1), "sines")
            norm_act("mem", mem_in)
            norm_evac_act("mem", None, memn)
            norm_act("n0", x)
            for s_, v_ in e.evacuations("vt1"):
                act.wait_ge(s_, v_)
            norm_evac_act("n0", V1["norm0"])
            for a, name in ((0, "mq"), (1, "mk")):
                for j in range(4):
                    evac((name, j), qk[:, a, :, 4 * j:4 * j + 4, :].rearrange("p t h d -> p t (h d)"), 512)
            act.wait_ge(dve_done, e.at("dve", ("hms", "m")))
            e.step(act.activation(hs_c[:, :], hs_b[:, :], ACT.Sqrt).then_inc(act_done, 1), ("hrt", "m"))
            for j in range(4):
                evac(("mz", j), zs[:, 2 * j:2 * j + 2, :], 512, ACT.Silu)
            for j in range(4):
                evac(("mT", 0, j), qT[:, 2 * j:2 * j + 2, :], 512)

            def m_exps(h):
                act.wait_ge(dve_done, e.at("dve", ("ma", "max", h)))
                for ins in causal_exps(sc[:, h % 3, :], h % 3, 0):
                    e.step(ins.then_inc(act_done, 1), ("ma", "exp", h))

            def m_copies(h):
                evac(("mp", h), pT[:, h % 3, 0:384], 384)

            attention_act("ma", H, m_exps, m_copies)

            def ple_act(i, ready):
                evac(("pT", i), pT.rearrange("p a b -> p (a b)")[:, 0:512], 512)
                for c in range(2):
                    for tt in range(TT):
                        evac(("pj", i, c, tt), prj[:, tt, 512 * c:512 * (c + 1)], 512)
                norm_act(("pl", i), x, ready)
                norm_evac_act(("pl", i), V1[f"ple{i}"])
                for j in range(4):
                    evac((("pg", i), j), g_tmp[:, j, :, :], 512, ACT.Sigmoid)

            ple_act(0, [("mw", j) for j in range(4)])
            act.wait_ge(dve_done, e.at("dve", ("x", 0)))
            norm_act("n1", x)
            norm_evac_act("n1", V1["norm1"])
            for j in range(4):
                evac(("nq", j), qk[:, 0, :, 4 * j:4 * j + 4, :].rearrange("p t h d -> p t (h d)"), 512)
            for j in range(6):
                evac(("nk", j), kvr[:, j, :, :], 512)
            evac(("ng", 0), gl_s[:, :, :, :], 96, ACT.Sigmoid)
            for j in range(4):
                evac(("nz", j), zs[:, 2 * j:2 * j + 2, :], 512, ACT.Silu)
            for n, c in (("ks", 8), ("kw", 8), ("nq", 32)):
                act.wait_ge(dve_done, e.at("dve", ("hms", n)))
                e.step(act.activation(hs_c[:, 0:c], hs_b[:, 0:c], ACT.Sqrt).then_inc(act_done, 1), ("hrt", n))
                if n == "kw":
                    for s in range(2):
                        for j in range(2):
                            evac(("cx", s, j), x2[0:HD, s, 2 * j:2 * j + 2, :], 512, p=HD)
            for s in range(2):
                evac(("ch", s), hid[:, s, :, :], 120, ACT.Gelu_apprx_tanh)
            evac(("cv", 0), kcf[0:NCMP, :, :], 256, p=NCMP)
            evac(("cv", 1), vcf[0:NCMP, :, :], 256, p=NCMP)
            act.wait_ge(dve_done, e.at("dve", ("hms", "kc")))
            e.step(act.activation(hs_c[0:NCMP, 0:4], hs_b[0:NCMP, 0:4], ACT.Sqrt).then_inc(act_done, 1), ("hrt", "kc"))
            for a in range(2):
                for j in range(2):
                    evac(("nkT", a, j), kT[:, 4 * a + 2 * j:4 * a + 2 * j + 2, :], 512)
            evac("ckT", kcT[:, :, 0:NCMP], 0, src=lambda b: b[:, 0:KV * NCP].rearrange("p (g n) -> p g n", g=KV)[:, :, 0:NCMP])
            for j in range(4):
                evac(("nqT", j), qT[:, 2 * j:2 * j + 2, :], 512)

            def n_exps(h):
                k = h % 3
                act.wait_ge(dve_done, e.at("dve", ("na", "max", h)))
                for tt in range(TT):
                    c = sc[:, k, 768 + NCP * tt:768 + NCP * (tt + 1)]
                    e.step(act.activation(c, c, ACT.Exp, bias=a_max[:, k, tt:tt + 1], accum_out=a_sum[:, k, tt:tt + 1]).then_inc(act_done, 1))
                for a in range(2):
                    for ins in causal_exps(sc[:, k, 384 * a:384 * (a + 1)], k, 2 + 2 * a):
                        e.step(ins.then_inc(act_done, 1), ("na", "exp", h))

            def n_copies(h):
                evac(("np", h, 0), pT[0:NCP, h % 3, 768:1024], 256, p=NCP)
                for a in range(2):
                    evac(("np", h, 1 + a), pT[:, h % 3, 384 * a:384 * (a + 1)], 384)

            attention_act("na", H, n_exps, n_copies)
            ple_act(1, [("nw", j) for j in range(4)])
            act.wait_ge(dve_done, e.at("dve", ("x", 1)))

            def layer(l):
                e.l = l
                before[0] = None
                norm_act("n2", x)
                for s_, v_ in e.evacuations("vt2"):
                    act.wait_ge(s_, v_)
                e.step(act.activation(s5v[:, 0, :], vt[:, V2["step"]:V2["step"] + SB], ACT.Exp).then_inc(act_done, 1), "s_step")
                act.wait_ge(dve_done, e.at("dve", "lb_diff"))
                e.step(act.activation(lbt[:, 2:4, :], lbt[:, 0:2, :], ACT.Exp).then_inc(act_done, 1), "lb_exp")
                norm_evac_act("n2", V2["mix"])
                act.wait_ge(dve_done, e.at("dve", "s_reduced"))
                e.step(act.activation(s5v[:, 5, :], s5v[:, 1, :], ACT.Exp).then_inc(act_done, 1))
                e.step(act.activation(s5v[:, 6, :], s5v[:, 4, :], ACT.Sin).then_inc(act_done, 1))
                e.step(act.activation(s5v[:, 7, :], s5v[:, 4, :], ACT.Sin, scale=0.5).then_inc(act_done, 1), "s_sines")
                for j in range(2):
                    evac(("u", j), uT[:, 2 * j:2 * j + 2, :], 512)
                for i in range(2):
                    evac(("ga", i), gates[:, 2 * i:2 * i + 2, :], 512, ACT.Sigmoid)
                for s in range(2):
                    evac(("bT", s), b_T[:, s, :, :], 512)
                for s in range(2):
                    evac(("cT", s), c_T[:, s, :, :], 512)
                for i in range(2, 12):
                    if i == 8:
                        act.wait_ge(pool_done, e.at("pool", "tables"))
                    evac(("ga", i), gates[:, 2 * i:2 * i + 2, :], 512, ACT.Sigmoid)
                for j in range(2):
                    evac(("ql", j), ql[:, :, 256 * j:256 * (j + 1)], 512)
                evac(("kvl", 0), kvl[:, :, :], 512)
                evac(("kr", 0), krp[:, :, :], 64)
                for q in range(4):
                    for s_, v_ in e.evacuations(("y", q)):
                        act.wait_ge(s_, v_)
                    e.step(act.activation(sT[:, q, :], y_s[:, q, :], ACT.Gelu_apprx_tanh).then_inc(act_done, 1), "s5_gelu")
                for s_, v_ in e.evacuations(("ql", 0), ("ql", 1), ("kvl", 0)):
                    act.wait_ge(s_, v_)
                for tt in range(TT):
                    e.step(act.activation(mlan[:, tt, :], ql[:, tt, :], ACT.Square, accum_out=mst[:, 0, tt:tt + 1]).then_inc(act_done, 1))
                kv_sq = m_tmp.rearrange("p a b c -> p (a b c)")[:, 0:512].rearrange("p (t c) -> p t c", t=TT)
                for tt in range(TT):
                    e.step(act.activation(kv_sq[:, tt, :], kvl[:, tt, :], ACT.Square,
                                         accum_out=mst[:, 0, 2 + tt:3 + tt]).then_inc(act_done, 1), "mla_sq")
                act.wait_ge(dve_done, e.at("dve", "mla_ms"))
                e.step(act.activation(mst[:, 2, :], mst[:, 1, :], ACT.Sqrt).then_inc(act_done, 1), "mla_rt")
                for u in range(2):
                    for j in range(2):
                        m = 4 * u + 2 * j
                        evac(("gl", u, j), sgl[:, m:m + 2, :], 512, ACT.Sigmoid)
                act.wait_ge(pe_done, e.at("pe", ("group", ("qlT", 0))))
                b = banks[e.bank(("qlT", 0))]
                for i in range(2):
                    e.evacuated(("qlT", 0), act.activation(qlT[:, i, :], b[:, T * i:T * (i + 1)], ACT.Copy,
                                                      scale=vt[:, V2["q"] + i:V2["q"] + i + 1]).then_inc(bank_evac[e.bank(("qlT", 0))], 1))
                for u in range(2):
                    for tt in range(TT):
                        evac(("uq", u, tt), m_q[:, tt, 4 * u:4 * u + 4, :].rearrange("p h d -> p (h d)"), 384)
                for c in range(2):
                    for tt in range(TT):
                        evac(("ukv", c, tt), m_k[:, tt, 4 * c:4 * c + 4, 0:NOPE], 0,
                             src=lambda b: b[:, :].rearrange("p (h d) -> p h d", h=4)[:, :, 0:NOPE])
                for j in range(4):
                    evac(("mqT", j), m_qT[0:QK, 2 * j:2 * j + 2, :], 512, p=QK)

                def l_exps(h):
                    act.wait_ge(dve_done, e.at("dve", ("la", "max", h)))
                    for ins in causal_exps(m_sc[:, h % 3, :], h % 3, 0):
                        e.step(ins.then_inc(act_done, 1), ("la", "exp", h))

                def l_copies(h):
                    evac(("lp", h), m_pT[:, h % 3, 0:384], 384)

                attention_act("la", MH, l_exps, l_copies)
                for s_, v_ in e.evacuations(*[("lo", j) for j in range(4)]):
                    act.wait_ge(s_, v_)
                for j in range(2):
                    evac(("hq", j), hq[:, 2 * j:2 * j + 2, :], 512, ACT.Silu)
                for j in range(2):
                    evac(("hf", j), hb[:, 2 * j:2 * j + 2, :], 512, ACT.Sigmoid)

                def between_levels(n):
                    name, j = BETWEEN_LEVELS[n]
                    if name != "mo2":
                        dst, func = (hv, ACT.Copy) if name == "hi" else (hg, ACT.Silu)
                        evac((name, j), dst[:, :, 2 * j:2 * j + 2, :].rearrange("p t h d -> p t (h d)"), 512, func)

                act.wait_ge(dve_done, e.at("dve", "hf"))
                e.step(act.activation(hE[:, :, :], hb[:, :, :], ACT.Ln).then_inc(act_done, 1), "lnf")
                between_levels(0)
                for n, L in enumerate(LEVELS, 1):
                    act.wait_ge(dve_done, e.at("dve", ("sub", L)))
                    e.step(act.activation(hE[:, :, :], hE[:, :, :], ACT.Exp).then_inc(act_done, 1), ("hexp", L))
                    if n < len(BETWEEN_LEVELS):
                        between_levels(n)
                act.wait_ge(dve_done, e.at("dve", "hg_ms"))
                e.step(act.activation(hs_c[:, 0:8], hs_b[:, 0:8], ACT.Sqrt).then_inc(act_done, 1), "hg_rt")
                for j in range(2):
                    act.wait_ge(pe_done, e.at("pe", ("group", ("hoT", j))))
                    b = banks[e.bank(("hoT", j))]
                    e.evacuated(("hoT", j), act.activation(sT[:, 2 * j:2 * j + 2, :], b[:, :].rearrange("p (a b) -> p a b", a=2),
                                                      ACT.Copy, scale=vt[:, V2["hgn"]:V2["hgn"] + 1]).then_inc(bank_evac[e.bank(("hoT", j))], 1))
                for j in range(2):
                    evac(("xk", j), xkT[:, 2 * j:2 * j + 2, :], 512)
                for j in range(2):
                    evac(("xv", j), xv[:, :, 256 * j:256 * (j + 1)], 512)
                norm_act("n3", x, [("wout", j) for j in range(4)])
                norm_evac_act("n3", V2["cross"])
                for j in range(2):
                    evac(("xq", j), xqT[:, 2 * j:2 * j + 2, :], 512)

                def x_exps(h):
                    k = h % 3
                    act.wait_ge(dve_done, e.at("dve", ("xa", "max", h)))
                    b = banks[e.bank(("xs", h))]
                    for tt in range(TT):
                        ins = act.activation(x_sc[:, k, T * tt:T * (tt + 1)], b[:, T * tt:T * (tt + 1)], ACT.Exp,
                                             bias=a_max[:, k, tt:tt + 1], scale=XK ** -0.5,
                                             accum_out=a_sum[:, k, tt:tt + 1])
                        if tt:
                            e.evacuated(("xs", h), ins.then_inc(bank_evac[e.bank(("xs", h))], 1))

                def x_copies(h):
                    evac(("xp", h), x_pT[:, h % 3, :], 512)

                attention_act("xa", XH, x_exps, x_copies)
                norm_act("n4", x, [("xw", u, tt) for u in range(2) for tt in range(TT)])
                norm_evac_act("n4", V2["ffn"])
                for i in range(FF // 256):
                    if i >= 4:
                        for s_, v_ in e.evacuations(("fu", i - 4)):
                            act.wait_ge(s_, v_)
                    evac(("fg", i), f_tmp[:, i % 4, :], 512, ACT.Silu)
                for s_, v_ in e.evacuations(*[("fd", tt, c) for tt in range(TT) for c in range(2)]):
                    act.wait_ge(s_, v_)

            in_layers(e, act, layer)
            norm_act("nf", x)

        @block.vector
        def _(dve):
            e = Hand(prog, "dve", bank_evac)
            tt_, ts_, stt_ = dve.tensor_tensor, dve.tensor_scalar, dve.scalar_tensor_tensor

            def norm_dve(n, src, dst=xn):
                dve.wait_ge(act_done, e.at("act", ("sq", n)))
                e.step(ts_(st_b[:, :], st_a[:, 0, :], 1.0 / D, EPS, ALU.mult, ALU.add).then_inc(dve_done, 1), ("ms", n))
                dve.wait_ge(act_done, e.at("act", ("rt", n)))
                e.step(dve.reciprocal(st_b[:, :], st_c[:, :]).then_inc(dve_done, 1))
                dve.wait_ge(dve_done, e.last())
                for tt in range(TT):
                    e.step(ts_(dst[:, tt, :], src[:, tt, :], st_b[:, tt:tt + 1], None, ALU.mult).then_inc(dve_done, 1), ("xn", n))

            def norm_evac_dve(n, gain, dst=hT):
                for j in range(1, KD // 2, 2):
                    dve.wait_ge(pe_done, e.at("pe", ("group", ("nT", n, j))))
                    b = banks[e.bank(("nT", n, j))]
                    for i in range(2):
                        k, src = 2 * j + i, b[:, T * i:T * (i + 1)]
                        if gain is None:
                            ins = dve.tensor_copy(dst[:, k, :], src)
                        else:
                            ins = ts_(dst[:, k, :], src, vt[:, gain + k:gain + k + 1], None, ALU.mult)
                        e.evacuated(("nT", n, j), ins.then_inc(bank_evac[e.bank(("nT", n, j))], 1))

            def evac(key, dst, cols, p=P, src=None):
                dve.wait_ge(pe_done, e.at("pe", ("group", key)))
                b = banks[e.bank(key)]
                src = b[0:p, 0:cols] if src is None else src(b)
                if len(dst.shape) == 3 and len(src.shape) == 2:
                    src = src.rearrange("p (a b) -> p a b", a=dst.shape[1])
                e.evacuated(key, dve.tensor_copy(dst, src).then_inc(bank_evac[e.bank(key)], 1))

            def reduce_angle(dst, kk, ang, mark):
                e.step(ts_(kk, ang, 1.0 / (2 * np.pi), ROUND, ALU.mult, ALU.add).then_inc(dve_done, 1))
                dve.wait_ge(dve_done, e.last())
                e.step(ts_(kk, kk, -ROUND, None, ALU.add).then_inc(dve_done, 1))
                dve.wait_ge(dve_done, e.last())
                e.step(stt_(dst, kk, -TWO_PI[0], ang, ALU.mult, ALU.add).then_inc(dve_done, 1))
                dve.wait_ge(dve_done, e.last())
                for part in TWO_PI[1:]:
                    e.step(stt_(dst, kk, -part, dst, ALU.mult, ALU.add).then_inc(dve_done, 1))
                    dve.wait_ge(dve_done, e.last())
                e.step(ts_(dst, dst, PI, -PI, ALU.min, ALU.max).then_inc(dve_done, 1), mark)
                dve.wait_ge(dve_done, e.last())

            def head_norm(n, v, p, count, gain_of, tmp_v):
                e.step(tt_(tmp_v, v, v, ALU.mult).then_inc(dve_done, 1))
                dve.wait_ge(dve_done, e.last())
                e.step(dve.tensor_reduce(hs_a[0:p, 0:count], tmp_v, AX.X, ALU.add).then_inc(dve_done, 1))
                dve.wait_ge(dve_done, e.last())
                e.step(ts_(hs_b[0:p, 0:count], hs_a[0:p, 0:count], 1.0 / HD, EPS, ALU.mult, ALU.add).then_inc(dve_done, 1), ("hms", n))
                dve.wait_ge(act_done, e.at("act", ("hrt", n)))
                e.step(dve.reciprocal(hs_a[0:p, 0:count], hs_c[0:p, 0:count]).then_inc(dve_done, 1))
                dve.wait_ge(dve_done, e.last())
                e.step(tt_(v, v, bc(hs_a[0:p, 0:count], 2, [count, HD]), ALU.mult).then_inc(dve_done, 1))
                dve.wait_ge(dve_done, e.last())
                for part, gain in gain_of:
                    e.step(tt_(part, part, bc(gains[0:p, gain, :], 1, [part.shape[1], HD]), ALU.mult).then_inc(dve_done, 1))
                dve.wait_ge(dve_done, e.last())

            def rope(v, c, s, half, t, mark):
                a, b = v.shape[1], v.shape[2]
                x1, x2_ = v[:, :, :, 0:half], v[:, :, :, half:2 * half]
                c, s = bc(c, 2, [a, b, half]), bc(s, 2, [a, b, half])
                e.step(tt_(t[0], x1, c, ALU.mult).then_inc(dve_done, 1))
                e.step(tt_(t[1], x2_, s, ALU.mult).then_inc(dve_done, 1))
                e.step(tt_(t[2], x2_, c, ALU.mult).then_inc(dve_done, 1))
                e.step(tt_(t[3], x1, s, ALU.mult).then_inc(dve_done, 1))
                dve.wait_ge(dve_done, e.last())
                e.step(tt_(x1, t[0], t[1], ALU.subtract).then_inc(dve_done, 1))
                e.step(tt_(x2_, t[2], t[3], ALU.add).then_inc(dve_done, 1), mark)
                dve.wait_ge(dve_done, e.last())

            def temps(p, a, b, half):
                return [tmp[0:p, i, 0:a * b * half].rearrange("p (a b c) -> p a b c", a=a, b=b) for i in range(4)]

            def attention_dve(key, nh, scores, sums, outs, lag=3):
                for i in range(nh + lag + 1):
                    if 0 <= i - lag - 1 < nh:
                        outs(i - lag - 1)
                    if i < nh:
                        scores(i)
                    if 1 <= i <= nh:
                        sums(i - 1)

            def causal_max(bank_key, s, slot, c0, scale):
                dve.wait_ge(pe_done, e.at("pe", ("group", bank_key)))
                b = banks[e.bank(bank_key)]
                e.evacuated(bank_key, stt_(s, b[:, 0:384], scale, causal3[:, :, :].rearrange("p a b -> p (a b)"),
                                      ALU.mult, ALU.add).then_inc(bank_evac[e.bank(bank_key)], 1))
                for s_, v_ in e.evacuations(bank_key):
                    dve.wait_ge(s_, v_)
                dve.tensor_reduce(a_max[:, slot, c0:c0 + 1], s[:, 0:P], AX.X, ALU.max, negate=True)
                return dve.tensor_reduce(a_max[:, slot, c0 + 1:c0 + 2], s[:, P:3 * P], AX.X, ALU.max, negate=True)

            dve.wait_ge(start_ready, 16 * START_LOADS)
            dve.wait_ge(pool_done, e.at("pool", "constants"))
            e.step(dve.tensor_copy(pos_f[:, 0:5], pos_i[:, 0:5]).then_inc(dve_done, 1))
            dve.wait_ge(dve_done, e.last())
            for tt in range(TT):
                e.step(ts_(angles[:, 32 * tt:32 * tt + 32], freqs[:, 0:32], pos_f[:, tt:tt + 1], None, ALU.mult).then_inc(dve_done, 1))
                e.step(ts_(angles[:, 96 + 16 * tt:112 + 16 * tt], freqs[:, 32:48], pos_f[:, 3 + tt:4 + tt], None, ALU.mult).then_inc(dve_done, 1))
            e.step(ts_(angles[:, 64:96], freqs[:, 0:32], pos_f[:, 2:3], None, ALU.mult).then_inc(dve_done, 1))
            dve.wait_ge(dve_done, e.last())
            reduce_angle(tr_b[:, :], tr_a[:, :], angles[:, :], "reduced")
            dve.wait_ge(act_done, e.at("act", "sines"))
            e.step(tt_(cos_t[:, :], cos_t[:, :], cos_t[:, :], ALU.mult).then_inc(dve_done, 1))
            dve.wait_ge(dve_done, e.last())
            e.step(ts_(cos_t[:, :], cos_t[:, :], -2.0, 1.0, ALU.mult, ALU.add).then_inc(dve_done, 1))
            dve.wait_ge(dve_done, e.last())
            e.step(ts_(chm_i[:, 1:2], chm_i[:, 0:1], 4, 1, ALU.logical_shift_right, ALU.bitwise_and).then_inc(dve_done, 1))
            dve.wait_ge(dve_done, e.last())
            e.step(dve.tensor_copy(chm[:, 0, 1:2], chm_i[:, 1:2]).then_inc(dve_done, 1))
            dve.wait_ge(dve_done, e.last())
            e.step(ts_(chm[:, 0, 0:1], chm[:, 0, 1:2], -1.0, 1.0, ALU.mult, ALU.add).then_inc(dve_done, 1))
            dve.wait_ge(dve_done, e.last())
            e.step(ts_(chm[:, 1, :], chm[:, 0, :], -1.0, None, ALU.mult).then_inc(dve_done, 1))
            dve.wait_ge(dve_done, e.last())
            dve.wait_ge(pe_done, e.at("pe", ("group", "vt1")))
            b = banks[e.bank("vt1")]
            e.evacuated("vt1", dve.tensor_copy(vt[:, 0:64], b[:, 0:64]).then_inc(bank_evac[e.bank("vt1")], 1))
            for s_, v_ in e.evacuations("vt1"):
                dve.wait_ge(s_, v_)
            norm_dve("mem", mem_in)
            norm_evac_dve("mem", None, memn)
            norm_dve("n0", x)
            norm_evac_dve("n0", V1["norm0"])

            for s_, v_ in e.evacuations(*[("mq", j) for j in range(4)], *[("mk", j) for j in range(4)]):
                dve.wait_ge(s_, v_)
            qkf = qk.rearrange("p a t h d -> p (a t h d)").rearrange("p (n d) -> p n d", d=HD)
            head_norm("m", qkf, P, 64, [(qkf[:, 0:32, :], 0), (qkf[:, 32:64, :], 1)],
                      tmp.rearrange("p a b -> p (a b)").rearrange("p (n d) -> p n d", d=HD))
            for a in range(2):
                rope(qk[:, a], cos_t[:, 0:64].rearrange("p (t c) -> p t c", t=TT),
                     sin_t[:, 0:64].rearrange("p (t c) -> p t c", t=TT), 32, temps(P, TT, H, 32), ("roped", "m", a))
            for j in range(4):
                evac(("mv", j), vf[:, :, 4 * j:4 * j + 4, :].rearrange("p t h d -> p t (h d)"), 512)
            for j in range(4):
                evac(("mT", 1, j), kT[:, 2 * j:2 * j + 2, :], 512)

            def m_scores(h):
                if h >= 3:
                    dve.wait_ge(pe_done, e.at("pe", ("group", ("mp", h - 3))))
                e.step(causal_max(("ms", h), sc[:, h % 3, 0:384], h % 3, 0, HD ** -0.5).then_inc(dve_done, 1), ("ma", "max", h))

            def m_sums(h):
                dve.wait_ge(act_done, e.at("act", ("ma", "exp", h)))
                e.step(dve.reciprocal(a_rec[:, h % 3, 0:2], a_sum[:, h % 3, 0:2]).then_inc(dve_done, 1), ("ma", "rec", h))

            def gated_out(key, h):
                if h % 2:
                    j = h // 2
                    dve.wait_ge(pe_done, e.at("pe", ("group", (key, j))))
                    b = banks[e.bank((key, j))]
                    e.evacuated((key, j), tt_(oT1[:, j, :], b[:, 0:T], zs[:, j, :], ALU.mult).then_inc(bank_evac[e.bank((key, j))], 1))

            for s_, v_ in e.evacuations(*[("mz", j) for j in range(4)]):
                dve.wait_ge(s_, v_)
            attention_dve("ma", H, m_scores, m_sums, lambda h: gated_out("mo", h))

            def add_x(key, j):
                dve.wait_ge(pe_done, e.at("pe", ("group", (key, j))))
                b = banks[e.bank((key, j))]
                xs = x[:, :, 256 * j:256 * (j + 1)]
                e.evacuated((key, j), tt_(xs, xs, b[:, :].rearrange("p (t c) -> p t c", t=TT), ALU.add).then_inc(bank_evac[e.bank((key, j))], 1))

            def ple_dve(i, key):
                for j in range(4):
                    add_x(key, j)
                for s_, v_ in e.evacuations(*[(key, j) for j in range(4)]):
                    dve.wait_ge(s_, v_)
                norm_dve(("pl", i), x)
                norm_evac_dve(("pl", i), V1[f"ple{i}"])
                for j in range(4):
                    for s_, v_ in e.evacuations((("pg", i), j)):
                        dve.wait_ge(s_, v_)
                    e.step(tt_(g_tmp[:, j], g_tmp[:, j], prj[:, :, 256 * j:256 * (j + 1)], ALU.mult).then_inc(dve_done, 1))
                    dve.wait_ge(dve_done, e.last())
                    xs = x[:, :, 256 * j:256 * (j + 1)]
                    e.step(tt_(xs, xs, g_tmp[:, j], ALU.add).then_inc(dve_done, 1), ("x", i))
                    dve.wait_ge(dve_done, e.last())

            ple_dve(0, "mw")
            norm_dve("n1", x)
            norm_evac_dve("n1", V1["norm1"])

            cos1, sin1 = (t[:, 0:64].rearrange("p (t c) -> p t c", t=TT) for t in (cos_t, sin_t))
            tmp_rows = tmp.rearrange("p a b -> p (a b)").rearrange("p (n d) -> p n d", d=HD)
            for n, kind, gain in (("ks", 2, 4), ("kw", 4, 5)):
                for s_, v_ in e.evacuations(("nk", kind)):
                    dve.wait_ge(s_, v_)
                v = kvr[:, kind]
                head_norm(n, v, P, 8, [(v, gain)], tmp_rows[:, 0:8, :])
                rope(v.rearrange("p (t g) d -> p t g d", t=TT), cos1, sin1, 32, temps(P, TT, KV, 32), ("roped", n))
            for s in range(2):
                for j in range(2):
                    dve.wait_ge(pe_done, e.at("pe", ("group", ("cx", s, j))))
                    b = banks[e.bank(("cx", s, j))]
                    e.evacuated(("cx", s, j), dve.tensor_copy(
                        x2[HD:P, s, 2 * j:2 * j + 2, 0:T - 1],
                        b[HD:P, :].rearrange("p (g t) -> p g t", g=2)[:, :, 1:T]).then_inc(bank_evac[e.bank(("cx", s, j))], 1))
            for s in range(2):
                for s_, v_ in e.evacuations(("cx", s, 0), ("cx", s, 1)):
                    dve.wait_ge(s_, v_)
                for g in range(KV):
                    for a in range(2):
                        src = x2[:, s, g, 16 * a:16 * a + 240].rearrange("p (n j c) -> p j n c", n=NCMP, c=2)[:, :, :, 0]
                        c0 = V1["pe"] + 16 * s + 8 * a
                        e.step(tt_(flat_v[s][:, 8 * a:8 * a + 8, NCMP * g:NCMP * (g + 1)], src,
                                  bc(vt[:, c0:c0 + 8], 2, [8, NCMP]), ALU.add).then_inc(dve_done, 1), ("flat", s))
            for s_, v_ in e.evacuations(*[("nq", j) for j in range(4)]):
                dve.wait_ge(s_, v_)
            v = qkf[:, 0:32, :]
            head_norm("nq", v, P, 32, [(v, 2)], tmp_rows[:, 0:32, :])
            rope(qk[:, 0], cos1, sin1, 32, temps(P, TT, H, 32), ("roped", "n", 0))
            for s_, v_ in e.evacuations(("cv", 0)):
                dve.wait_ge(s_, v_)
            v = kcf[0:NCMP, :, :]
            head_norm("kc", v, NCMP, KV, [(v, 3)], tmp_rows[0:NCMP, 0:KV, :])
            rope(v.unsqueeze(1), cos_t[0:NCMP, 64:96].unsqueeze(1), sin_t[0:NCMP, 64:96].unsqueeze(1), 32,
                 temps(NCMP, 1, KV, 32), None)
            e.step(dve.tensor_copy(kcd[0:NCMP], bc(v, 2, [KV, 2, HD])).then_inc(dve_done, 1), "ckv")

            def n_scores(h):
                k = h % 3
                if h >= 3:
                    dve.wait_ge(pe_done, e.at("pe", ("group", ("np", h - 3, 2))))
                dve.wait_ge(pe_done, e.at("pe", ("group", ("ns", h, 0))))
                b = banks[e.bank(("ns", h, 0))]
                e.evacuated(("ns", h, 0), stt_(sc[:, k, 768:800], b[:, 0:32], HD ** -0.5,
                                          cmp_neg.rearrange("p a b -> p (a b)"), ALU.mult, ALU.add).then_inc(bank_evac[e.bank(("ns", h, 0))], 1))
                for s_, v_ in e.evacuations(("ns", h, 0)):
                    dve.wait_ge(s_, v_)
                dve.tensor_reduce(a_max[:, k, 0:2], sc[:, k, 768:800].rearrange("p (t n) -> p t n", t=TT), AX.X, ALU.max,
                                  negate=True)
                causal_max(("ns", h, 1), sc[:, k, 0:384], k, 2, HD ** -0.5)
                e.step(causal_max(("ns", h, 2), sc[:, k, 384:768], k, 4, HD ** -0.5).then_inc(dve_done, 1), ("na", "max", h))

            def n_sums(h):
                k = h % 3
                dve.wait_ge(act_done, e.at("act", ("na", "exp", h)))
                e.step(dve.reciprocal(a_rec[:, k, :], a_sum[:, k, :]).then_inc(dve_done, 1))
                dve.wait_ge(dve_done, e.last())
                e.step(tt_(a_nrm[:, k, :].rearrange("p (b t) -> p b t", b=3), a_rec[:, k, :].rearrange("p (b t) -> p b t", b=3),
                          gl_s[:, :, h, :].rearrange("p t b -> p b t"), ALU.mult).then_inc(dve_done, 1), ("na", "rec", h))

            for s_, v_ in e.evacuations(("ng", 0), *[("nz", j) for j in range(4)]):
                dve.wait_ge(s_, v_)
            attention_dve("na", H, n_scores, n_sums, lambda h: gated_out("no", h))
            ple_dve(1, "nw")
            e.step(dve.memset(low[:, :], 0.0).then_inc(dve_done, 1))
            dve.wait_ge(dve_done, e.last())

            def layer(l):
                e.l = l
                sv = lambda i: s5v[:, i, :]
                dve.wait_ge(params_ready, 16 * PARAM_LOADS + l * 16 * PARAM_LOADS)
                e.step(dve.tensor_copy(rows[96:112, :].rearrange("p (a b) -> p a b", a=2),
                                      bc(lsr[96:112, :], 2, [2, SN])).then_inc(dve_done, 1), "log_steps")
                dve.wait_ge(pe_done, e.at("pe", ("group", "vt2")))
                b = banks[e.bank("vt2")]
                e.evacuated("vt2", dve.tensor_copy(vt[:, :], b[:, 0:P]).then_inc(bank_evac[e.bank("vt2")], 1))
                for s_, v_ in e.evacuations("vt2"):
                    dve.wait_ge(s_, v_)
                b0, b1 = vt[:, V2["lb0"]:V2["lb0"] + HH], vt[:, V2["lb1"]:V2["lb1"] + HH]
                e.step(tt_(lbt[:, 2, :], b0, b1, ALU.max).then_inc(dve_done, 1))
                dve.wait_ge(dve_done, e.last())
                e.step(tt_(lbt[:, 0, :], b0, lbt[:, 2, :], ALU.subtract).then_inc(dve_done, 1))
                e.step(tt_(lbt[:, 1, :], b1, lbt[:, 2, :], ALU.subtract).then_inc(dve_done, 1), "lb_diff")
                norm_dve("n2", x)
                dve.wait_ge(act_done, e.at("act", "s_step"))
                lr, li = vt[:, V2["lam_re"]:V2["lam_re"] + SB], vt[:, V2["lam_im"]:V2["lam_im"] + SB]
                e.step(tt_(sv(1), lr, sv(0), ALU.mult).then_inc(dve_done, 1))
                e.step(tt_(sv(2), li, sv(0), ALU.mult).then_inc(dve_done, 1))
                dve.wait_ge(dve_done, e.last())
                reduce_angle(sv(4), sv(3), sv(2), "s_reduced")
                norm_evac_dve("n2", V2["mix"])
                e.step(dve.memset(b_diag, 0.0).then_inc(dve_done, 1))
                e.step(tt_(sv(11), lr, lr, ALU.mult).then_inc(dve_done, 1))
                e.step(tt_(sv(12), li, li, ALU.mult).then_inc(dve_done, 1))
                dve.wait_ge(dve_done, e.last())
                e.step(tt_(sv(11), sv(11), sv(12), ALU.add).then_inc(dve_done, 1))
                dve.wait_ge(dve_done, e.last())
                dve.wait_ge(act_done, e.at("act", "s_sines"))
                e.step(tt_(sv(8), sv(7), sv(7), ALU.mult).then_inc(dve_done, 1))
                dve.wait_ge(dve_done, e.last())
                e.step(ts_(sv(8), sv(8), -2.0, 1.0, ALU.mult, ALU.add).then_inc(dve_done, 1), "s_cos")
                dve.wait_ge(dve_done, e.last())
                e.step(dve.reciprocal(sv(13), sv(11)).then_inc(dve_done, 1))
                e.step(tt_(sv(10), sv(5), sv(6), ALU.mult).then_inc(dve_done, 1))
                e.step(tt_(sv(9), sv(5), sv(8), ALU.mult).then_inc(dve_done, 1))
                dve.wait_ge(dve_done, e.last())
                e.step(ts_(sv(9), sv(9), -1.0, None, ALU.add).then_inc(dve_done, 1))
                dve.wait_ge(dve_done, e.last())
                e.step(tt_(sv(14), sv(9), lr, ALU.mult).then_inc(dve_done, 1))
                e.step(tt_(sv(15), sv(10), li, ALU.mult).then_inc(dve_done, 1))
                e.step(tt_(sv(16), sv(10), lr, ALU.mult).then_inc(dve_done, 1))
                e.step(tt_(sv(17), sv(9), li, ALU.mult).then_inc(dve_done, 1))
                dve.wait_ge(dve_done, e.last())
                e.step(tt_(sv(14), sv(14), sv(15), ALU.add).then_inc(dve_done, 1))
                e.step(tt_(sv(16), sv(16), sv(17), ALU.subtract).then_inc(dve_done, 1))
                dve.wait_ge(dve_done, e.last())
                e.step(tt_(sv(18), sv(14), sv(13), ALU.mult).then_inc(dve_done, 1))
                e.step(tt_(sv(19), sv(16), sv(13), ALU.mult).then_inc(dve_done, 1))
                dve.wait_ge(dve_done, e.last())
                cr, ci = bc(sv(18), 2, [SB, SC]), bc(sv(19), 2, [SB, SC])
                e.step(tt_(b_tmp[0], b_raw[:, 0], cr, ALU.mult).then_inc(dve_done, 1))
                e.step(tt_(b_tmp[1], b_raw[:, 1], ci, ALU.mult).then_inc(dve_done, 1))
                e.step(tt_(b_tmp[2], b_raw[:, 1], cr, ALU.mult).then_inc(dve_done, 1))
                e.step(tt_(b_tmp[3], b_raw[:, 0], ci, ALU.mult).then_inc(dve_done, 1))
                dve.wait_ge(dve_done, e.last())
                for g in range(2):
                    r = slice(SN * g, SN * (g + 1))
                    e.step(tt_(b_diag[r, 0, :, g, :], b_tmp[0][r], b_tmp[1][r], ALU.subtract).then_inc(dve_done, 1))
                    e.step(tt_(b_diag[r, 1, :, g, :], b_tmp[2][r], b_tmp[3][r], ALU.add).then_inc(dve_done, 1), "b_diag")
                for s in range(2):
                    mask = chm[:, s, :].unsqueeze(1).unsqueeze(3).to_broadcast([P, 4, 2, SN])
                    e.step(tt_(c_diag[:, s], bc(c_raw[:, s], 2, [4, 2, SN]), mask, ALU.mult).then_inc(dve_done, 1), "c_diag")
                dve.wait_ge(pool_done, e.at("pool", "tables"))
                for s_, v_ in e.evacuations(("u", 0), ("u", 1)):
                    dve.wait_ge(s_, v_)

                def y_part(q):
                    dve.wait_ge(pe_done, e.at("pe", ("group", ("y", q))))
                    b = banks[e.bank(("y", q))]
                    e.evacuated(("y", q), stt_(y_s[:, q, :], uT[:, q, :], vt[:, V2["skip"] + q:V2["skip"] + q + 1],
                                          b[:, 0:T], ALU.mult, ALU.add).then_inc(bank_evac[e.bank(("y", q))], 1))

                for blk in range(SB):
                    k = blk % 2
                    c, s = e_re[:, blk, 0:T], e_im[:, blk, 0:T]
                    if blk >= 6 and (blk - 6) % 4 == 0:
                        y_part((blk - 6) // 4)
                    dve.wait_ge(pe_done, e.at("pe", ("group", ("bu", blk))))
                    b = banks[e.bank(("bu", blk))]
                    re, im = b[:, 0:T], b[:, T:2 * T]
                    for i, (u, v) in enumerate(((re, c), (im, s), (im, c), (re, s))):
                        e.evacuated(("bu", blk), tt_(z_tm[:, i, :], u, v, ALU.mult).then_inc(bank_evac[e.bank(("bu", blk))], 1))
                    for s_, v_ in e.evacuations(("bu", blk)):
                        dve.wait_ge(s_, v_)
                    e.step(tt_(z_in[:, k, 0, :], z_tm[:, 0, :], z_tm[:, 1, :], ALU.add).then_inc(dve_done, 1))
                    e.step(tt_(z_in[:, k, 1, :], z_tm[:, 2, :], z_tm[:, 3, :], ALU.subtract).then_inc(dve_done, 1))
                    dve.wait_ge(dve_done, e.last())
                    if blk >= 2:
                        dve.wait_ge(pool_done, e.at("pool", ("state", blk - 2)))
                    rate = s5v[:, 5, blk:blk + 1].to_broadcast([P, T])
                    for i in range(2):
                        e.step(dve.tensor_tensor_scan(z_st[:, k, i, :], rate, z_in[:, k, i, :], 0.0, ALU.mult, ALU.add).then_inc(dve_done, 1), ("z", blk))
                y_part(3)

                dve.wait_ge(act_done, e.at("act", "mla_sq"))
                e.step(ts_(mst[:, 1, 0:2], mst[:, 0, 0:2], 1.0 / QR, EPS, ALU.mult, ALU.add).then_inc(dve_done, 1))
                e.step(ts_(mst[:, 1, 2:4], mst[:, 0, 2:4], 1.0 / KR, EPS, ALU.mult, ALU.add).then_inc(dve_done, 1), "mla_ms")
                dve.wait_ge(act_done, e.at("act", "mla_rt"))
                e.step(dve.reciprocal(mst[:, 1, :], mst[:, 2, :]).then_inc(dve_done, 1))
                dve.wait_ge(dve_done, e.last())
                for tt in range(TT):
                    e.step(ts_(mlan[:, tt, :], ql[:, tt, :], mst[:, 1, tt:tt + 1], None, ALU.mult).then_inc(dve_done, 1), "mla_xn")
                for tt in range(TT):
                    e.step(ts_(kvl[:, tt, :], kvl[:, tt, :], mst[:, 1, 2 + tt:3 + tt], None, ALU.mult).then_inc(dve_done, 1), "mla_kn")
                for u in range(2, 4):
                    for j in range(2):
                        m = 4 * (u - 2) + 2 * j
                        dve.wait_ge(pe_done, e.at("pe", ("group", ("gl", u, j))))
                        b = banks[e.bank(("gl", u, j))]
                        dve.wait_ge(pool_done, e.at("pool", ("sg", u - 2, j)))
                        e.evacuated(("gl", u, j), tt_(merged[:, m:m + 2, :], b[:, :].rearrange("p (a b) -> p a b", a=2),
                                                 sgl[:, m:m + 2, :], ALU.mult).then_inc(bank_evac[e.bank(("gl", u, j))], 1))
                for key, dst, k0, gain in ((("qlT", 1), qlT, 2, V2["q"]), ("kvT", kvT, 0, V2["kv"])):
                    dve.wait_ge(pe_done, e.at("pe", ("group", key)))
                    b = banks[e.bank(key)]
                    for k in range(k0, k0 + 2):
                        src = b[:, T * (k - k0):T * (k - k0 + 1)]
                        e.evacuated(key, ts_(dst[:, k, :], src, vt[:, gain + k:gain + k + 1], None, ALU.mult).then_inc(bank_evac[e.bank(key)], 1))
                cos2, sin2 = (t[:, 96:128].rearrange("p (t c) -> p t c", t=TT) for t in (cos_t, sin_t))
                rt = [m_tmp[:, i, :, :].rearrange("p (a b) c -> p a b c", a=TT) for i in range(4)]
                rk = [m_tmp[:, i, 0:TT, :].unsqueeze(2) for i in range(4)]
                for s_, v_ in e.evacuations(("kr", 0)):
                    dve.wait_ge(s_, v_)
                rope(krp.unsqueeze(2), cos2, sin2, ROPE // 2, rk, None)
                e.step(dve.tensor_copy(m_k[:, :, :, NOPE:QK], bc(krp, 2, [TT, MH, ROPE])).then_inc(dve_done, 1))
                for c in range(2):
                    for tt in range(TT):
                        dve.wait_ge(pe_done, e.at("pe", ("group", ("ukv", c, tt))))
                        b = banks[e.bank(("ukv", c, tt))]
                        dve.wait_ge(bank_evac[e.bank(("ukv", c, tt))], e.evac_value(("ukv", c, tt)) - 1)
                        e.evacuated(("ukv", c, tt), dve.tensor_copy(
                            m_v[:, tt, 4 * c:4 * c + 4, :], b[:, :].rearrange("p (h d) -> p h d", h=4)[:, :, NOPE:]).then_inc(bank_evac[e.bank(("ukv", c, tt))], 1))
                for s_, v_ in e.evacuations(*[("uq", u, tt) for u in range(2) for tt in range(TT)]):
                    dve.wait_ge(s_, v_)
                rope(m_q[:, :, :, NOPE:QK], cos2, sin2, ROPE // 2, rt, "mq_roped")
                for s_, v_ in e.evacuations(*[("ukv", c, tt) for c in range(2) for tt in range(TT)]):
                    dve.wait_ge(s_, v_)
                e.step(dve.tensor_copy(m_tmp[:, 0, 0, 0:1], krp[:, 0, 0:1]).then_inc(dve_done, 1), "mk_roped")
                for j in range(4):
                    evac(("mkT", j), m_kT[0:QK, 2 * j:2 * j + 2, :], 512, p=QK)

                def l_scores(h):
                    if h >= 3:
                        dve.wait_ge(pe_done, e.at("pe", ("group", ("lp", h - 3))))
                    e.step(causal_max(("ls", h), m_sc[:, h % 3, 0:384], h % 3, 0, QK ** -0.5).then_inc(dve_done, 1), ("la", "max", h))

                def l_sums(h):
                    dve.wait_ge(act_done, e.at("act", ("la", "exp", h)))
                    e.step(dve.reciprocal(a_rec[:, h % 3, 0:2], a_sum[:, h % 3, 0:2]).then_inc(dve_done, 1), ("la", "rec", h))

                def l_outs(h):
                    if h % 2:
                        evac(("lo", h // 2), mT[:, h // 2, :], T)

                attention_dve("la", MH, l_scores, l_sums, l_outs)

                dve.wait_ge(act_done, e.at("act", "lb_exp"))
                e.step(ts_(lbt[:, 0, :], low[:, :], -1.0, 1.0, ALU.mult, ALU.add).then_inc(dve_done, 1))
                dve.wait_ge(dve_done, e.last())
                for s_, v_ in e.evacuations(("hf", 0), ("hf", 1)):
                    dve.wait_ge(s_, v_)
                for h in range(HH):
                    e.step(ts_(hb[:, h, :], hb[:, h, :], lbt[:, 0, h:h + 1], low[:, h:h + 1], ALU.mult, ALU.add).then_inc(dve_done, 1))
                dve.wait_ge(dve_done, e.last())
                e.step(ts_(hk[:, :, :], hb[:, :, :], -1.0, 1.0, ALU.mult, ALU.add).then_inc(dve_done, 1), "hk")
                dve.wait_ge(dve_done, e.last())
                e.step(ts_(hb[:, :, :], hb[:, :, :], 2.0 ** -63, None, ALU.max).then_inc(dve_done, 1), "hf")
                dve.wait_ge(dve_done, e.last())
                dve.wait_ge(act_done, e.at("act", "lnf"))
                for h in range(HH):
                    e.step(dve.tensor_tensor_scan(hb[:, h, :], ones[:, :], hE[:, h, :], 0.0, ALU.mult, ALU.add).then_inc(dve_done, 1))
                dve.wait_ge(dve_done, e.last())
                dve.wait_ge(pool_done, e.at("pool", "h_init"))

                def take_level(n, L):
                    if L == P:
                        dve.wait_ge(pe_done, e.at("pe", ("group", ("hl", L))))
                        b = banks[e.bank(("hl", L))]
                        e.evacuated(("hl", L), dve.tensor_copy(hA[:, :, 2, :], b[:, :].rearrange("p (h t) -> p h t", h=HH)).then_inc(bank_evac[e.bank(("hl", L))], 1))
                        return
                    for half in range(2):
                        b = banks[e.bank(("hl", L, half))]
                        for i in range(2):
                            ins = dve.copy_predicated(
                                hA[:, 2 * half + i, 0:2, :], bc(level_mask[:, n, :], 1, [2, P]),
                                b[:, T * i:T * (i + 1)].rearrange("p (b c) -> p b c", b=2))
                            if i:
                                e.evacuated(("hl", L, half), ins.then_inc(bank_evac[e.bank(("hl", L, half))], 1))

                for s_, v_ in e.evacuations(("hq", 0), ("hq", 1)):
                    dve.wait_ge(s_, v_)
                for n, L in enumerate(LEVELS, 1):
                    ns = HH * T // (2 * L)
                    v = [t.rearrange("p h t -> p (h t)").rearrange("p (n l) -> p n l", n=ns)
                         for t in (hb, hE, hq, hk, hQ[:, n % 2], hKp[:, n % 2])]
                    ref = v[0][:, :, L - 1:L].to_broadcast([P, ns, L])
                    dve.wait_ge(pe_done, e.at("pe", ("group", ("hl", L // 2 if n > 1 else 0, 1))))
                    e.step(tt_(v[1][:, :, L:2 * L], v[0][:, :, L:2 * L], ref, ALU.subtract).then_inc(dve_done, 1))
                    e.step(tt_(v[1][:, :, 0:L], ref, v[0][:, :, 0:L], ALU.subtract).then_inc(dve_done, 1), ("sub", L))
                    take_level(n - 1, L // 2 if n > 1 else 0)
                    dve.wait_ge(act_done, e.at("act", ("hexp", L)))
                    e.step(tt_(v[4][:, :, L:2 * L], v[2][:, :, L:2 * L], v[1][:, :, L:2 * L], ALU.mult).then_inc(dve_done, 1))
                    e.step(tt_(v[5][:, :, 0:L], v[3][:, :, 0:L], v[1][:, :, 0:L], ALU.mult).then_inc(dve_done, 1), ("level", L))
                    dve.wait_ge(dve_done, e.last())
                    if n < len(BETWEEN_LEVELS) and BETWEEN_LEVELS[n][0] == "mo2":
                        i = BETWEEN_LEVELS[n][1]
                        product("mo2", i // 2, i % 2, 1)
                take_level(len(LEVELS), P)
                for tt in range(TT):
                    evac(("ho", tt), ho[:, tt, :, :].rearrange("p h d -> p (h d)"), 512)
                for s_, v_ in e.evacuations(("ho", 0), ("ho", 1)):
                    dve.wait_ge(s_, v_)
                of, sf, gf = (t.rearrange("p t h d -> p (t h d)").rearrange("p (n d) -> p n d", d=HK)
                              for t in (ho, hsq, hg))
                dve.wait_ge(pool_done, e.at("pool", ("mg", "mo2", 3)))
                e.step(tt_(sf, of, of, ALU.mult).then_inc(dve_done, 1))
                dve.wait_ge(dve_done, e.last())
                e.step(dve.tensor_reduce(hs_a[:, 0:8], sf, AX.X, ALU.add).then_inc(dve_done, 1))
                dve.wait_ge(dve_done, e.last())
                e.step(ts_(hs_b[:, 0:8], hs_a[:, 0:8], 1.0 / HK, EPS, ALU.mult, ALU.add).then_inc(dve_done, 1), "hg_ms")
                dve.wait_ge(act_done, e.at("act", "hg_rt"))
                e.step(dve.reciprocal(hs_a[:, 0:8], hs_c[:, 0:8]).then_inc(dve_done, 1))
                dve.wait_ge(dve_done, e.last())
                e.step(tt_(of, of, bc(hs_a[:, 0:8], 2, [8, HK]), ALU.mult).then_inc(dve_done, 1))
                dve.wait_ge(dve_done, e.last())
                for s_, v_ in e.evacuations(("hg", 0), ("hg", 1)):
                    dve.wait_ge(s_, v_)
                e.step(tt_(of, of, gf, ALU.mult).then_inc(dve_done, 1), "hg_out")
                e.step(tt_(lbt[:, 0, :], lbt[:, 2, :], lbt[:, 3, :], ALU.add).then_inc(dve_done, 1))
                dve.wait_ge(dve_done, e.last())
                e.step(dve.reciprocal(lbt[:, 1, :], lbt[:, 0, :]).then_inc(dve_done, 1))
                dve.wait_ge(dve_done, e.last())
                e.step(tt_(lbt[:, 3, :], lbt[:, 3, :], lbt[:, 1, :], ALU.mult).then_inc(dve_done, 1))
                dve.wait_ge(dve_done, e.last())
                e.step(tt_(low[:, :], low[:, :], lbt[:, 3, :], ALU.add).then_inc(dve_done, 1))
                for u in range(2):
                    for j in range(2):
                        product("ho2", u, j, 2)
                for j in range(4):
                    add_x("wout", j)
                for s_, v_ in e.evacuations(*[("wout", j) for j in range(4)]):
                    dve.wait_ge(s_, v_)
                norm_dve("n3", x)
                norm_evac_dve("n3", V2["cross"])

                def x_scores(h):
                    k = h % 3
                    dve.wait_ge(pe_done, e.at("pe", ("group", ("xs", h))))
                    b = banks[e.bank(("xs", h))]
                    if h >= 3:
                        for s_, v_ in e.evacuations(("xs", h - 3)):
                            dve.wait_ge(s_, v_)
                    e.evacuated(("xs", h), dve.tensor_reduce(a_rec[:, k, 2:4], b[:, :].rearrange("p (t n) -> p t n", t=TT),
                                                        AX.X, ALU.max).then_inc(bank_evac[e.bank(("xs", h))], 1))
                    dve.wait_ge(bank_evac[e.bank(("xs", h))], e.evac_value(("xs", h)) - 1)
                    e.step(ts_(a_max[:, k, 0:2], a_rec[:, k, 2:4], -(XK ** -0.5), None, ALU.mult).then_inc(dve_done, 1), ("xa", "max", h))

                def x_sums(h):
                    for s_, v_ in e.evacuations(("xs", h)):
                        dve.wait_ge(s_, v_)
                    e.step(dve.reciprocal(a_rec[:, h % 3, 0:2], a_sum[:, h % 3, 0:2]).then_inc(dve_done, 1), ("xa", "rec", h))

                attention_dve("xa", XH, x_scores, x_sums, lambda h: evac(("xo", h), xoT[:, h, :], T))
                for u in range(2):
                    for tt in range(TT):
                        xs = x[:, tt, 512 * u:512 * (u + 1)]
                        dve.wait_ge(pe_done, e.at("pe", ("group", ("xw", u, tt))))
                        b = banks[e.bank(("xw", u, tt))]
                        e.evacuated(("xw", u, tt), tt_(xs, xs, b[:, :], ALU.add).then_inc(bank_evac[e.bank(("xw", u, tt))], 1))
                for s_, v_ in e.evacuations(*[("xw", u, tt) for u in range(2) for tt in range(TT)]):
                    dve.wait_ge(s_, v_)
                norm_dve("n4", x)
                norm_evac_dve("n4", V2["ffn"])
                for i in range(FF // 256):
                    for s_, v_ in e.evacuations(("fg", i)):
                        dve.wait_ge(s_, v_)
                    dve.wait_ge(pe_done, e.at("pe", ("group", ("fu", i))))
                    b = banks[e.bank(("fu", i))]
                    e.evacuated(("fu", i), tt_(gu[:, 2 * i:2 * i + 2, :].rearrange("p a b -> p (a b)"), b[:, :],
                                          f_tmp[:, i % 4, :], ALU.mult).then_inc(bank_evac[e.bank(("fu", i))], 1))
                for tt in range(TT):
                    for c in range(2):
                        xs = x[:, tt, 512 * c:512 * (c + 1)]
                        dve.wait_ge(pe_done, e.at("pe", ("group", ("fd", tt, c))))
                        b = banks[e.bank(("fd", tt, c))]
                        e.evacuated(("fd", tt, c), tt_(xs, xs, b[:, :], ALU.add).then_inc(bank_evac[e.bank(("fd", tt, c))], 1))
                for s_, v_ in e.evacuations(*[("fd", tt, c) for tt in range(TT) for c in range(2)]):
                    dve.wait_ge(s_, v_)

            def product(key, u, j, branch):
                m, k = 4 * u + 2 * j, j % 2
                dve.wait_ge(pe_done, e.at("pe", ("group", (key, u, j))))
                b = banks[e.bank((key, u, j))]
                if u == 0 and branch == 1:
                    if j == 0:
                        dve.wait_ge(pool_done, e.at("pool", "h_init"))
                else:
                    dve.wait_ge(pool_done, e.at("pool", ("mg", key, 2 * u + j - 2) if u else ("mg", "mo2", 2 + j)))
                e.evacuated((key, u, j), tt_(m_tmp2[:, k, :], b[:, :], gates[:, 8 * branch + m:8 * branch + m + 2, :]
                                        .rearrange("p a b -> p (a b)"), ALU.mult).then_inc(bank_evac[e.bank((key, u, j))], 1))

            in_layers(e, dve, layer)
            norm_dve("nf", x)
            dve.wait_ge(dve_done, e.last())
            dve.wait_ge(out_stored, 16)
            for tt in range(TT):
                e.step(tt_(xn[:, tt, :], xn[:, tt, :], nfin, ALU.mult).then_inc(dve_done, 1), "final")

        @block.gpsimd
        def _(pool):
            e = Hand(prog, "pool", bank_evac)

            def select(out, pattern, base, cm, fill, op=ALU.is_ge):
                e.step(pool.affine_select(out=out, in_=out, compare_op=op, fill=fill, base=base,
                                             pattern=pattern, channel_multiplier=cm).then_inc(pool_done, 1))
                pool.wait_ge(pool_done, e.last())

            e.step(pool.memset(rows[:, :], 0.0).then_inc(pool_done, 1), "rows_clear")
            pool.wait_ge(pool_done, e.last())
            e.step(pool.iota(pos_i[:, 0:2], [[P, TT]], base=0, channel_multiplier=1).then_inc(pool_done, 1))
            e.step(pool.iota(pos_i[:, 2:3], [[0, 1]], base=CL - 1, channel_multiplier=CS).then_inc(pool_done, 1))
            e.step(pool.iota(chm_i[:, 0:1], [[0, 1]], base=0, channel_multiplier=1).then_inc(pool_done, 1))
            for n, half in ((0, HD // 2), (32, ROPE // 2)):
                f = np.float32(10000.0) ** (-np.arange(half, dtype=np.float32) / np.float32(half))
                for i in range(half):
                    e.step(pool.memset(freqs[:, n + i:n + i + 1], float(f[i])).then_inc(pool_done, 1))
            e.step(pool.memset(ones[:, :], 1.0).then_inc(pool_done, 1))
            e.step(pool.memset(causal3[:, :, :], 0.0).then_inc(pool_done, 1))
            e.step(pool.memset(cmp_neg, 0.0).then_inc(pool_done, 1))
            e.step(pool.memset(cmp_on, 1.0).then_inc(pool_done, 1))
            e.step(pool.memset(kcT, 0.0).then_inc(pool_done, 1))
            e.step(pool.memset(vcf, 0.0).then_inc(pool_done, 1))
            e.step(pool.memset(ident[:, :], 0.0).then_inc(pool_done, 1))
            pool.wait_ge(pool_done, e.last())
            select(ident[:, :], [[-1, P]], 0, 1, 1.0, ALU.not_equal)
            for i in (0, 2):
                select(causal3[:, i, :], [[-1, P]], 0, 1, NEG)
            for m, fill in ((cmp_neg, NEG), (cmp_on, 0.0)):
                select(m, [[P, TT], [-CS, NCP]], -(CL - 1), 1, fill)
                e.step(pool.memset(m[:, :, NCMP:], fill).then_inc(pool_done, 1))
                pool.wait_ge(pool_done, e.last())
            e.step(pool.memset(level_mask[:, :, :], 0).then_inc(pool_done, 1))
            pool.wait_ge(pool_done, e.last())
            for n, L in enumerate([0] + LEVELS[:-1]):
                if L == 0:
                    select(level_mask[:, 0, :], [[-1, P]], 0, 1, 1.0, ALU.not_equal)
                    continue
                ns = P // (2 * L)
                odd = level_mask[:, n, :].rearrange("p (n l) -> p n l", n=ns)[:, :, L:2 * L]
                e.step(pool.memset(odd, 1).then_inc(pool_done, 1))
                pool.wait_ge(pool_done, e.last())
                select(odd, [[-2 * L, ns], [0, L]], 0, 1, 0.0)
                select(odd, [[2 * L, ns], [0, L]], L - 1, -1, 0.0)
            e.line.mark("constants", False)

            def scaled(out, src, col):
                return pool.tensor_tensor(out, src, col.to_broadcast([P, src.shape[1]]), ALU.mult)

            def normalise(s, slot, c0, norm, mark):
                for tt, (a, b) in enumerate(((0, P), (P, 3 * P))):
                    e.step(scaled(s[:, a:b], s[:, a:b], norm[:, slot, c0 + tt:c0 + tt + 1]).then_inc(pool_done, 1), mark)

            for h in range(H):
                pool.wait_ge(dve_done, e.at("dve", ("ma", "rec", h)))
                normalise(sc[:, h % 3, 0:384], h % 3, 0, a_rec, ("ma", "norm", h))
            for s in range(2):
                for s_, v_ in e.evacuations(("nk", s)):
                    pool.wait_ge(s_, v_)
                e.step(pool.tensor_copy(dup[:, s], bc(kvr[:, s], 2, [TT * KV, 2, HD])).then_inc(pool_done, 1), ("dup", s))
            for a, n in enumerate(("ks", "kw")):
                pool.wait_ge(dve_done, e.at("dve", ("roped", n)))
                pool.wait_ge(pe_done, e.at("pe", ("group", ("cx", a, 1))))
                e.step(pool.tensor_copy(dup[:, a], bc(kvr[:, 2 + 2 * a], 2, [TT * KV, 2, HD])).then_inc(pool_done, 1), ("dup", 2 + a))
            for h in range(H):
                k = h % 3
                pool.wait_ge(dve_done, e.at("dve", ("na", "rec", h)))
                c = sc[:, k, 768:800].rearrange("p (t n) -> p t n", t=TT)
                e.step(pool.tensor_tensor(c, c, cmp_on, ALU.mult).then_inc(pool_done, 1))
                pool.wait_ge(pool_done, e.last())
                for tt in range(TT):
                    ct = sc[:, k, 768 + NCP * tt:768 + NCP * (tt + 1)]
                    e.step(pool.tensor_scalar(ct, ct, a_nrm[:, k, tt:tt + 1], None, ALU.mult).then_inc(pool_done, 1))
                for a in range(2):
                    normalise(sc[:, k, 384 * a:384 * (a + 1)], k, 2 + 2 * a, a_nrm, ("na", "norm", h))
            pool.wait_ge(dve_done, e.at("dve", ("x", 1)))

            def layer(l):
                e.l = l
                pool.wait_ge(dve_done, e.at("dve", "s_cos"))
                e.step(pool.tensor_tensor(e_re[:, :, 0:1], ones[:, 0:SB].unsqueeze(2), ones[:, 0:SB].unsqueeze(2), ALU.mult).then_inc(pool_done, 1))
                e.step(pool.tensor_tensor(e_im[:, :, 0:1], causal3[:, 1, 0:SB].unsqueeze(2),
                                         causal3[:, 1, 0:SB].unsqueeze(2), ALU.add).then_inc(pool_done, 1))
                e.step(pool.tensor_copy(e_re[:, :, 1:2], s5v[:, 8, :].unsqueeze(2)).then_inc(pool_done, 1))
                e.step(pool.tensor_copy(e_im[:, :, 1:2], s5v[:, 6, :].unsqueeze(2)).then_inc(pool_done, 1))
                pool.wait_ge(pool_done, e.last())
                n = 1
                while n < T:
                    cn, sn_ = (t[:, :, n:n + 1].to_broadcast([P, SB, n]) for t in (e_re, e_im))
                    c1, s1 = e_re[:, :, 1:n + 1], e_im[:, :, 1:n + 1]
                    c2, s2 = e_re[:, :, n + 1:2 * n + 1], e_im[:, :, n + 1:2 * n + 1]
                    tm = e_tmp[:, :, 0:n]
                    e.step(pool.tensor_tensor(c2, c1, cn, ALU.mult).then_inc(pool_done, 1))
                    e.step(pool.tensor_tensor(s2, s1, cn, ALU.mult).then_inc(pool_done, 1))
                    e.step(pool.tensor_tensor(tm, s1, sn_, ALU.mult).then_inc(pool_done, 1))
                    pool.wait_ge(pool_done, e.last())
                    e.step(pool.tensor_tensor(c2, c2, tm, ALU.subtract).then_inc(pool_done, 1))
                    pool.wait_ge(pool_done, e.last())
                    e.step(pool.tensor_tensor(tm, c1, sn_, ALU.mult).then_inc(pool_done, 1))
                    pool.wait_ge(pool_done, e.last())
                    e.step(pool.tensor_tensor(s2, s2, tm, ALU.add).then_inc(pool_done, 1), "tables")
                    pool.wait_ge(pool_done, e.last())
                    n *= 2
                for blk in range(SB):
                    k = blk % 2
                    c, s = e_re[:, blk, 0:T], e_im[:, blk, 0:T]
                    pool.wait_ge(dve_done, e.at("dve", ("z", blk)))
                    zr, zi = z_st[:, k, 0, :], z_st[:, k, 1, :]
                    for i, (u, v) in enumerate(((zr, c), (zi, s), (zi, c), (zr, s))):
                        ins = pool.tensor_tensor(x_tm[:, i, :], u, v, ALU.mult)
                        e.step(ins.then_inc(pool_done, 1))
                    pool.wait_ge(pool_done, e.last())
                    if blk >= 2:
                        pool.wait_ge(pe_done, e.at("pe", ("s5_out", blk - 2)))
                    e.step(pool.tensor_tensor(x_st[:, k, 0, :], x_tm[:, 0, :], x_tm[:, 1, :], ALU.subtract).then_inc(pool_done, 1))
                    e.step(pool.tensor_tensor(x_st[:, k, 1, :], x_tm[:, 2, :], x_tm[:, 3, :], ALU.add).then_inc(pool_done, 1), ("state", blk))
                    pool.wait_ge(pool_done, e.last())
                for u in range(2):
                    for j in range(2):
                        m = 4 * u + 2 * j
                        for s_, v_ in e.evacuations(("gl", u, j)):
                            pool.wait_ge(s_, v_)
                        e.step(pool.tensor_tensor(sgl[:, m:m + 2, :], sgl[:, m:m + 2, :], gates[:, m:m + 2, :], ALU.mult).then_inc(pool_done, 1), ("sg", u, j))
                for h in range(MH):
                    pool.wait_ge(dve_done, e.at("dve", ("la", "rec", h)))
                    normalise(m_sc[:, h % 3, 0:384], h % 3, 0, a_rec, ("la", "norm", h))
                pool.wait_ge(pe_done, e.at("pe", ("group", ("lo", 3))))
                for buf, n in ((hQ, 2 * HH * T), (hKp, 2 * HH * T), (hA, HH * 3 * P)):
                    flat_buf = buf.rearrange("p a b c -> p (a b c)")
                    zeros = causal3[:, 1, 0:1].to_broadcast([P, n])
                    e.step(pool.tensor_tensor(flat_buf, zeros, zeros, ALU.add).then_inc(pool_done, 1), "h_init")

                def add_merged(key):
                    for u in range(2):
                        for j in range(2):
                            m = 4 * u + 2 * j
                            for s_, v_ in e.evacuations((key, u, j)):
                                pool.wait_ge(s_, v_)
                            mv = merged[:, m:m + 2, :].rearrange("p a b -> p (a b)")
                            e.step(pool.tensor_tensor(mv, mv, m_tmp2[:, j % 2, :], ALU.add).then_inc(pool_done, 1), ("mg", key, 2 * u + j))
                            pool.wait_ge(pool_done, e.last())

                for u in range(2, 4):
                    for s_, v_ in e.evacuations(("gl", u, 0), ("gl", u, 1)):
                        pool.wait_ge(s_, v_)
                add_merged("mo2")
                pool.wait_ge(dve_done, e.at("dve", "hg_out"))
                for k in range(KD):
                    e.step(scaled(memT[:, k, :], memn[:, k, :], vt[:, V2["mem"] + k:V2["mem"] + k + 1]).then_inc(pool_done, 1), "memT")
                add_merged("ho2")
                for h in range(XH):
                    k = h % 3
                    pool.wait_ge(dve_done, e.at("dve", ("xa", "rec", h)))
                    for tt in range(TT):
                        s = x_sc[:, k, T * tt:T * (tt + 1)]
                        e.step(scaled(s, s, a_rec[:, k, tt:tt + 1]).then_inc(pool_done, 1), ("xa", "norm", h))

            in_layers(e, pool, layer)

        @block.sync
        def _(sp):
            e = Hand(prog, "sp", bank_evac)

            def start(dst, src, **how):
                sp.dma_start(dst, src, **how).then_inc(start_ready, 16)
                loads.append(1)

            def param(dst, src):
                sp.dma_start(dst, src).then_inc(params_ready, 16)
                loads.append(1)

            def row_view(v):
                return v.rearrange("(r c) -> r c", c=P)

            def load_unit(plan, n, before):
                if plan[n] is None:
                    return
                if before is not None:
                    sp.wait_ge(pe_done, e.at("pe", before))
                _, (nk, nc_), src = plan[n]
                s = n % RING
                sp.dma_start(ring[:, s, 0:nk * nc_].rearrange("p (k n) -> p k n", k=nk), src).then_inc(unit_ready[s], 16)

            loads = []
            start(x[:, :, :], A["x"][0].rearrange("(t p) d -> p t d", p=P))
            start(mem_in, A["mem_2"][0].rearrange("(t p) d -> p t d", p=P))
            sp.wait_ge(pool_done, e.at("pool", "rows_clear"))
            start(rows[0:16, :], A["norm_gain"].rearrange("l (r c) -> (l r) c", c=P))
            start(rows[16:32, :], A["ple_gate_gain"].rearrange("l (r c) -> (l r) c", c=P))
            start(rows[32:64, :], A["nsa_cmp_pe"][0].rearrange("s (j i) d -> (s j) (i d)", i=2))
            for i, (name, n) in enumerate((("moba_q_gain", 1), ("moba_k_gain", 1), ("nsa_q_gain", 1), ("nsa_k_gain", 3))):
                src = A[name].rearrange("a d -> a d") if n == 1 else A[name].rearrange("a b d -> a (b d)")
                start(gains[:, i:i + n, :].rearrange("p a b -> p (a b)"), src.to_broadcast([P, n * HD]))
            start(pos_i[:, 3:5], A["positions_2"][0].rearrange("(t p) -> p t", p=P),
                  allow_slow_non_contiguous=True)
            start(w2s, A["nsa_cmp_w2"][0].rearrange("s (k p) d -> p s k d", p=P))
            for i in range(2):
                start(p_in[:, i], A["p"][i, 0].rearrange("(t p) d -> p t d", p=P))
            assert len(loads) == START_LOADS
            for n in range(len(plan1)):
                load_unit(plan1, n, ("unit", True, n - RING) if n >= RING else None)
            last1 = plan1

            def params(l):
                loads.clear()
                for c, n, v in ((V2["mix"], 8, "norm_mix_2"), (V2["cross"], 8, "norm_cross_2"), (V2["mem"], 8, "norm_mem_2"),
                                (V2["ffn"], 8, "norm_ffn_2"), (V2["q"], 4, "mla_q_norm_2"), (V2["kv"], 2, "mla_kv_norm_2"),
                                (V2["hgn"], 1, "hg_g_norm_2")):
                    param(rows[c:c + n, :], row_view(A[v][l]))
                for i in range(DEPTH):
                    param(rows[V2["lb0"] + 4 * i:V2["lb0"] + 4 * i + 4, :], row_view(A["hg_lb_2"][i]))
                param(rows[V2["skip"]:V2["skip"] + 4, :], A["ssm_d_2"][l].rearrange("(q g) c -> q (g c)", q=4))
                for c, v in ((V2["lam_re"], "ssm_lam_re_2"), (V2["lam_im"], "ssm_lam_im_2")):
                    param(rows[c:c + SB, :], A[v][l].rearrange("(b g) n -> b (g n)", g=2))
                param(lsr[96:112, :], A["ssm_log_step_2"][l].rearrange("(b g) -> b g", g=2))
                for i, v in enumerate(("ssm_b_re_2", "ssm_b_im_2")):
                    param(b_raw[:, i], A[v][l].rearrange("(b g) n c -> (g n) b c", g=2))
                for i, v in enumerate(("ssm_c_re_2", "ssm_c_im_2")):
                    param(c_raw[:, i], A[v][l].rearrange("(q g) c n -> (g c) q n", q=4))
                assert len(loads) == PARAM_LOADS

            sp.wait_ge(dve_done, e.at("dve", ("x", 1)))
            params(0)
            n_layer = len(plan2[0])
            late = n_layer - 4
            prev = lambda n: ("unit", True, len(plan1) + n - RING)
            for l in range(DEPTH):
                for n in range(n_layer):
                    if n >= RING:
                        e.l = l
                        load_unit(plan2[l], n, ("unit", False, n - RING))
                    elif l == 0:
                        load_unit(plan2[l], n, used(prev(n), plan1))
                    else:
                        e.l = l - 1
                        load_unit(plan2[l], n, used(("unit", False, n_layer + n - RING), plan2[0]))
                    if n == late and l + 1 < DEPTH:
                        e.l = l
                        for s_, v_ in e.evacuations(("fu", FF // 256 - 1)):
                            sp.wait_ge(s_, v_)
                        params(l + 1)
            e.l = DEPTH - 1
            sp.wait_ge(pe_done, e.at("pe", ("group", ("fu", FF // 256 - 1))))
            sp.dma_start(nfin, A["norm_final_2"].rearrange("(a d) -> a d", a=1).to_broadcast([P, D])).then_inc(out_stored, 16)
            sp.wait_ge(dve_done, e.at("dve", "final"))
            sp.dma_start(out.rearrange("a (t p) d -> p (a t) d", p=P), xn[:, :, :]).then_inc(out_stored, 16)
            sp.wait_ge(out_stored, 32)

        if looped and known:
            for key, want in prog.evacs.items():
                if isinstance(key, tuple) and key[0] == "want":
                    assert prog.evacs.get(key[1], 0) == want, (key, prog.evacs.get(key[1]))

    return {"lines": {n: {"marks": v.marks, "layer": v.layer_now} for n, v in prog.lines.items()},
            "bank_layer": prog.bank_now, "groups": prog.groups}


_INS = ["x", "p", "norm_gain", "moba_w_in", "moba_q_gain", "moba_k_gain", "moba_w_out", "nsa_w_in", "nsa_q_gain",
        "nsa_k_gain", "nsa_cmp_pe", "nsa_cmp_w1", "nsa_cmp_w2", "nsa_w_out", "ple_w_proj", "ple_gate_gain",
        "ple_w_gate", "mem_2", "positions_2", "norm_mix_2", "w_in_2", "ssm_lam_re_2", "ssm_lam_im_2", "ssm_b_re_2",
        "ssm_b_im_2", "ssm_c_re_2", "ssm_c_im_2", "ssm_d_2", "ssm_log_step_2", "ssm_w_glu_2", "mla_q_norm_2",
        "mla_kv_norm_2", "mla_w_uq_2", "mla_w_ukv_2", "mla_w_o_2", "hg_lb_2", "hg_g_norm_2", "hg_w_o_2", "w_out_2",
        "norm_cross_2", "norm_mem_2", "x_w_q_2", "x_w_kv_2", "x_w_o_2", "norm_ffn_2", "ffn_w_gate_up_2",
        "ffn_w_down_2", "norm_final_2"]
LOOPED = True


def kernel(**inputs):
    import concourse.bacc as _bacc
    from concourse.bass_utils import run_bass_kernel_spmd as _run

    arrays = {f"in_{name}_dram": np.ascontiguousarray(inputs[name]) for name in _INS}
    known = None
    for _ in range(2):
        nc = _bacc.Bacc("TRN2", target_bir_lowering=False, num_devices=1)
        A = {}
        for name in _INS:
            a = arrays[f"in_{name}_dram"]
            A[name] = nc.dram_tensor(f"in_{name}_dram", a.shape, mybir.dt.from_np(a.dtype), kind="ExternalInput").ap()
        out = nc.dram_tensor("out_0_dram", (1, T, D), F32, kind="ExternalOutput").ap()
        known = build(nc, A, out, known, LOOPED)
    r = _run(nc, [arrays], core_ids=[0])
    return r.results[0]["out_0_dram"]
```

```python
from contextlib import ExitStack

import numpy as np
import concourse.bass as bass
from concourse import mybir
from concourse.alu_op_type import AluOpType as ALU

F32 = mybir.dt.float32
F32R = mybir.dt.float32r
I32 = mybir.dt.int32
I8 = mybir.dt.int8
ACT = mybir.ActivationFunctionType
AX = mybir.AxisListType

P = 128
D = 1024
T = 256
TT = T // P
KD = D // P
DEPTH = 2
EPS = 1e-6
NEG = -1e30
RING = 6
UNIT = 2048
BANKS = 8
PI = 3.1415925
ROUND = 12582912.0
TWO_PI = (6.28125, 0.0019340515136718750, 1.2556659146435e-06)

H, HD = 16, 64
KV = 4
NCMP = 15
NCP = 16
CL, CS = 32, 16

SG, SC, SN = 32, 16, 64
SB = SG * SN // P
QR, KR, NOPE, ROPE, MV, MH = 512, 256, 64, 32, 64, 8
QK = NOPE + ROPE
HH, HK = 4, 128
XH, XK = 4, 128
FF = 2816
SHARED_DOUBLINGS = [32, 64, 128]
LEVELS = [1, 2, 4, 8, 16, 32, 64, 128]

V1 = dict(norm0=0, norm1=8, ple0=16, ple1=24, pe=32)
V2 = dict(mix=0, cross=8, mem=16, ffn=24, q=32, kv=36, lb0=38, lb1=42, hgn=46, skip=47,
          lam_re=51, lam_im=67, step=96)


class Line:

    def __init__(self, known):
        self.known = known
        self.count, self.base, self.marks = 0, None, {}
        self.layer = known["layer"] if known else 0

    def mark(self, name, in_layer):
        self.marks[name] = (self.count, in_layer)

    def at(self, name, l):
        if not self.known:
            return 1
        value, in_layer = self.known["marks"][name]
        return value + l * self.layer if in_layer else value


class Program:

    def __init__(self, known):
        self.known = known
        self.lines, self.groups, self.evacs = {}, {}, {}
        self.in_layer = False
        self.bank_layer = known["bank_layer"] if known else [0] * BANKS


class Hand:

    def __init__(self, prog, name, bank_evac):
        self.p, self.line, self.bank_evac = prog, prog.lines[name], bank_evac
        self.l = 0

    def step(self, ins, mark=None):
        self.line.count += 1
        if mark is not None:
            self.line.mark(mark, self.p.in_layer)

    def last(self):
        return self.line.count + self.l * self.line.layer if self.p.in_layer else self.line.count

    def at(self, who, mark):
        return self.p.lines[who].at(mark, self.l)

    def bank(self, key):
        return self.p.groups[key][0]

    def evac_value(self, key):
        bank, value, in_layer = self.p.groups[key]
        return value + self.l * self.p.bank_layer[bank] if in_layer else value

    def evacuations(self, *keys):
        last = {}
        for key in keys:
            bank, value, _ = self.p.groups[key]
            if bank not in last or value > self.p.groups[last[bank]][1]:
                last[bank] = key
        return [(self.bank_evac[bank], self.evac_value(key)) for bank, key in last.items()]

    def evacuated(self, key, ins):
        self.p.evacs[key] = self.p.evacs.get(key, 0) + 1


def kview(w, k0, nk, c0, nc):
    return w[k0 * P:(k0 + nk) * P, c0:c0 + nc].rearrange("(k p) n -> p k n", p=P)


def weight_plan_first(A):
    out = []

    def cols(name, w, c0, n):
        for c in range(0, n, 256):
            out.append((name, (8, 256), kview(w, 0, 8, c0 + c, 256)))

    def ple(i):
        out.append(("proj", (2, 1024), kview(A["ple_w_proj"][i], 0, 2, 0, 1024)))
        cols("gate", A["ple_w_gate"][i], 0, 1024)

    w = A["moba_w_in"][0]
    for name, c0 in (("q", 0), ("k", D), ("v", 2 * D), ("z", 3 * D)):
        cols(name, w, c0, D)
    cols("out", A["moba_w_out"][0], 0, D)
    ple(0)
    w = A["nsa_w_in"][0]
    cols("q", w, 0, D)
    cols("kv", w, D, 6 * 256)
    out.append(("gl", (8, 48), kview(w, 0, 8, D + 6 * 256, 48)))
    cols("z", w, D + 6 * 256 + 48, D)
    for s in range(2):
        for c in range(2):
            out.append(("cmp", (8, 256), kview(A["nsa_cmp_w1"][0, s], 8 * c, 8, 0, 256)))
    cols("out", A["nsa_w_out"][0], 0, D)
    ple(1)
    while len(out) % RING:
        out.append(None)
    return out


def weight_plan_layer(A, l):
    out = []

    def cols(name, w, c0, n):
        for c in range(0, n, 256):
            out.append((name, (8, 256), kview(w, 0, 8, c0 + c, 256)))

    w = A["w_in_2"][l]
    cols("u", w, 0, 512)
    cols("gates", w, 3360, 3 * D - 256)
    cols("ql", w, 512, 512)
    cols("kvl", w, 1024, 256)
    out.append(("kr", (8, 32), kview(w, 0, 8, 1280, 32)))
    cols("gates", w, 3360 + 3 * D - 256, 256)
    glu = [("glu", (4, 512), kview(A["ssm_w_glu_2"][l], 0, 4, 512 * c, 512)) for c in (2, 3, 0, 1)]
    out += glu[:3]
    for c in range(2):
        out.append(("uq", (4, 384), kview(A["mla_w_uq_2"][l], 0, 4, 384 * c, 384)))
    out.append(("ukv", (2, 1024), kview(A["mla_w_ukv_2"][l], 0, 2, 0, 1024)))
    out.append(glu[3])
    cols("hq", w, 1312, 512)
    cols("hf", w, 1824, 512)
    cols("hi", w, 2336, 512)
    cols("hg", w, 2848, 512)
    for c in range(2):
        out.append(("mo", (4, 512), kview(A["mla_w_o_2"][l], 0, 4, 512 * c, 512)))
    cols("xk", A["x_w_kv_2"][l], 0, 512)
    for c in range(2):
        out.append(("ho", (4, 512), kview(A["hg_w_o_2"][l], 0, 4, 512 * c, 512)))
    cols("xv", A["x_w_kv_2"][l], 512, 512)
    cols("wout", A["w_out_2"][l], 0, D)
    cols("xq", A["x_w_q_2"][l], 0, 512)
    for c in range(2):
        out.append(("xo", (4, 512), kview(A["x_w_o_2"][l], 0, 4, 512 * c, 512)))
    for c in range(0, FF, 256):
        out.append(("fg", (8, 256), kview(A["ffn_w_gate_up_2"][l], 0, 8, c, 256)))
        out.append(("fu", (8, 256), kview(A["ffn_w_gate_up_2"][l], 0, 8, FF + c, 256)))
    for c in range(FF // P // 2):
        out.append(("fd", (2, 1024), kview(A["ffn_w_down_2"][l], 2 * c, 2, 0, 1024)))
    while len(out) % RING:
        out.append(None)
    return out


def slot_loads(plan, i):
    return sum(1 for j in range(i % RING, i + 1, RING) if plan[j] is not None)


GU_LOW = 24000
FIRST_LOADS = 4
START_LOADS = 9
GATES_EARLY = 5
LATENTS_AT = (13, 15)
BETWEEN_LEVELS = [("hi", 0), ("hi", 1), ("hg", 0), ("hg", 1), ("mo2", 0), ("mo2", 1), ("mo2", 2), ("mo2", 3)]
PARAM_LOADS = 17


def last_unit(plan):
    return max(n for n, u in enumerate(plan) if u is not None)


def used(mark, plan):
    kind, first, n = mark
    while plan[n] is None:
        n -= RING
    return kind, first, n


def build(nc, A, out, known):
    plan1 = weight_plan_first(A)
    plan2 = [weight_plan_layer(A, l) for l in range(DEPTH)]
    prog = Program(known)

    with ExitStack() as ctx:
        def sb(name, shape, dt=F32):
            return ctx.enter_context(nc.sbuf_tensor(name, shape, dt))

        def sem(name):
            return ctx.enter_context(nc.semaphore(name))

        banks = [ctx.enter_context(nc.psum_tensor(f"bank{i}", [P, 512], F32)) for i in range(BANKS)]
        bank_evac = [sem(f"bank_evac{i}") for i in range(BANKS)]
        unit_ready = [sem(f"unit_ready{i}") for i in range(RING)]
        params_ready = sem("params_ready")
        first_ready = sem("first_ready")
        start_ready = sem("start_ready")
        out_stored = sem("out_stored")
        pe_done = sem("pe_done")
        act_done = sem("act_done")
        dve_done = sem("dve_done")
        pool_done = sem("pool_done")
        for name in ("pe", "dve", "act", "pool", "sp"):
            prog.lines[name] = Line(known["lines"][name] if known else None)

        ring = sb("ring", [P, RING, UNIT])
        x = sb("x", [P, TT, D])
        xn = sb("xn", [P, TT, D])
        hT = sb("hT", [P, KD, T])
        ident = sb("ident", [P, P])
        causal3 = sb("causal3", [P, 3, P])
        level_mask = sb("level_mask", [P, 8, P], I8)
        ones = sb("ones", [P, T])
        angles = sb("angles", [P, P])
        cos_t = sb("cos_t", [P, P])
        sin_t = sb("sin_t", [P, P])
        tr_a = sb("tr_a", [P, P])
        tr_b = sb("tr_b", [P, P])
        freqs = sb("freqs", [P, 48])
        pos_i = sb("pos_i", [P, 6], I32)
        pos_f = sb("pos_f", [P, 6])
        rows = sb("rows", [P, P])
        vt = sb("vt", [P, P])
        lsr = sb("lsr", [P, 2])
        st_p = sb("st_p", [P, 2, 4])
        st_a = sb("st_a", [P, 2])
        scales = sb("scales", [P, TT, P])
        st_b = sb("st_b", [P, 2])
        st_c = sb("st_c", [P, 2])
        hs_a = sb("hs_a", [P, 64])
        hs_b = sb("hs_b", [P, 64])
        hs_c = sb("hs_c", [P, 64])
        a_max = sb("a_max", [P, 3, 6])
        a_sum = sb("a_sum", [P, 3, 6])
        a_rec = sb("a_rec", [P, 3, 6])
        a_nrm = sb("a_nrm", [P, 3, 6])
        memn = sb("memn", [P, KD, T])
        chm = sb("chm", [P, 2, 2])
        chm_i = sb("chm_i", [P, 2], I32)
        low = sb("low", [P, HH])
        lbt = sb("lbt", [P, 4, HH])
        mst = sb("mst", [P, 3, 4])
        ARENA = 30050
        arena_scope = ExitStack()
        arena = arena_scope.enter_context(nc.sbuf_tensor("arena", [P, ARENA], F32))
        top = {"at": 0}

        def take(*shape, at=None):
            n = int(np.prod(shape))
            a = top["at"] if at is None else at
            if at is None:
                top["at"] += n
            assert a + n <= ARENA, (a + n, ARENA)
            v = arena[:, a:a + n]
            if len(shape) == 2:
                v = v.rearrange("p (a b) -> p a b", a=shape[0])
            if len(shape) == 3:
                v = v.rearrange("p (a b c) -> p a b c", a=shape[0], b=shape[1])
            if len(shape) == 4:
                v = v.rearrange("p (a b c d) -> p a b c d", a=shape[0], b=shape[1], c=shape[2])
            return v

        qk = take(2, TT, H, HD)
        vf = take(TT, H, HD)
        tmp = take(4, TT * H * HD // 2)
        qT_at = top["at"]
        qT = take(KD, T)
        kT = take(KD, T)
        zs = take(KD, T)
        sc_at = top["at"]
        sc = take(3, 832)
        pT = take(3, 1024)
        gains = take(6, HD)
        gl_s = take(TT, H, 3)
        w2s = take(2, 2, HD)
        cmp_neg = take(TT, NCP)
        cmp_on = take(TT, NCP)
        kcT = take(KV, NCP)
        vcf = take(KV, HD)
        p_in = take(2, TT, 256)
        kvr_at = top["at"]
        kvr = take(6, TT * KV, HD)
        kcf = take(KV, HD)
        hid = take(2, 2, 60)
        kcd = tmp[:, 3, 512:512 + KV * 2 * HD].rearrange("p (a b c) -> p a b c", a=KV, b=2)
        dup = take(2, TT * KV, 2, HD)
        x2 = vf.rearrange("p t h d -> p (t h d)").rearrange("p (s g t) -> p s g t", s=2, g=KV)
        flat_v = [sc.rearrange("p a b -> p (a b)")[:, 960 * i:960 * (i + 1)].rearrange("p (j n) -> p j n", j=16)
                  for i in range(2)]
        mem_in = zs.rearrange("p k t -> p (k t)").rearrange("p (t d) -> p t d", t=TT)
        oT1 = qk[:, 0, :, :, :].rearrange("p t h d -> p (t h d)").rearrange("p (k t) -> p k t", k=KD)
        prj = qk[:, 1, :, :, :].rearrange("p t h d -> p t (h d)")
        g_tmp = tmp.rearrange("p a b -> p (a b)")[:, 0:4 * 512].rearrange("p (a t c) -> p a t c", a=4, t=TT)
        assert 4 * 512 <= 4 * TT * H * HD // 2

        top["at"] = 0
        gates = take(3 * KD, T)
        merged = take(KD, T)
        sgl = take(KD, T)
        sT = take(4, T)
        mT = take(4, T)
        work = top["at"]
        e_re = take(SB, T + 1)
        e_im = take(SB, T + 1)
        e_tmp = gates[:, 16:24, :].rearrange("p a b -> p (a b)").rearrange("p (a b) -> p a b", a=SB)
        e_tmp2 = sgl.rearrange("p a b -> p (a b)").rearrange("p (a b) -> p a b", a=SB)
        b_raw = take(2, SB, SC)
        low_part = sgl.rearrange("p a b -> p (a b)")
        b_tmp = [low_part[:, 256 * i:256 * (i + 1)].rearrange("p (a b) -> p a b", a=SB) for i in range(4)]
        b_diag = low_part[:, 1024:2048].rearrange("p (s a b c) -> p s a b c", s=2, a=SB, b=2)
        b_T = take(2, 4, P)
        c_raw = take(2, 4, SN)
        c_diag = merged.rearrange("p a b -> p (a b)")[:, 0:1024].rearrange("p (s a b c) -> p s a b c", s=2, a=4, b=2)
        c_T = take(2, 4, P)
        s5v = take(20, SB)
        uT = take(4, T)
        z_in = take(2, 2, T)
        z_st = take(2, 2, T)
        z_tm = take(4, T)
        x_st = take(2, 2, T)
        x_tm = mT
        y_s = take(4, T)
        top["at"] = work
        ql = take(TT, QR)
        kvl = take(TT, KR)
        krp = take(TT, ROPE)
        qlT = take(4, T)
        kvT = take(2, T)
        m_q = take(TT, MH, QK)
        m_k = take(TT, MH, QK)
        m_v = take(TT, MH, MV)
        m_tmp = take(4, TT * MH, ROPE // 2)
        m_qT = take(MH, T)
        m_kT = take(MH, T)
        m_sc = take(3, 512)
        m_pT = take(3, 512)
        mlan = take(TT, QR)
        top["at"] = work
        hq = take(HH, T)
        hb = take(HH, T)
        hk = take(HH, T)
        hE = take(HH, T)
        hQ = take(2, HH, T)
        hKp = take(2, HH, T)
        hA = take(HH, 3, P)
        hv = take(TT, HH, HK)
        hg = take(TT, HH, HK)
        ho = take(TT, HH, HK)
        hsq = take(TT, HH, HK)
        top["at"] = work
        memT = take(KD, T)
        xkT = take(XH, T)
        xv = take(TT, XH * XK)
        xqT = take(XH, T)
        x_sc = take(3, 512)
        x_pT = take(3, 512)
        xoT = take(XH, T)
        nfin = hT[:, 0:4, :].rearrange("p k t -> p (k t)")
        m_tmp2 = hsq.rearrange("p t h d -> p (t h d)").rearrange("p (a b) -> p a b", a=2)

        arena_scope.close()

        def over_arena(name, at, shape):
            with ExitStack() as scope:
                if at:
                    scope.enter_context(nc.sbuf_tensor(f"{name}_starts", [P, at], F32))
                return scope.enter_context(nc.sbuf_tensor(name, shape, F32R))

        in_high = over_arena("in_high", qT_at, [P, KD, T])
        in_low = over_arena("in_low", qT_at + KD * T, [P, KD, T])
        q_high = over_arena("q_high", sc_at, [P, 2, UNIT])
        gate_high = over_arena("gate_high", sc_at - UNIT, [P, 2, UNIT])
        first_low = over_arena("first_low", kvr_at, [P, 2, UNIT])
        first_split = [n for n, u in enumerate(plan1)
                       if u is not None and (u[0] in ("q", "gate") or n < 8)]

        def first_high(c):
            if plan1[first_split[c]][0] == "gate":
                return gate_high[:, c % 2, :]
            return q_high[:, c % 2 if c < 8 else 1 - c % 2, :]

        def first_group(c):
            return ((("mq", "mk", ("pg", 0), "nq", ("pg", 1))[c // 4]), c % 4)

        def before_first(c):
            if c in (8, 9):
                return "mw", 0
            if c in (16, 17):
                return "nw", 0
            return first_group(c - 2)

        gu_high = over_arena("gu_high", 0, [P, FF // P, T])
        w_high = over_arena("w_high", 3 * KD * T, [P, 2, UNIT])
        w_low = over_arena("w_low", 3 * KD * T + 2 * UNIT, [P, 2, UNIT])
        h_high = over_arena("h_high", 3 * KD * T + 4 * UNIT, [P, KD, T])
        h_low = over_arena("h_low", 3 * KD * T + 4 * UNIT + KD * T, [P, KD, T])
        at_f = 3 * KD * T + 4 * UNIT + 2 * KD * T
        f_tmp = arena[:, at_f:at_f + 4 * 512].rearrange("p (a b) -> p a b", a=4)
        gu_low = over_arena("gu_low", GU_LOW, [P, FF // P, T])
        assert at_f + 4 * 512 <= work + 2 * SB * (T + 1) + 64 and GU_LOW + FF // P * T <= ARENA
        ffn_first = [u is not None and u[0] == "fg" for u in plan2[0]].index(True)
        n_down = FF // 256
        ffn_units = 3 * n_down

        def unit_loaded(n, l):
            slot = n % RING
            return (16 * (slot_loads(plan1, len(plan1) - RING + slot) + slot_loads(plan2[0], n))
                    + l * 16 * slot_loads(plan2[0], len(plan2[0]) - RING + slot))

        def before_ffn(c):
            if c < 2:
                return "group", ("xq", 1)
            c -= 2
            if c < 2 * n_down:
                return "group", ("fu" if c % 2 else "fg", c // 2)
            return "down", c - 2 * n_down

        def is_split(n):
            return ffn_first <= n < ffn_first + ffn_units

        prog.lines["sp"].layer_now = 0

        def in_layers(e, eng, body, before=lambda: None):
            prog.in_layer = True
            base = e.line.count
            with eng.Fori(0, DEPTH) as l:
                before()
                body(l)
            e.line.layer_now = e.line.count - base
            e.line.count = base + DEPTH * e.line.layer_now
            prog.in_layer = False
            e.l = DEPTH - 1

        def bc(ap, axis, shape):
            return ap.unsqueeze(axis).to_broadcast([ap.shape[0], *shape])

        block = ctx.enter_context(nc.Block())

        @block.tensor
        def _(pe):
            e = Hand(prog, "pe", bank_evac)
            total = [0] * BANKS
            turn = [0]
            unit_at = {"n": 0, "plan": plan1, "base": [0] * RING, "layer": [0] * RING}
            for s in range(RING):
                unit_at["layer"][s] = slot_loads(plan2[0], len(plan2[0]) - RING + s)

            def opened(key, evacs):
                b = turn[0] % BANKS
                turn[0] += 1
                if total[b] > 0 or prog.in_layer:
                    pe.wait_ge(bank_evac[b], total[b] + e.l * prog.bank_layer[b]
                               if prog.in_layer else total[b])
                total[b] += evacs
                prog.groups[key] = (b, total[b], prog.in_layer)
                assert key not in prog.evacs
                prog.evacs[("want", key)] = evacs
                return banks[b]

            def closed(key, ins):
                e.step(ins.then_inc(pe_done, 1), ("group", key))

            def unit(name):
                plan, n = unit_at["plan"], unit_at["n"]
                unit_at["n"] += 1
                s = n % RING
                got, (nk, ncol), _ = plan[n]
                assert got == name, (got, name, n)
                value = 16 * (unit_at["base"][s] + slot_loads(plan, n))
                pe.wait_ge(unit_ready[s], value + e.l * 16 * unit_at["layer"][s]
                           if prog.in_layer else value)
                return ring[:, s, 0:nk * ncol].rearrange("p (k n) -> p k n", k=nk)

            def unit_used():
                e.line.mark(("unit", unit_at["plan"] is plan1, unit_at["n"] - 1), prog.in_layer)

            def unit_skip():
                while unit_at["n"] % RING:
                    assert unit_at["plan"][unit_at["n"]] is None
                    unit_at["n"] += 1

            def feature_major(key, w, src, nk, m0, nm, evacs=1):
                b = opened(key, evacs)
                for m in range(nm):
                    for k in range(nk):
                        ins = pe.matmul(b[:, m * T:(m + 1) * T], w[:, k, (m0 + m) * P:(m0 + m + 1) * P],
                                        src[:, k, :], start=(k == 0), stop=(k == nk - 1))
                closed(key, ins)

            def token_major(key, w, src, nk, c0, n, tts, evacs=1):
                b = opened(key, evacs)
                for i, tt in enumerate(tts):
                    for k in range(nk):
                        ins = pe.matmul(b[:, i * n:(i + 1) * n], src[:, k, tt * P:(tt + 1) * P],
                                        w[:, k, c0:c0 + n], start=(k == 0), stop=(k == nk - 1))
                closed(key, ins)

            def transposes(key, pieces, evacs=1):
                b = opened(key, evacs)
                for c, src in pieces:
                    m, n = src.shape[0], src.shape[1]
                    ins = pe.transpose(b[0:n, c:c + m], src, ident[0:m, 0:m])
                closed(key, ins)

            def norm_pe(n, src=x, evacs=2):
                pe.wait_ge(dve_done, e.at("dve", ("scales", n)))
                for j in range(KD // 2):
                    b = opened(("nT", n, j), evacs)
                    for i in range(2):
                        for tt in range(TT):
                            c = 2 * j + i
                            ins = pe.matmul(b[:, T * i + P * tt:T * i + P * (tt + 1)], src[:, tt, c * P:(c + 1) * P],
                                            scales[:, tt, :], start=True, stop=True)
                    closed(("nT", n, j), ins)

            def norm_ready(n):
                for s_, v_ in e.evacuations(*[("nT", n, j) for j in range(KD // 2)]):
                    pe.wait_ge(s_, v_)

            def units_fm(name, key, src, count):
                for i in range(count):
                    w = unit(name)
                    feature_major((key, i), w, src, 8, 0, 2)
                    unit_used()

            def units_tm(name, key, src, count):
                for i in range(count):
                    w = unit(name)
                    token_major((key, i), w, src, 8, 0, w.shape[2], (0, 1))
                    unit_used()

            def split_units(cs):
                for c in cs:
                    pe.wait_ge(dve_done, e.at("dve", ("first_low", c)))
                    unit_at["n"] += 1
                    wh, wl = (t.rearrange("p (k n) -> p k n", k=KD) for t in (first_high(c), first_low[:, c % 2, :]))
                    key = first_group(c)
                    b = opened(key, 1)
                    for tt in range(TT):
                        o, tok = b[:, 256 * tt:256 * (tt + 1)], slice(tt * P, (tt + 1) * P)
                        for k in range(KD):
                            pe.matmul(o, in_high[:, k, tok], wh[:, k, :], start=(k == 0), stop=False)
                            pe.matmul(o, in_high[:, k, tok], wl[:, k, :], start=False, stop=False)
                            ins = pe.matmul(o, in_low[:, k, tok], wh[:, k, :], start=False, stop=(k == KD - 1))
                    closed(key, ins)

            def attention_pe(key, nh, scores, moved, values, lag=2):
                for i in range(nh + lag + 1):
                    if i < nh:
                        scores(i)
                    if 0 <= i - lag < nh:
                        pe.wait_ge(pool_done, e.at("pool", (key, "norm", i - lag)))
                        moved(i - lag)
                    if 0 <= i - lag - 1 < nh:
                        values(i - lag - 1)

            def causal_scores(key, q, k):
                b = opened(key, 1)
                pe.matmul(b[:, 0:P], q[:, 0:P], k[:, 0:P], start=True, stop=True)
                ins = pe.matmul(b[:, P:3 * P], q[:, P:T], k[:, 0:T], start=True, stop=True)
                closed(key, ins)

            def causal_moved(key, s):
                transposes(key, [(P * j, s[:, P * j:P * (j + 1)]) for j in range(3)])

            pe.wait_ge(first_ready, 16 * FIRST_LOADS)
            pe.wait_ge(pool_done, e.at("pool", "ident"))
            transposes("vt1", [(0, rows[0:64, :])])

            norm_pe("n0", evacs=4)
            norm_ready("n0")
            split_units(range(0, 4))
            split_units(range(4, 8))
            pe.wait_ge(start_ready, 16 * START_LOADS)
            norm_pe("mem", mem_in)
            pe.wait_ge(pool_done, e.at("pool", ("hT", "n0")))
            units_tm("v", "mv", hT, 4)
            units_fm("z", "mz", hT, 4)
            for a in range(2):
                pe.wait_ge(dve_done, e.at("dve", ("roped", "m", a)))
                src = qk[:, a, :, :, :].rearrange("p t h d -> p t (h d)")
                for j in range(4):
                    transposes(("mT", a, j), [(T * i + P * tt, src[:, tt, (2 * j + i) * P:(2 * j + i + 1) * P])
                                              for i in range(2) for tt in range(TT)])
            for a in range(2):
                for s_, v_ in e.evacuations(*[("mT", a, j) for j in range(4)]):
                    pe.wait_ge(s_, v_)
            for s_, v_ in e.evacuations(*[("mv", j) for j in range(4)]):
                pe.wait_ge(s_, v_)

            def m_scores(h):
                o, j = HD * (h % 2), h // 2
                causal_scores(("ms", h), qT[o:o + HD, j, :], kT[o:o + HD, j, :])

            def m_moved(h):
                causal_moved(("mp", h), sc[:, h % 3, 0:384])

            def pair_bank(key, h):
                if h % 2 == 0:
                    opened(key, 1)
                return banks[e.bank(key)]

            def causal_values(b, o, nv, v0, v1, p, first, last):
                pe.matmul(b[o:o + nv, 0:T], v0, p[:, 0:T], start=first, stop=False)
                return pe.matmul(b[o:o + nv, P:T], v1, p[:, T:T + P], start=False, stop=last)

            def m_values(h):
                for s_, v_ in e.evacuations(("mp", h)):
                    pe.wait_ge(s_, v_)
                key = ("mo", h // 2)
                b = pair_bank(key, h)
                ins = causal_values(b, HD * (h % 2), HD, vf[:, 0, h, :], vf[:, 1, h, :], pT[:, h % 3, :], True, True)
                if h % 2:
                    closed(key, ins)
                else:
                    e.step(ins.then_inc(pe_done, 1))

            attention_pe("ma", H, m_scores, m_moved, m_values)
            for s_, v_ in e.evacuations(*[("mo", j) for j in range(KD)]):
                pe.wait_ge(s_, v_)
            units_tm("out", "mw", oT1, 4)

            def ple_pe(i):
                transposes(("pT", i), [(T * k + P * tt, p_in[:, i, tt, P * k:P * (k + 1)])
                                       for k in range(2) for tt in range(TT)])
                for s_, v_ in e.evacuations(("pT", i)):
                    pe.wait_ge(s_, v_)
                w = unit("proj")
                for c in range(2):
                    for tt in range(TT):
                        token_major(("pj", i, c, tt), w, pT_in, 2, 512 * c, 512, (tt,))
                unit_used()
                norm_pe(("pl", i), evacs=4)
                norm_ready(("pl", i))
                split_units(range(8 + 8 * i, 12 + 8 * i))

            pT_in = pT.rearrange("p a b -> p (a b)")[:, 0:2 * T].rearrange("p (k t) -> p k t", k=2)
            ple_pe(0)

            norm_pe("n1", evacs=4)
            norm_ready("n1")
            split_units(range(12, 16))
            pe.wait_ge(pool_done, e.at("pool", ("hT", "n1")))
            units_tm("kv", "nk", hT, 6)
            units_tm("gl", "ng", hT, 1)
            for i in range(2):
                feature_major(("nz", i), unit("z"), hT, 8, 0, 2)
                unit_used()
            for s in range(2):
                pe.wait_ge(pool_done, e.at("pool", ("dup", s)))
                for j in range(2):
                    transposes(("cx", s, j), [(T * i + P * tt, dup[:, s, tt * KV + 2 * j + i, :, :].rearrange("p c d -> p (c d)"))
                                              for i in range(2) for tt in range(TT)], evacs=2)
            for i in range(2, 4):
                feature_major(("nz", i), unit("z"), hT, 8, 0, 2)
                unit_used()
            for s in range(2):
                pe.wait_ge(dve_done, e.at("dve", ("flat", s)))
                b = opened(("ch", s), 1)
                ws = [unit("cmp"), unit("cmp")]
                for m in range(2):
                    for j in range(16):
                        ins = pe.matmul(b[:, m * 60:(m + 1) * 60], ws[j // 8][:, j % 8, m * P:(m + 1) * P],
                                        flat_v[s][:, j, :], start=(j == 0), stop=(j == 15))
                closed(("ch", s), ins)
                for back in (2, 1):
                    e.line.mark(("unit", True, unit_at["n"] - back), False)
            for s in range(2):
                for s_, v_ in e.evacuations(("ch", s)):
                    pe.wait_ge(s_, v_)
                b = opened(("cv", s), 1)
                for g in range(KV):
                    for k in range(2):
                        ins = pe.matmul(b[0:NCMP, g * HD:(g + 1) * HD], hid[:, s, k, g * NCMP:(g + 1) * NCMP],
                                        w2s[:, s, k, :], start=(k == 0), stop=(k == 1))
                closed(("cv", s), ins)
            for a in range(2):
                pe.wait_ge(pool_done, e.at("pool", ("dup", 2 + a)))
                for j in range(2):
                    transposes(("nkT", a, j), [(T * i + P * tt, dup[:, a, tt * KV + 2 * j + i, :, :].rearrange("p c d -> p (c d)"))
                                               for i in range(2) for tt in range(TT)])
            pe.wait_ge(dve_done, e.at("dve", "ckv"))
            transposes("ckT", [(NCP * g, kcd[0:NCMP, g, :, :].rearrange("p c d -> p (c d)")) for g in range(KV)])
            pe.wait_ge(dve_done, e.at("dve", ("roped", "n", 0)))
            src_q = qk[:, 0, :, :, :].rearrange("p t h d -> p t (h d)")
            for j in range(4):
                transposes(("nqT", j), [(T * i + P * tt, src_q[:, tt, (2 * j + i) * P:(2 * j + i + 1) * P])
                                        for i in range(2) for tt in range(TT)])
            for s_, v_ in e.evacuations("ckT", *[("nqT", j) for j in range(4)], *[("nkT", a, j) for a in range(2) for j in range(2)]):
                pe.wait_ge(s_, v_)
            for s_, v_ in e.evacuations(*[("nk", j) for j in range(6)]):
                pe.wait_ge(s_, v_)

            def n_scores(h):
                o, j, g = HD * (h % 2), h // 2, h // 4
                q = qT[o:o + HD, j, :]
                b = opened(("ns", h, 0), 1)
                for tt in range(TT):
                    ins = pe.matmul(b[:, NCP * tt:NCP * (tt + 1)], q[:, P * tt:P * (tt + 1)], kcT[o:o + HD, g, :],
                                    start=True, stop=True)
                closed(("ns", h, 0), ins)
                for a in range(2):
                    causal_scores(("ns", h, 1 + a), q, kT[o:o + HD, KV * a + g, :])

            def n_moved(h):
                s = sc[:, h % 3, :]
                transposes(("np", h, 0), [(P * tt, s[:, 768 + NCP * tt:768 + NCP * (tt + 1)]) for tt in range(TT)])
                for a in range(2):
                    causal_moved(("np", h, 1 + a), s[:, 384 * a:384 * (a + 1)])

            def n_values(h):
                g, o = h // 4, HD * (h % 2)
                for s_, v_ in e.evacuations(*[("np", h, a) for a in range(3)]):
                    pe.wait_ge(s_, v_)
                key = ("no", h // 2)
                b = pair_bank(key, h)
                p = pT[:, h % 3, :]
                pe.matmul(b[o:o + HD, 0:T], vcf[0:NCP, g, :], p[0:NCP, 768:768 + T], start=True, stop=False)
                for a in range(2):
                    v = kvr[:, 3 + 2 * a, :, :]
                    ins = causal_values(b, o, HD, v[:, g, :], v[:, KV + g, :], p[:, 384 * a:384 * (a + 1)], False, a == 1)
                if h % 2:
                    closed(key, ins)
                else:
                    e.step(ins.then_inc(pe_done, 1))

            attention_pe("na", H, n_scores, n_moved, n_values)
            for s_, v_ in e.evacuations(*[("no", j) for j in range(KD)]):
                pe.wait_ge(s_, v_)
            units_tm("out", "nw", oT1, 4)
            ple_pe(1)
            unit_skip()

            while turn[0] % BANKS:
                turn[0] += 1
            n_first = len(plan1)
            unit_at.update(plan=plan2[0], n=0, base=[slot_loads(plan1, n_first - RING + s) for s in range(RING)])
            group_base = list(total)

            def layer(l):
                e.l = l
                unit_at["n"] = 0
                pe.wait_ge(params_ready, 16 * PARAM_LOADS + l * 16 * PARAM_LOADS)
                pe.wait_ge(dve_done, e.at("dve", "log_steps"))
                transposes("vt2", [(0, rows[:, :])])
                norm_pe("n2")
                norm_ready("n2")
                units_fm("u", "u", hT, 2)

                def gate(i):
                    w = unit("gates")
                    feature_major(("ga", i), w, hT, 8, 0, 2)
                    unit_used()

                def half_gate(i, m):
                    if m == 0:
                        half["w"], half["bank"] = unit("gates"), opened(("ga", i), 1)
                    for k in range(KD):
                        ins = pe.matmul(half["bank"][:, m * T:(m + 1) * T], half["w"][:, k, m * P:(m + 1) * P],
                                        hT[:, k, :], start=(k == 0), stop=(k == KD - 1))
                    if m == 1:
                        closed(("ga", i), ins)
                        unit_used()

                half = {}
                gate(0)
                gate(1)
                pe.wait_ge(dve_done, e.at("dve", "b_diag"))
                for s in range(2):
                    transposes(("bT", s), [(P * q, b_diag[:, s, 4 * q:4 * q + 4, :, :].rearrange("p a b c -> p (a b c)"))
                                           for q in range(4)])
                pe.wait_ge(dve_done, e.at("dve", "c_diag"))
                for s in range(2):
                    transposes(("cT", s), [(P * q, c_diag[:, s, q, :, :].rearrange("p a b -> p (a b)"))
                                           for q in range(4)])
                for i in range(2, GATES_EARLY):
                    gate(i)
                for s_, v_ in e.evacuations(("u", 0), ("u", 1), ("bT", 0), ("bT", 1), ("cT", 0), ("cT", 1)):
                    pe.wait_ge(s_, v_)

                def s5_in(b):
                    q, r = b // 4, 32 * (b % 4)
                    bank = opened(("bu", b), 4)
                    for s in range(2):
                        ins = pe.matmul(bank[:, T * s:T * (s + 1)], b_T[r:r + 32, s, q, :], uT[r:r + 32, q, :],
                                        start=True, stop=True)
                    closed(("bu", b), ins)

                def s5_out(b):
                    q, r = b // 4, 32 * (b % 4)
                    key = ("y", q)
                    bank = opened(key, 1) if b % 4 == 0 else banks[e.bank(key)]
                    pe.wait_ge(pool_done, e.at("pool", ("state", b)))
                    pe.matmul(bank[r:r + 32, 0:T], c_T[:, 0, q, r:r + 32], x_st[:, b % 2, 0, :], start=True, stop=False)
                    ins = pe.matmul(bank[r:r + 32, 0:T], c_T[:, 1, q, r:r + 32], x_st[:, b % 2, 1, :],
                                    start=False, stop=True)
                    if b % 4 == 3:
                        closed(key, ins)
                    else:
                        e.step(ins.then_inc(pe_done, 1))
                    e.line.mark(("s5_out", b), True)

                for i in range(SB + 2):
                    if i < SB:
                        s5_in(i)
                    if i >= 2:
                        s5_out(i - 2)
                    if 1 <= i <= 2 * (11 - GATES_EARLY):
                        half_gate(GATES_EARLY + (i - 1) // 2, (i - 1) % 2)
                    if i in LATENTS_AT:
                        token_major(("ql", LATENTS_AT.index(i)), unit("ql"), hT, 8, 0, 256, (0, 1))
                        unit_used()

                units_tm("kvl", "kvl", hT, 1)
                units_tm("kr", "kr", hT, 1)
                gate(11)

                def glu(u):
                    w = unit("glu")
                    for j in range(2):
                        feature_major(("gl", u, j), w, sT, 4, 2 * j, 2)
                    unit_used()

                pe.wait_ge(act_done, e.at("act", "s5_gelu"))
                for u in range(3):
                    glu(u)
                pe.wait_ge(dve_done, e.at("dve", "mla_xn"))
                for j in range(2):
                    transposes(("qlT", j), [(T * i + P * tt, mlan[:, tt, (2 * j + i) * P:(2 * j + i + 1) * P])
                                            for i in range(2) for tt in range(TT)], evacs=2)
                pe.wait_ge(dve_done, e.at("dve", "mla_kn"))
                transposes("kvT", [(T * i + P * tt, kvl[:, tt, i * P:(i + 1) * P])
                                   for i in range(2) for tt in range(TT)], evacs=2)
                for s_, v_ in e.evacuations(("qlT", 0), ("qlT", 1), "kvT"):
                    pe.wait_ge(s_, v_)
                for u in range(2):
                    w = unit("uq")
                    for tt in range(TT):
                        token_major(("uq", u, tt), w, qlT, 4, 0, 384, (tt,))
                    unit_used()
                w = unit("ukv")
                for c in range(2):
                    for tt in range(TT):
                        token_major(("ukv", c, tt), w, kvT, 2, 512 * c, 512, (tt,), evacs=2)
                unit_used()
                glu(3)
                pe.wait_ge(dve_done, e.at("dve", "mq_roped"))
                for j in range(4):
                    transposes(("mqT", j), [(T * i + P * tt, m_q[:, tt, 2 * j + i, :]) for i in range(2) for tt in range(TT)])
                pe.wait_ge(dve_done, e.at("dve", "mk_roped"))
                for j in range(4):
                    transposes(("mkT", j), [(T * i + P * tt, m_k[:, tt, 2 * j + i, :]) for i in range(2) for tt in range(TT)])
                for s_, v_ in e.evacuations(*[("mqT", j) for j in range(4)], *[("mkT", j) for j in range(4)]):
                    pe.wait_ge(s_, v_)

                def l_scores(h):
                    causal_scores(("ls", h), m_qT[0:QK, h, :], m_kT[0:QK, h, :])

                def l_moved(h):
                    causal_moved(("lp", h), m_sc[:, h % 3, 0:384])

                def l_values(h):
                    for s_, v_ in e.evacuations(("lp", h)):
                        pe.wait_ge(s_, v_)
                    key = ("lo", h // 2)
                    b = pair_bank(key, h)
                    ins = causal_values(b, MV * (h % 2), MV, m_v[:, 0, h, :], m_v[:, 1, h, :], m_pT[:, h % 3, :], True, True)
                    if h % 2:
                        closed(key, ins)
                    else:
                        e.step(ins.then_inc(pe_done, 1))

                attention_pe("la", MH, l_scores, l_moved, l_values)

                units_fm("hq", "hq", hT, 2)
                units_fm("hf", "hf", hT, 2)
                for s_, v_ in e.evacuations(*[("lo", j) for j in range(4)]):
                    pe.wait_ge(s_, v_)
                held = {}

                def between_levels(n):
                    name, i = BETWEEN_LEVELS[n]
                    if name == "mo2":
                        if i % 2 == 0:
                            held["mo"] = unit("mo")
                        feature_major((name, i // 2, i % 2), held["mo"], mT, 4, 2 * (i % 2), 2)
                        if i % 2:
                            unit_used()
                    else:
                        token_major((name, i), unit(name), hT, 8, 0, 256, (0, 1))
                        unit_used()

                between_levels(0)
                pe.wait_ge(dve_done, e.at("dve", "hk"))
                for s_, v_ in e.evacuations(("hq", 0), ("hq", 1)):
                    pe.wait_ge(s_, v_)
                for n, L in enumerate([0] + LEVELS):
                    q_, k_ = (hq, hk) if L == 0 else (hQ[:, n % 2], hKp[:, n % 2])
                    if L:
                        pe.wait_ge(dve_done, e.at("dve", ("level", L)))
                    if L < P:
                        for half in range(2):
                            b = opened(("hl", L, half), 1)
                            for i in range(2):
                                h = 2 * half + i
                                for tt in range(TT):
                                    c = (2 * i + tt) * P
                                    ins = pe.matmul(b[:, c:c + P], k_[:, h, tt * P:(tt + 1) * P],
                                                    q_[:, h, tt * P:(tt + 1) * P], start=True, stop=True)
                            closed(("hl", L, half), ins)
                    else:
                        b = opened(("hl", L), 1)
                        for h in range(HH):
                            ins = pe.matmul(b[:, h * P:(h + 1) * P], k_[:, h, 0:P], q_[:, h, P:T], start=True, stop=True)
                        closed(("hl", L), ins)
                    if n + 1 < len(BETWEEN_LEVELS):
                        between_levels(n + 1)
                for s_, v_ in e.evacuations(("hl", P), ("hl", 64, 0), ("hl", 64, 1), ("hi", 0), ("hi", 1)):
                    pe.wait_ge(s_, v_)
                for tt in range(TT):
                    b = opened(("ho", tt), 1)
                    for h in range(HH):
                        o = b[:, h * P:(h + 1) * P]
                        if tt == 0:
                            ins = pe.matmul(o, hA[:, h, 0, :], hv[:, 0, h, :], start=True, stop=True)
                        else:
                            pe.matmul(o, hA[:, h, 2, :], hv[:, 0, h, :], start=True, stop=False)
                            ins = pe.matmul(o, hA[:, h, 1, :], hv[:, 1, h, :], start=False, stop=True)
                    closed(("ho", tt), ins)
                pe.wait_ge(pool_done, e.at("pool", "memT"))
                units_fm("xk", "xk", memT, 2)
                pe.wait_ge(dve_done, e.at("dve", "hg_out"))
                for j in range(2):
                    transposes(("hoT", j), [(T * i + P * tt, ho[:, tt, 2 * j + i, :]) for i in range(2) for tt in range(TT)])
                for s_, v_ in e.evacuations(("hoT", 0), ("hoT", 1)):
                    pe.wait_ge(s_, v_)
                for u in range(2):
                    w = unit("ho")
                    for j in range(2):
                        feature_major(("ho2", u, j), w, sT, 4, 2 * j, 2)
                    unit_used()

                units_tm("xv", "xv", memT, 2)
                pe.wait_ge(pool_done, e.at("pool", ("mg", "ho2", 3)))
                units_tm("wout", "wout", merged, 4)
                norm_pe("n3")
                norm_ready("n3")
                units_fm("xq", "xq", hT, 2)
                for s_, v_ in e.evacuations(("xq", 0), ("xq", 1), ("xk", 0), ("xk", 1), ("xv", 0), ("xv", 1)):
                    pe.wait_ge(s_, v_)

                def x_scores(h):
                    b = opened(("xs", h), 2)
                    for tt in range(TT):
                        ins = pe.matmul(b[:, T * tt:T * (tt + 1)], xqT[:, h, P * tt:P * (tt + 1)], xkT[:, h, :],
                                        start=True, stop=True)
                    closed(("xs", h), ins)

                def x_moved(h):
                    s = x_sc[:, h % 3, :].rearrange("p (t k) -> p t k", t=TT)
                    transposes(("xp", h), [(T * k + P * tt, s[:, tt, P * k:P * (k + 1)])
                                           for k in range(2) for tt in range(TT)])

                def x_values(h):
                    for s_, v_ in e.evacuations(("xp", h)):
                        pe.wait_ge(s_, v_)
                    b = opened(("xo", h), 1)
                    for k in range(2):
                        ins = pe.matmul(b[:, 0:T], xv[:, k, XK * h:XK * (h + 1)], x_pT[:, h % 3, T * k:T * (k + 1)],
                                        start=(k == 0), stop=(k == 1))
                    closed(("xo", h), ins)

                attention_pe("xa", XH, x_scores, x_moved, x_values)
                for s_, v_ in e.evacuations(*[("xo", h) for h in range(XH)]):
                    pe.wait_ge(s_, v_)
                for u in range(2):
                    w = unit("xo")
                    for tt in range(TT):
                        token_major(("xw", u, tt), w, xoT, 4, 0, 512, (tt,))
                    unit_used()
                norm_pe("n4", evacs=4)
                norm_ready("n4")

                def ffn_unit(c):
                    pe.wait_ge(dve_done, e.at("dve", ("low", c)))
                    nk = 8 if c < 2 * n_down else 2
                    unit_at["n"] += 1
                    return [t[:, c % 2, :].rearrange("p (k n) -> p k n", k=nk) for t in (w_high, w_low)]

                for c in range(2 * n_down):
                    wh, wl = ffn_unit(c)
                    key = ("fu" if c % 2 else "fg", c // 2)
                    b = opened(key, 1)
                    for m in range(2):
                        for k in range(KD):
                            o, cols = b[:, m * T:(m + 1) * T], slice(m * P, (m + 1) * P)
                            pe.matmul(o, wh[:, k, cols], h_high[:, k, :], start=(k == 0), stop=False)
                            pe.matmul(o, wh[:, k, cols], h_low[:, k, :], start=False, stop=False)
                            ins = pe.matmul(o, wl[:, k, cols], h_high[:, k, :], start=False, stop=(k == KD - 1))
                    closed(key, ins)
                out_b = {}
                for tt in range(TT):
                    for c in range(2):
                        out_b[tt, c] = opened(("fd", tt, c), 1)
                for i in range(n_down):
                    wh, wl = ffn_unit(2 * n_down + i)
                    pe.wait_ge(dve_done, e.at("dve", ("gu", i)))
                    for tt in range(TT):
                        for c in range(2):
                            o, cols = out_b[tt, c][:, :], slice(512 * c, 512 * (c + 1))
                            for k in range(2):
                                gh, gl = (t[:, 2 * i + k, P * tt:P * (tt + 1)] for t in (gu_high, gu_low))
                                pe.matmul(o, gh, wh[:, k, cols], start=(i == 0 and k == 0), stop=False)
                                pe.matmul(o, gh, wl[:, k, cols], start=False, stop=False)
                                ins = pe.matmul(o, gl, wh[:, k, cols], start=False, stop=(i == n_down - 1 and k == 1))
                            if i == n_down - 1:
                                closed(("fd", tt, c), ins)
                    if i < n_down - 1:
                        e.step(ins.then_inc(pe_done, 1), ("down", i))
                unit_skip()
                while turn[0] % BANKS:
                    turn[0] += 1

            in_layers(e, pe, layer, before=lambda: total.__setitem__(slice(None), group_base))
            prog.bank_now = [t - g for t, g in zip(total, group_base)]

        @block.scalar
        def _(act):
            e = Hand(prog, "act", bank_evac)

            before = [None]

            def norm_squares(n, src, pieces=(((), (), (0, 1), 0, D),)):
                if before[0] is not None:
                    act.wait_ge(pe_done, e.at("pe", ("group", ("nT", before[0], KD // 2 - 1))))
                before[0] = n
                for groups, steps, tts, c0, nc_ in pieces:
                    for s_, v_ in e.evacuations(*groups):
                        act.wait_ge(s_, v_)
                    for step in steps:
                        act.wait_ge(dve_done, e.at("dve", step))
                    for tt in tts:
                        ins = act.activation(xn[:, tt, c0:c0 + nc_], src[:, tt, c0:c0 + nc_], ACT.Square,
                                             accum_out=st_p[:, tt, c0 // nc_:c0 // nc_ + 1])
                        e.step(ins.then_inc(act_done, 1), ("sq", n))

            def norm_root(n):
                act.wait_ge(dve_done, e.at("dve", ("ms", n)))
                e.step(act.activation(st_c[:, :], st_b[:, :], ACT.Sqrt).then_inc(act_done, 1), ("rt", n))

            def norm_act(n, src, *pieces):
                norm_squares(n, src, *pieces)
                norm_root(n)

            def norm_evac_act(n, gain, dst=hT):
                for j in range(0, KD // 2, 2):
                    act.wait_ge(pe_done, e.at("pe", ("group", ("nT", n, j))))
                    b = banks[e.bank(("nT", n, j))]
                    for i in range(2):
                        k, src = 2 * j + i, b[:, T * i:T * (i + 1)]
                        if gain is None:
                            ins = act.activation(dst[:, k, :], src, ACT.Copy)
                        else:
                            ins = act.activation(dst[:, k, :], src, ACT.Copy, scale=vt[:, gain + k:gain + k + 1])
                        e.evacuated(("nT", n, j), ins.then_inc(bank_evac[e.bank(("nT", n, j))], 1))

            def norm_high(n, gain, dst):
                for j in range(KD // 2):
                    act.wait_ge(pe_done, e.at("pe", ("group", ("nT", n, j))))
                    b = banks[e.bank(("nT", n, j))]
                    for k in range(2 * j, 2 * j + 2):
                        ins = act.activation(dst[:, k, :], b[:, T * (k % 2):T * (k % 2 + 1)], ACT.Copy,
                                             scale=vt[:, gain + k:gain + k + 1])
                        e.evacuated(("nT", n, j), ins.then_inc(bank_evac[e.bank(("nT", n, j))], 1))

            def split_high(c):
                if c >= len(first_split):
                    return
                n = first_split[c]
                act.wait_ge(unit_ready[n % RING], 16 * slot_loads(plan1, n))
                if c >= 2:
                    act.wait_ge(pe_done, e.at("pe", ("group", before_first(c))))
                e.step(act.activation(first_high(c), ring[:, n % RING, :], ACT.Copy).then_inc(act_done, 1), ("first_high", c))

            def evac(key, dst, cols, func=ACT.Copy, p=P, src=None):
                act.wait_ge(pe_done, e.at("pe", ("group", key)))
                b = banks[e.bank(key)]
                src = b[0:p, 0:cols] if src is None else src(b)
                if len(dst.shape) == 3 and len(src.shape) == 2:
                    src = src.rearrange("p (a b) -> p a b", a=dst.shape[1])
                if len(dst.shape) == 4 and len(src.shape) == 2:
                    src = src.rearrange("p (a b c) -> p a b c", a=dst.shape[1], b=dst.shape[2])
                e.evacuated(key, act.activation(dst, src, func).then_inc(bank_evac[e.bank(key)], 1))

            def attention_act(key, nh, exps, copies, lag=2):
                for i in range(nh + lag):
                    if i < nh:
                        exps(i)
                    if i >= lag:
                        copies(i - lag)

            def causal_exps(s, slot, c0):
                for tt, (a, b) in enumerate(((0, P), (P, 3 * P))):
                    ins = act.activation(s[:, a:b], s[:, a:b], ACT.Exp, bias=a_max[:, slot, c0 + tt:c0 + tt + 1],
                                         accum_out=a_sum[:, slot, c0 + tt:c0 + tt + 1])
                    yield ins

            act.wait_ge(first_ready, 16 * FIRST_LOADS)
            norm_act("n0", x)
            split_high(0)
            for s_, v_ in e.evacuations("vt1"):
                act.wait_ge(s_, v_)
            norm_high("n0", V1["norm0"], in_high)
            split_high(1)
            for a, name in ((0, "mq"), (1, "mk")):
                for j in range(4):
                    evac((name, j), qk[:, a, :, 4 * j:4 * j + 4, :].rearrange("p t h d -> p t (h d)"), 512)
                    if 4 * a + j + 2 < 8:
                        split_high(4 * a + j + 2)
                    if name == "mk" and j == 2:
                        act.wait_ge(start_ready, 16 * START_LOADS)
                        norm_act("mem", mem_in)
            norm_evac_act("mem", None, memn)
            act.wait_ge(dve_done, e.at("dve", "reduced"))
            e.step(act.activation(sin_t[:, :], tr_b[:, :], ACT.Sin).then_inc(act_done, 1))
            e.step(act.activation(cos_t[:, :], tr_b[:, :], ACT.Sin, scale=0.5).then_inc(act_done, 1), "sines")
            act.wait_ge(dve_done, e.at("dve", ("hms", "m")))
            e.step(act.activation(hs_c[:, :], hs_b[:, :], ACT.Sqrt).then_inc(act_done, 1), ("hrt", "m"))
            for j in range(4):
                evac(("mz", j), zs[:, 2 * j:2 * j + 2, :], 512, ACT.Silu)
            for j in range(4):
                evac(("mT", 0, j), qT[:, 2 * j:2 * j + 2, :], 512)

            def m_exps(h):
                act.wait_ge(dve_done, e.at("dve", ("ma", "max", h)))
                for ins in causal_exps(sc[:, h % 3, :], h % 3, 0):
                    e.step(ins.then_inc(act_done, 1), ("ma", "exp", h))

            def m_copies(h):
                evac(("mp", h), pT[:, h % 3, 0:384], 384)

            attention_act("ma", H, m_exps, m_copies)

            def ple_act(i, key):
                norm_squares(("pl", i), x, [([(key, j)], (), (0, 1), 256 * j, 256) for j in range(4)])
                evac(("pT", i), pT.rearrange("p a b -> p (a b)")[:, 0:512], 512)
                norm_root(("pl", i))
                split_high(8 + 8 * i)
                split_high(9 + 8 * i)
                for c in range(2):
                    for tt in range(TT):
                        evac(("pj", i, c, tt), prj[:, tt, 512 * c:512 * (c + 1)], 512)
                norm_high(("pl", i), V1[f"ple{i}"], in_high)
                for j in range(4):
                    evac((("pg", i), j), g_tmp[:, j, :, :], 512, ACT.Sigmoid)
                    if j < (3 if i == 0 else 2):
                        split_high(8 + 8 * i + j + 2)

            ple_act(0, "mw")
            norm_act("n1", x, [((), [("x", 0, j)], (0, 1), 256 * j, 256) for j in range(4)])
            norm_high("n1", V1["norm1"], in_high)
            split_high(13)
            for j in range(4):
                evac(("nq", j), qk[:, 0, :, 4 * j:4 * j + 4, :].rearrange("p t h d -> p t (h d)"), 512)
                if j < 2:
                    split_high(12 + j + 2)
            def head_root(n, c):
                act.wait_ge(dve_done, e.at("dve", ("hms", n)))
                e.step(act.activation(hs_c[:, 0:c], hs_b[:, 0:c], ACT.Sqrt).then_inc(act_done, 1), ("hrt", n))

            for j in range(6):
                evac(("nk", j), kvr[:, j, :, :], 512)
                if j == 1:
                    head_root("nq", 32)
            evac(("ng", 0), gl_s[:, :, :, :], 96, ACT.Sigmoid)
            for j, n in enumerate(("ks", "kw")):
                head_root(n, 8)
                evac(("nz", j), zs[:, 2 * j:2 * j + 2, :], 512, ACT.Silu)
            for s in range(2):
                for j in range(2):
                    evac(("cx", s, j), x2[0:HD, s, 2 * j:2 * j + 2, :], 512, p=HD)
            for j in range(2, 4):
                evac(("nz", j), zs[:, 2 * j:2 * j + 2, :], 512, ACT.Silu)
            for s in range(2):
                evac(("ch", s), hid[:, s, :, :], 120, ACT.Gelu_apprx_tanh)
            evac(("cv", 0), kcf[0:NCMP, :, :], 256, p=NCMP)
            evac(("cv", 1), vcf[0:NCMP, :, :], 256, p=NCMP)
            act.wait_ge(dve_done, e.at("dve", ("hms", "kc")))
            e.step(act.activation(hs_c[0:NCMP, 0:4], hs_b[0:NCMP, 0:4], ACT.Sqrt).then_inc(act_done, 1), ("hrt", "kc"))
            for a in range(2):
                for j in range(2):
                    evac(("nkT", a, j), kT[:, 4 * a + 2 * j:4 * a + 2 * j + 2, :], 512)
            evac("ckT", kcT[:, :, 0:NCMP], 0, src=lambda b: b[:, 0:KV * NCP].rearrange("p (g n) -> p g n", g=KV)[:, :, 0:NCMP])
            for j in range(4):
                evac(("nqT", j), qT[:, 2 * j:2 * j + 2, :], 512)

            def n_exps(h):
                k = h % 3
                act.wait_ge(dve_done, e.at("dve", ("na", "max", h)))
                for tt in range(TT):
                    c = sc[:, k, 768 + NCP * tt:768 + NCP * (tt + 1)]
                    e.step(act.activation(c, c, ACT.Exp, bias=a_max[:, k, tt:tt + 1], accum_out=a_sum[:, k, tt:tt + 1]).then_inc(act_done, 1))
                for a in range(2):
                    for ins in causal_exps(sc[:, k, 384 * a:384 * (a + 1)], k, 2 + 2 * a):
                        e.step(ins.then_inc(act_done, 1), ("na", "exp", h))

            def n_copies(h):
                evac(("np", h, 0), pT[0:NCP, h % 3, 768:1024], 256, p=NCP)
                for a in range(2):
                    evac(("np", h, 1 + a), pT[:, h % 3, 384 * a:384 * (a + 1)], 384)

            attention_act("na", H, n_exps, n_copies)
            ple_act(1, "nw")
            act.wait_ge(dve_done, e.at("dve", ("x", 1)))

            def layer(l):
                e.l = l
                before[0] = None
                norm_act("n2", x)
                for s_, v_ in e.evacuations("vt2"):
                    act.wait_ge(s_, v_)
                e.step(act.activation(s5v[:, 0, :], vt[:, V2["step"]:V2["step"] + SB], ACT.Exp).then_inc(act_done, 1), "s_step")
                act.wait_ge(dve_done, e.at("dve", "lb_diff"))
                e.step(act.activation(lbt[:, 2:4, :], lbt[:, 0:2, :], ACT.Exp).then_inc(act_done, 1), "lb_exp")
                norm_evac_act("n2", V2["mix"])
                act.wait_ge(dve_done, e.at("dve", "s_reduced"))
                e.step(act.activation(s5v[:, 5, :], s5v[:, 1, :], ACT.Exp).then_inc(act_done, 1))
                e.step(act.activation(s5v[:, 6, :], s5v[:, 4, :], ACT.Sin).then_inc(act_done, 1))
                e.step(act.activation(s5v[:, 7, :], s5v[:, 4, :], ACT.Sin, scale=0.5).then_inc(act_done, 1), "s_sines")
                for j in range(2):
                    evac(("u", j), uT[:, 2 * j:2 * j + 2, :], 512)
                for i in range(2):
                    evac(("ga", i), gates[:, 2 * i:2 * i + 2, :], 512, ACT.Sigmoid)
                for s in range(2):
                    evac(("bT", s), b_T[:, s, :, :], 512)
                for s in range(2):
                    evac(("cT", s), c_T[:, s, :, :], 512)
                for i in range(2, 11):
                    if i == 8:
                        act.wait_ge(pool_done, e.at("pool", ("doubled", SHARED_DOUBLINGS[-1])))
                    evac(("ga", i), gates[:, 2 * i:2 * i + 2, :], 512, ACT.Sigmoid)
                act.wait_ge(pool_done, e.at("pool", ("state", SB - 1)))
                for j in range(2):
                    evac(("ql", j), ql[:, :, 256 * j:256 * (j + 1)], 512)
                evac(("kvl", 0), kvl[:, :, :], 512)
                evac(("kr", 0), krp[:, :, :], 64)
                for q in range(4):
                    for s_, v_ in e.evacuations(("y", q)):
                        act.wait_ge(s_, v_)
                    e.step(act.activation(sT[:, q, :], y_s[:, q, :], ACT.Gelu_apprx_tanh).then_inc(act_done, 1), "s5_gelu")
                evac(("ga", 11), gates[:, 22:24, :], 512, ACT.Sigmoid)
                for s_, v_ in e.evacuations(("ql", 0), ("ql", 1), ("kvl", 0)):
                    act.wait_ge(s_, v_)
                for tt in range(TT):
                    e.step(act.activation(mlan[:, tt, :], ql[:, tt, :], ACT.Square, accum_out=mst[:, 0, tt:tt + 1]).then_inc(act_done, 1))
                kv_sq = m_tmp.rearrange("p a b c -> p (a b c)")[:, 0:512].rearrange("p (t c) -> p t c", t=TT)
                for tt in range(TT):
                    e.step(act.activation(kv_sq[:, tt, :], kvl[:, tt, :], ACT.Square,
                                         accum_out=mst[:, 0, 2 + tt:3 + tt]).then_inc(act_done, 1), "mla_sq")
                act.wait_ge(dve_done, e.at("dve", "mla_ms"))
                e.step(act.activation(mst[:, 2, :], mst[:, 1, :], ACT.Sqrt).then_inc(act_done, 1), "mla_rt")
                for u in range(2):
                    for j in range(2):
                        m = 4 * u + 2 * j
                        evac(("gl", u, j), sgl[:, m:m + 2, :], 512, ACT.Sigmoid)
                act.wait_ge(pe_done, e.at("pe", ("group", ("qlT", 0))))
                b = banks[e.bank(("qlT", 0))]
                for i in range(2):
                    e.evacuated(("qlT", 0), act.activation(qlT[:, i, :], b[:, T * i:T * (i + 1)], ACT.Copy,
                                                      scale=vt[:, V2["q"] + i:V2["q"] + i + 1]).then_inc(bank_evac[e.bank(("qlT", 0))], 1))
                for u in range(2):
                    for tt in range(TT):
                        evac(("uq", u, tt), m_q[:, tt, 4 * u:4 * u + 4, :].rearrange("p h d -> p (h d)"), 384)
                for c in range(2):
                    for tt in range(TT):
                        evac(("ukv", c, tt), m_k[:, tt, 4 * c:4 * c + 4, 0:NOPE], 0,
                             src=lambda b: b[:, :].rearrange("p (h d) -> p h d", h=4)[:, :, 0:NOPE])
                for j in range(4):
                    evac(("mqT", j), m_qT[0:QK, 2 * j:2 * j + 2, :], 512, p=QK)

                def l_exps(h):
                    act.wait_ge(dve_done, e.at("dve", ("la", "max", h)))
                    for ins in causal_exps(m_sc[:, h % 3, :], h % 3, 0):
                        e.step(ins.then_inc(act_done, 1), ("la", "exp", h))

                def l_copies(h):
                    evac(("lp", h), m_pT[:, h % 3, 0:384], 384)

                attention_act("la", MH, l_exps, l_copies)
                for s_, v_ in e.evacuations(*[("lo", j) for j in range(4)]):
                    act.wait_ge(s_, v_)
                for j in range(2):
                    evac(("hq", j), hq[:, 2 * j:2 * j + 2, :], 512, ACT.Silu)
                for j in range(2):
                    evac(("hf", j), hb[:, 2 * j:2 * j + 2, :], 512, ACT.Sigmoid)

                def between_levels(n):
                    name, j = BETWEEN_LEVELS[n]
                    if name != "mo2":
                        dst, func = (hv, ACT.Copy) if name == "hi" else (hg, ACT.Silu)
                        evac((name, j), dst[:, :, 2 * j:2 * j + 2, :].rearrange("p t h d -> p t (h d)"), 512, func)

                act.wait_ge(dve_done, e.at("dve", "hf"))
                e.step(act.activation(hE[:, :, :], hb[:, :, :], ACT.Ln).then_inc(act_done, 1), "lnf")
                between_levels(0)
                for n, L in enumerate(LEVELS, 1):
                    act.wait_ge(dve_done, e.at("dve", ("sub", L)))
                    e.step(act.activation(hE[:, :, :], hE[:, :, :], ACT.Exp).then_inc(act_done, 1), ("hexp", L))
                    if n < len(BETWEEN_LEVELS):
                        between_levels(n)
                act.wait_ge(dve_done, e.at("dve", "hg_ms"))
                e.step(act.activation(hs_c[:, 0:8], hs_b[:, 0:8], ACT.Sqrt).then_inc(act_done, 1), "hg_rt")
                for j in range(2):
                    evac(("xk", j), xkT[:, 2 * j:2 * j + 2, :], 512)
                for j in range(2):
                    act.wait_ge(pe_done, e.at("pe", ("group", ("hoT", j))))
                    b = banks[e.bank(("hoT", j))]
                    e.evacuated(("hoT", j), act.activation(sT[:, 2 * j:2 * j + 2, :], b[:, :].rearrange("p (a b) -> p a b", a=2),
                                                      ACT.Copy, scale=vt[:, V2["hgn"]:V2["hgn"] + 1]).then_inc(bank_evac[e.bank(("hoT", j))], 1))
                for j in range(2):
                    evac(("xv", j), xv[:, :, 256 * j:256 * (j + 1)], 512)
                norm_act("n3", x, [([("wout", j)], (), (0, 1), 256 * j, 256) for j in range(4)])
                norm_evac_act("n3", V2["cross"])
                for j in range(2):
                    evac(("xq", j), xqT[:, 2 * j:2 * j + 2, :], 512)

                def x_exps(h):
                    k = h % 3
                    act.wait_ge(dve_done, e.at("dve", ("xa", "max", h)))
                    b = banks[e.bank(("xs", h))]
                    for tt in range(TT):
                        ins = act.activation(x_sc[:, k, T * tt:T * (tt + 1)], b[:, T * tt:T * (tt + 1)], ACT.Exp,
                                             bias=a_max[:, k, tt:tt + 1], scale=XK ** -0.5,
                                             accum_out=a_sum[:, k, tt:tt + 1])
                        if tt:
                            e.evacuated(("xs", h), ins.then_inc(bank_evac[e.bank(("xs", h))], 1))

                def x_copies(h):
                    evac(("xp", h), x_pT[:, h % 3, :], 512)

                attention_act("xa", XH, x_exps, x_copies)

                def ffn_high(c):
                    act.wait_ge(unit_ready[(ffn_first + c) % RING], unit_loaded(ffn_first + c, e.l))
                    act.wait_ge(pe_done, e.at("pe", before_ffn(c)))
                    e.step(act.activation(w_high[:, c % 2, :], ring[:, (ffn_first + c) % RING, :], ACT.Copy).then_inc(act_done, 1), ("high", c))

                ffn_high(0)
                ffn_high(1)
                norm_act("n4", x, [([("xw", u, tt)], (), (tt,), 512 * u, 512) for u in range(2) for tt in range(TT)])
                norm_high("n4", V2["ffn"], h_high)
                for i in range(n_down):
                    if i >= 4:
                        act.wait_ge(dve_done, e.at("dve", ("gu", i - 4)))
                    evac(("fg", i), f_tmp[:, i % 4, :], 512, ACT.Silu)
                    ffn_high(2 * i + 2)
                    ffn_high(2 * i + 3)
                    for s_, v_ in e.evacuations(("fu", i)):
                        act.wait_ge(s_, v_)
                    e.step(act.activation(gu_high[:, 2 * i:2 * i + 2, :].rearrange("p a b -> p (a b)"), f_tmp[:, i % 4, :],
                                          ACT.Copy).then_inc(act_done, 1), ("gu_high", i))
                for c in range(2 * n_down + 2, ffn_units):
                    ffn_high(c)
                for s_, v_ in e.evacuations(*[("fd", tt, c) for tt in range(TT) for c in range(2)]):
                    act.wait_ge(s_, v_)

            in_layers(e, act, layer)
            norm_act("nf", x)

        @block.vector
        def _(dve):
            e = Hand(prog, "dve", bank_evac)
            tt_, ts_, stt_ = dve.tensor_tensor, dve.tensor_scalar, dve.scalar_tensor_tensor

            def norm_dve(n, parts=1):
                dve.wait_ge(act_done, e.at("act", ("sq", n)))
                if parts > 1:
                    e.step(dve.tensor_reduce(st_a[:, :], st_p[:, :, 0:parts], AX.X, ALU.add).then_inc(dve_done, 1))
                    dve.wait_ge(dve_done, e.last())
                sums = st_a[:, :] if parts > 1 else st_p[:, :, 0]
                e.step(ts_(st_b[:, :], sums, 1.0 / D, EPS, ALU.mult, ALU.add).then_inc(dve_done, 1), ("ms", n))
                dve.wait_ge(act_done, e.at("act", ("rt", n)))
                e.step(dve.reciprocal(st_b[:, :], st_c[:, :]).then_inc(dve_done, 1))
                dve.wait_ge(dve_done, e.last())
                if n != "nf":
                    for tt in range(TT):
                        e.step(ts_(scales[:, tt, :], ident[:, :], st_b[:, tt:tt + 1], None, ALU.mult).then_inc(dve_done, 1), ("scales", n))

            def norm_low(n, gain, high, low_):
                for j in range(KD // 2):
                    dve.wait_ge(bank_evac[e.bank(("nT", n, j))], e.evac_value(("nT", n, j)) - 2)
                    b = banks[e.bank(("nT", n, j))]
                    for k in range(2 * j, 2 * j + 2):
                        ins = stt_(low_[:, k, :], b[:, T * (k % 2):T * (k % 2 + 1)], vt[:, gain + k:gain + k + 1],
                                   high[:, k, :].bitcast(F32), ALU.mult, ALU.subtract)
                        e.evacuated(("nT", n, j), ins.then_inc(bank_evac[e.bank(("nT", n, j))], 1))

            def split_low(c):
                dve.wait_ge(act_done, e.at("act", ("first_high", c)))
                e.step(tt_(first_low[:, c % 2, :], ring[:, first_split[c] % RING, :], first_high(c).bitcast(F32),
                           ALU.subtract).then_inc(dve_done, 1), ("first_low", c))

            def norm_evac_dve(n, gain, dst=hT):
                for j in range(1, KD // 2, 2):
                    dve.wait_ge(pe_done, e.at("pe", ("group", ("nT", n, j))))
                    b = banks[e.bank(("nT", n, j))]
                    for i in range(2):
                        k, src = 2 * j + i, b[:, T * i:T * (i + 1)]
                        if gain is None:
                            ins = dve.tensor_copy(dst[:, k, :], src)
                        else:
                            ins = ts_(dst[:, k, :], src, vt[:, gain + k:gain + k + 1], None, ALU.mult)
                        e.evacuated(("nT", n, j), ins.then_inc(bank_evac[e.bank(("nT", n, j))], 1))

            def evac(key, dst, cols, p=P, src=None):
                dve.wait_ge(pe_done, e.at("pe", ("group", key)))
                b = banks[e.bank(key)]
                src = b[0:p, 0:cols] if src is None else src(b)
                if len(dst.shape) == 3 and len(src.shape) == 2:
                    src = src.rearrange("p (a b) -> p a b", a=dst.shape[1])
                e.evacuated(key, dve.tensor_copy(dst, src).then_inc(bank_evac[e.bank(key)], 1))

            def reduce_angle(dst, kk, ang, mark):
                e.step(ts_(kk, ang, 1.0 / (2 * np.pi), ROUND, ALU.mult, ALU.add).then_inc(dve_done, 1))
                dve.wait_ge(dve_done, e.last())
                e.step(ts_(kk, kk, -ROUND, None, ALU.add).then_inc(dve_done, 1))
                dve.wait_ge(dve_done, e.last())
                e.step(stt_(dst, kk, -TWO_PI[0], ang, ALU.mult, ALU.add).then_inc(dve_done, 1))
                dve.wait_ge(dve_done, e.last())
                for part in TWO_PI[1:]:
                    e.step(stt_(dst, kk, -part, dst, ALU.mult, ALU.add).then_inc(dve_done, 1))
                    dve.wait_ge(dve_done, e.last())
                e.step(ts_(dst, dst, PI, -PI, ALU.min, ALU.max).then_inc(dve_done, 1), mark)
                dve.wait_ge(dve_done, e.last())

            def head_norm(n, v, p, count, gain_of, tmp_v):
                e.step(tt_(tmp_v, v, v, ALU.mult).then_inc(dve_done, 1))
                dve.wait_ge(dve_done, e.last())
                e.step(dve.tensor_reduce(hs_a[0:p, 0:count], tmp_v, AX.X, ALU.add).then_inc(dve_done, 1))
                dve.wait_ge(dve_done, e.last())
                e.step(ts_(hs_b[0:p, 0:count], hs_a[0:p, 0:count], 1.0 / HD, EPS, ALU.mult, ALU.add).then_inc(dve_done, 1), ("hms", n))
                dve.wait_ge(act_done, e.at("act", ("hrt", n)))
                e.step(dve.reciprocal(hs_a[0:p, 0:count], hs_c[0:p, 0:count]).then_inc(dve_done, 1))
                dve.wait_ge(dve_done, e.last())
                e.step(tt_(v, v, bc(hs_a[0:p, 0:count], 2, [count, HD]), ALU.mult).then_inc(dve_done, 1))
                dve.wait_ge(dve_done, e.last())
                for part, gain in gain_of:
                    e.step(tt_(part, part, bc(gains[0:p, gain, :], 1, [part.shape[1], HD]), ALU.mult).then_inc(dve_done, 1))
                dve.wait_ge(dve_done, e.last())

            def rope(v, c, s, half, t, mark):
                a, b = v.shape[1], v.shape[2]
                x1, x2_ = v[:, :, :, 0:half], v[:, :, :, half:2 * half]
                c, s = bc(c, 2, [a, b, half]), bc(s, 2, [a, b, half])
                e.step(tt_(t[0], x1, c, ALU.mult).then_inc(dve_done, 1))
                e.step(tt_(t[1], x2_, s, ALU.mult).then_inc(dve_done, 1))
                e.step(tt_(t[2], x2_, c, ALU.mult).then_inc(dve_done, 1))
                e.step(tt_(t[3], x1, s, ALU.mult).then_inc(dve_done, 1))
                dve.wait_ge(dve_done, e.last())
                e.step(tt_(x1, t[0], t[1], ALU.subtract).then_inc(dve_done, 1))
                e.step(tt_(x2_, t[2], t[3], ALU.add).then_inc(dve_done, 1), mark)
                dve.wait_ge(dve_done, e.last())

            def temps(p, a, b, half):
                return [tmp[0:p, i, 0:a * b * half].rearrange("p (a b c) -> p a b c", a=a, b=b) for i in range(4)]

            def attention_dve(key, nh, scores, sums, outs, lag=3):
                for i in range(nh + lag + 1):
                    if 0 <= i - lag - 1 < nh:
                        outs(i - lag - 1)
                    if i < nh:
                        scores(i)
                    if 1 <= i <= nh:
                        sums(i - 1)

            def causal_max(bank_key, s, slot, c0, scale):
                dve.wait_ge(pe_done, e.at("pe", ("group", bank_key)))
                b = banks[e.bank(bank_key)]
                e.evacuated(bank_key, stt_(s, b[:, 0:384], scale, causal3[:, :, :].rearrange("p a b -> p (a b)"),
                                      ALU.mult, ALU.add).then_inc(bank_evac[e.bank(bank_key)], 1))
                for s_, v_ in e.evacuations(bank_key):
                    dve.wait_ge(s_, v_)
                dve.tensor_reduce(a_max[:, slot, c0:c0 + 1], s[:, 0:P], AX.X, ALU.max, negate=True)
                return dve.tensor_reduce(a_max[:, slot, c0 + 1:c0 + 2], s[:, P:3 * P], AX.X, ALU.max, negate=True)

            dve.wait_ge(first_ready, 16 * FIRST_LOADS)
            dve.wait_ge(pe_done, e.at("pe", ("group", "vt1")))
            b = banks[e.bank("vt1")]
            e.evacuated("vt1", dve.tensor_copy(vt[:, 0:64], b[:, 0:64]).then_inc(bank_evac[e.bank("vt1")], 1))
            for s_, v_ in e.evacuations("vt1"):
                dve.wait_ge(s_, v_)
            dve.wait_ge(pool_done, e.at("pool", "ident"))
            norm_dve("n0")
            split_low(0)
            norm_low("n0", V1["norm0"], in_high, in_low)
            for c in range(1, 4):
                split_low(c)

            for c in range(4, 8):
                split_low(c)
            norm_dve("mem")
            norm_evac_dve("mem", None, memn)
            dve.wait_ge(start_ready, 16 * START_LOADS)
            dve.wait_ge(pool_done, e.at("pool", "constants"))
            e.step(dve.tensor_copy(pos_f[:, 0:5], pos_i[:, 0:5]).then_inc(dve_done, 1))
            dve.wait_ge(dve_done, e.last())
            for tt in range(TT):
                e.step(ts_(angles[:, 32 * tt:32 * tt + 32], freqs[:, 0:32], pos_f[:, tt:tt + 1], None, ALU.mult).then_inc(dve_done, 1))
                e.step(ts_(angles[:, 96 + 16 * tt:112 + 16 * tt], freqs[:, 32:48], pos_f[:, 3 + tt:4 + tt], None, ALU.mult).then_inc(dve_done, 1))
            e.step(ts_(angles[:, 64:96], freqs[:, 0:32], pos_f[:, 2:3], None, ALU.mult).then_inc(dve_done, 1))
            dve.wait_ge(dve_done, e.last())
            reduce_angle(tr_b[:, :], tr_a[:, :], angles[:, :], "reduced")
            e.step(ts_(chm_i[:, 1:2], chm_i[:, 0:1], 4, 1, ALU.logical_shift_right, ALU.bitwise_and).then_inc(dve_done, 1))
            dve.wait_ge(dve_done, e.last())
            e.step(dve.tensor_copy(chm[:, 0, 1:2], chm_i[:, 1:2]).then_inc(dve_done, 1))
            dve.wait_ge(dve_done, e.last())
            e.step(ts_(chm[:, 0, 0:1], chm[:, 0, 1:2], -1.0, 1.0, ALU.mult, ALU.add).then_inc(dve_done, 1))
            dve.wait_ge(dve_done, e.last())
            e.step(ts_(chm[:, 1, :], chm[:, 0, :], -1.0, None, ALU.mult).then_inc(dve_done, 1))
            dve.wait_ge(dve_done, e.last())
            dve.wait_ge(act_done, e.at("act", "sines"))
            e.step(tt_(cos_t[:, :], cos_t[:, :], cos_t[:, :], ALU.mult).then_inc(dve_done, 1))
            dve.wait_ge(dve_done, e.last())
            e.step(ts_(cos_t[:, :], cos_t[:, :], -2.0, 1.0, ALU.mult, ALU.add).then_inc(dve_done, 1))
            dve.wait_ge(dve_done, e.last())

            for s_, v_ in e.evacuations(*[("mq", j) for j in range(4)], *[("mk", j) for j in range(4)]):
                dve.wait_ge(s_, v_)
            qkf = qk.rearrange("p a t h d -> p (a t h d)").rearrange("p (n d) -> p n d", d=HD)
            head_norm("m", qkf, P, 64, [(qkf[:, 0:32, :], 0), (qkf[:, 32:64, :], 1)],
                      tmp.rearrange("p a b -> p (a b)").rearrange("p (n d) -> p n d", d=HD))
            for a in range(2):
                rope(qk[:, a], cos_t[:, 0:64].rearrange("p (t c) -> p t c", t=TT),
                     sin_t[:, 0:64].rearrange("p (t c) -> p t c", t=TT), 32, temps(P, TT, H, 32), ("roped", "m", a))
            for j in range(4):
                evac(("mv", j), vf[:, :, 4 * j:4 * j + 4, :].rearrange("p t h d -> p t (h d)"), 512)
            for j in range(4):
                evac(("mT", 1, j), kT[:, 2 * j:2 * j + 2, :], 512)

            def m_scores(h):
                if h >= 3:
                    dve.wait_ge(pe_done, e.at("pe", ("group", ("mp", h - 3))))
                e.step(causal_max(("ms", h), sc[:, h % 3, 0:384], h % 3, 0, HD ** -0.5).then_inc(dve_done, 1), ("ma", "max", h))

            def m_sums(h):
                dve.wait_ge(act_done, e.at("act", ("ma", "exp", h)))
                e.step(dve.reciprocal(a_rec[:, h % 3, 0:2], a_sum[:, h % 3, 0:2]).then_inc(dve_done, 1), ("ma", "rec", h))

            def gated_out(key, h):
                if h % 2:
                    j = h // 2
                    dve.wait_ge(pe_done, e.at("pe", ("group", (key, j))))
                    b = banks[e.bank((key, j))]
                    e.evacuated((key, j), tt_(oT1[:, j, :], b[:, 0:T], zs[:, j, :], ALU.mult).then_inc(bank_evac[e.bank((key, j))], 1))

            for s_, v_ in e.evacuations(*[("mz", j) for j in range(4)]):
                dve.wait_ge(s_, v_)
            attention_dve("ma", H, m_scores, m_sums, lambda h: gated_out("mo", h))

            def add_x(key, j):
                dve.wait_ge(pe_done, e.at("pe", ("group", (key, j))))
                b = banks[e.bank((key, j))]
                xs = x[:, :, 256 * j:256 * (j + 1)]
                e.evacuated((key, j), tt_(xs, xs, b[:, :].rearrange("p (t c) -> p t c", t=TT), ALU.add).then_inc(bank_evac[e.bank((key, j))], 1))

            def ple_dve(i, key):
                for j in range(4):
                    add_x(key, j)
                for s_, v_ in e.evacuations(*[(key, j) for j in range(4)]):
                    dve.wait_ge(s_, v_)
                norm_dve(("pl", i), 4)
                split_low(8 + 8 * i)
                split_low(9 + 8 * i)
                norm_low(("pl", i), V1[f"ple{i}"], in_high, in_low)
                for j in range(4):
                    if j < (3 if i == 0 else 2):
                        split_low(8 + 8 * i + j + 2)
                    for s_, v_ in e.evacuations((("pg", i), j)):
                        dve.wait_ge(s_, v_)
                    e.step(tt_(g_tmp[:, j], g_tmp[:, j], prj[:, :, 256 * j:256 * (j + 1)], ALU.mult).then_inc(dve_done, 1))
                    dve.wait_ge(dve_done, e.last())
                    xs = x[:, :, 256 * j:256 * (j + 1)]
                    e.step(tt_(xs, xs, g_tmp[:, j], ALU.add).then_inc(dve_done, 1), ("x", i))
                    e.line.mark(("x", i, j), False)
                    dve.wait_ge(dve_done, e.last())

            ple_dve(0, "mw")
            norm_dve("n1", 4)
            norm_low("n1", V1["norm1"], in_high, in_low)
            for c in range(13, 16):
                split_low(c)

            cos1, sin1 = (t[:, 0:64].rearrange("p (t c) -> p t c", t=TT) for t in (cos_t, sin_t))
            tmp_rows = tmp.rearrange("p a b -> p (a b)").rearrange("p (n d) -> p n d", d=HD)
            for s_, v_ in e.evacuations(*[("nq", j) for j in range(4)]):
                dve.wait_ge(s_, v_)
            v = qkf[:, 0:32, :]
            head_norm("nq", v, P, 32, [(v, 2)], tmp_rows[:, 0:32, :])
            rope(qk[:, 0], cos1, sin1, 32, temps(P, TT, H, 32), ("roped", "n", 0))
            for n, kind, gain in (("ks", 2, 4), ("kw", 4, 5)):
                for s_, v_ in e.evacuations(("nk", kind)):
                    dve.wait_ge(s_, v_)
                v = kvr[:, kind]
                head_norm(n, v, P, 8, [(v, gain)], tmp_rows[:, 0:8, :])
                rope(v.rearrange("p (t g) d -> p t g d", t=TT), cos1, sin1, 32, temps(P, TT, KV, 32), ("roped", n))
            for s in range(2):
                for j in range(2):
                    dve.wait_ge(pe_done, e.at("pe", ("group", ("cx", s, j))))
                    b = banks[e.bank(("cx", s, j))]
                    e.evacuated(("cx", s, j), dve.tensor_copy(
                        x2[HD:P, s, 2 * j:2 * j + 2, 0:T - 1],
                        b[HD:P, :].rearrange("p (g t) -> p g t", g=2)[:, :, 1:T]).then_inc(bank_evac[e.bank(("cx", s, j))], 1))
            for s in range(2):
                for s_, v_ in e.evacuations(("cx", s, 0), ("cx", s, 1)):
                    dve.wait_ge(s_, v_)
                for g in range(KV):
                    for a in range(2):
                        src = x2[:, s, g, 16 * a:16 * a + 240].rearrange("p (n j c) -> p j n c", n=NCMP, c=2)[:, :, :, 0]
                        c0 = V1["pe"] + 16 * s + 8 * a
                        e.step(tt_(flat_v[s][:, 8 * a:8 * a + 8, NCMP * g:NCMP * (g + 1)], src,
                                  bc(vt[:, c0:c0 + 8], 2, [8, NCMP]), ALU.add).then_inc(dve_done, 1), ("flat", s))
            for s_, v_ in e.evacuations(("cv", 0)):
                dve.wait_ge(s_, v_)
            v = kcf[0:NCMP, :, :]
            head_norm("kc", v, NCMP, KV, [(v, 3)], tmp_rows[0:NCMP, 0:KV, :])
            rope(v.unsqueeze(1), cos_t[0:NCMP, 64:96].unsqueeze(1), sin_t[0:NCMP, 64:96].unsqueeze(1), 32,
                 temps(NCMP, 1, KV, 32), None)
            e.step(dve.tensor_copy(kcd[0:NCMP], bc(v, 2, [KV, 2, HD])).then_inc(dve_done, 1), "ckv")

            def n_scores(h):
                k = h % 3
                if h >= 3:
                    dve.wait_ge(pe_done, e.at("pe", ("group", ("np", h - 3, 2))))
                dve.wait_ge(pe_done, e.at("pe", ("group", ("ns", h, 0))))
                b = banks[e.bank(("ns", h, 0))]
                e.evacuated(("ns", h, 0), stt_(sc[:, k, 768:800], b[:, 0:32], HD ** -0.5,
                                          cmp_neg.rearrange("p a b -> p (a b)"), ALU.mult, ALU.add).then_inc(bank_evac[e.bank(("ns", h, 0))], 1))
                for s_, v_ in e.evacuations(("ns", h, 0)):
                    dve.wait_ge(s_, v_)
                dve.tensor_reduce(a_max[:, k, 0:2], sc[:, k, 768:800].rearrange("p (t n) -> p t n", t=TT), AX.X, ALU.max,
                                  negate=True)
                causal_max(("ns", h, 1), sc[:, k, 0:384], k, 2, HD ** -0.5)
                e.step(causal_max(("ns", h, 2), sc[:, k, 384:768], k, 4, HD ** -0.5).then_inc(dve_done, 1), ("na", "max", h))

            def n_sums(h):
                k = h % 3
                dve.wait_ge(act_done, e.at("act", ("na", "exp", h)))
                e.step(dve.reciprocal(a_rec[:, k, :], a_sum[:, k, :]).then_inc(dve_done, 1))
                dve.wait_ge(dve_done, e.last())
                e.step(tt_(a_nrm[:, k, :].rearrange("p (b t) -> p b t", b=3), a_rec[:, k, :].rearrange("p (b t) -> p b t", b=3),
                          gl_s[:, :, h, :].rearrange("p t b -> p b t"), ALU.mult).then_inc(dve_done, 1), ("na", "rec", h))

            for s_, v_ in e.evacuations(("ng", 0), *[("nz", j) for j in range(4)]):
                dve.wait_ge(s_, v_)
            attention_dve("na", H, n_scores, n_sums, lambda h: gated_out("no", h))
            ple_dve(1, "nw")
            e.step(dve.memset(low[:, :], 0.0).then_inc(dve_done, 1))
            dve.wait_ge(dve_done, e.last())

            def layer(l):
                e.l = l
                sv = lambda i: s5v[:, i, :]
                dve.wait_ge(params_ready, 16 * PARAM_LOADS + l * 16 * PARAM_LOADS)
                e.step(dve.tensor_copy(rows[96:112, :].rearrange("p (a b) -> p a b", a=2),
                                      bc(lsr[96:112, :], 2, [2, SN])).then_inc(dve_done, 1), "log_steps")
                dve.wait_ge(pe_done, e.at("pe", ("group", "vt2")))
                b = banks[e.bank("vt2")]
                e.evacuated("vt2", dve.tensor_copy(vt[:, :], b[:, 0:P]).then_inc(bank_evac[e.bank("vt2")], 1))
                for s_, v_ in e.evacuations("vt2"):
                    dve.wait_ge(s_, v_)
                b0, b1 = vt[:, V2["lb0"]:V2["lb0"] + HH], vt[:, V2["lb1"]:V2["lb1"] + HH]
                e.step(tt_(lbt[:, 2, :], b0, b1, ALU.max).then_inc(dve_done, 1))
                dve.wait_ge(dve_done, e.last())
                e.step(tt_(lbt[:, 0, :], b0, lbt[:, 2, :], ALU.subtract).then_inc(dve_done, 1))
                e.step(tt_(lbt[:, 1, :], b1, lbt[:, 2, :], ALU.subtract).then_inc(dve_done, 1), "lb_diff")
                norm_dve("n2")
                dve.wait_ge(act_done, e.at("act", "s_step"))
                lr, li = vt[:, V2["lam_re"]:V2["lam_re"] + SB], vt[:, V2["lam_im"]:V2["lam_im"] + SB]
                e.step(tt_(sv(1), lr, sv(0), ALU.mult).then_inc(dve_done, 1))
                e.step(tt_(sv(2), li, sv(0), ALU.mult).then_inc(dve_done, 1))
                dve.wait_ge(dve_done, e.last())
                reduce_angle(sv(4), sv(3), sv(2), "s_reduced")
                norm_evac_dve("n2", V2["mix"])
                e.step(dve.memset(b_diag, 0.0).then_inc(dve_done, 1))
                e.step(tt_(sv(11), lr, lr, ALU.mult).then_inc(dve_done, 1))
                e.step(tt_(sv(12), li, li, ALU.mult).then_inc(dve_done, 1))
                dve.wait_ge(dve_done, e.last())
                e.step(tt_(sv(11), sv(11), sv(12), ALU.add).then_inc(dve_done, 1))
                dve.wait_ge(dve_done, e.last())
                dve.wait_ge(act_done, e.at("act", "s_sines"))
                e.step(tt_(sv(8), sv(7), sv(7), ALU.mult).then_inc(dve_done, 1))
                dve.wait_ge(dve_done, e.last())
                e.step(ts_(sv(8), sv(8), -2.0, 1.0, ALU.mult, ALU.add).then_inc(dve_done, 1), "s_cos")
                dve.wait_ge(dve_done, e.last())
                e.step(dve.reciprocal(sv(13), sv(11)).then_inc(dve_done, 1))
                e.step(tt_(sv(10), sv(5), sv(6), ALU.mult).then_inc(dve_done, 1))
                e.step(tt_(sv(9), sv(5), sv(8), ALU.mult).then_inc(dve_done, 1))
                dve.wait_ge(dve_done, e.last())
                e.step(ts_(sv(9), sv(9), -1.0, None, ALU.add).then_inc(dve_done, 1))
                dve.wait_ge(dve_done, e.last())
                e.step(tt_(sv(14), sv(9), lr, ALU.mult).then_inc(dve_done, 1))
                e.step(tt_(sv(15), sv(10), li, ALU.mult).then_inc(dve_done, 1))
                e.step(tt_(sv(16), sv(10), lr, ALU.mult).then_inc(dve_done, 1))
                e.step(tt_(sv(17), sv(9), li, ALU.mult).then_inc(dve_done, 1))
                dve.wait_ge(dve_done, e.last())
                e.step(tt_(sv(14), sv(14), sv(15), ALU.add).then_inc(dve_done, 1))
                e.step(tt_(sv(16), sv(16), sv(17), ALU.subtract).then_inc(dve_done, 1))
                dve.wait_ge(dve_done, e.last())
                e.step(tt_(sv(18), sv(14), sv(13), ALU.mult).then_inc(dve_done, 1))
                e.step(tt_(sv(19), sv(16), sv(13), ALU.mult).then_inc(dve_done, 1))
                dve.wait_ge(dve_done, e.last())
                cr, ci = bc(sv(18), 2, [SB, SC]), bc(sv(19), 2, [SB, SC])
                e.step(tt_(b_tmp[0], b_raw[:, 0], cr, ALU.mult).then_inc(dve_done, 1))
                e.step(tt_(b_tmp[1], b_raw[:, 1], ci, ALU.mult).then_inc(dve_done, 1))
                e.step(tt_(b_tmp[2], b_raw[:, 1], cr, ALU.mult).then_inc(dve_done, 1))
                e.step(tt_(b_tmp[3], b_raw[:, 0], ci, ALU.mult).then_inc(dve_done, 1))
                dve.wait_ge(dve_done, e.last())
                for g in range(2):
                    r = slice(SN * g, SN * (g + 1))
                    e.step(tt_(b_diag[r, 0, :, g, :], b_tmp[0][r], b_tmp[1][r], ALU.subtract).then_inc(dve_done, 1))
                    e.step(tt_(b_diag[r, 1, :, g, :], b_tmp[2][r], b_tmp[3][r], ALU.add).then_inc(dve_done, 1), "b_diag")
                for s in range(2):
                    mask = chm[:, s, :].unsqueeze(1).unsqueeze(3).to_broadcast([P, 4, 2, SN])
                    e.step(tt_(c_diag[:, s], bc(c_raw[:, s], 2, [4, 2, SN]), mask, ALU.mult).then_inc(dve_done, 1), "c_diag")
                dve.wait_ge(pe_done, e.at("pe", ("group", ("bT", 1))))
                for n in SHARED_DOUBLINGS:
                    dve.wait_ge(pool_done, e.at("pool", ("doubled", n // 2)))
                    cn, sn_ = (t[:, :, n:n + 1].to_broadcast([P, SB, n]) for t in (e_re, e_im))
                    c2, tm = e_re[:, :, n + 1:2 * n + 1], e_tmp2[:, :, 0:n]
                    e.step(tt_(c2, e_re[:, :, 1:n + 1], cn, ALU.mult).then_inc(dve_done, 1))
                    e.step(tt_(tm, e_im[:, :, 1:n + 1], sn_, ALU.mult).then_inc(dve_done, 1))
                    dve.wait_ge(dve_done, e.last())
                    e.step(tt_(c2, c2, tm, ALU.subtract).then_inc(dve_done, 1), ("re", n))
                    dve.wait_ge(dve_done, e.last())
                dve.wait_ge(pool_done, e.at("pool", ("doubled", SHARED_DOUBLINGS[-1])))
                for s_, v_ in e.evacuations(("u", 0), ("u", 1)):
                    dve.wait_ge(s_, v_)

                def y_part(q):
                    dve.wait_ge(pe_done, e.at("pe", ("group", ("y", q))))
                    b = banks[e.bank(("y", q))]
                    e.evacuated(("y", q), stt_(y_s[:, q, :], uT[:, q, :], vt[:, V2["skip"] + q:V2["skip"] + q + 1],
                                          b[:, 0:T], ALU.mult, ALU.add).then_inc(bank_evac[e.bank(("y", q))], 1))

                for blk in range(SB):
                    k = blk % 2
                    c, s = e_re[:, blk, 0:T], e_im[:, blk, 0:T]
                    if blk >= 6 and (blk - 6) % 4 == 0:
                        y_part((blk - 6) // 4)
                    dve.wait_ge(pe_done, e.at("pe", ("group", ("bu", blk))))
                    b = banks[e.bank(("bu", blk))]
                    re, im = b[:, 0:T], b[:, T:2 * T]
                    for i, (u, v) in enumerate(((re, c), (im, s), (im, c), (re, s))):
                        e.evacuated(("bu", blk), tt_(z_tm[:, i, :], u, v, ALU.mult).then_inc(bank_evac[e.bank(("bu", blk))], 1))
                    for s_, v_ in e.evacuations(("bu", blk)):
                        dve.wait_ge(s_, v_)
                    e.step(tt_(z_in[:, k, 0, :], z_tm[:, 0, :], z_tm[:, 1, :], ALU.add).then_inc(dve_done, 1))
                    e.step(tt_(z_in[:, k, 1, :], z_tm[:, 2, :], z_tm[:, 3, :], ALU.subtract).then_inc(dve_done, 1))
                    dve.wait_ge(dve_done, e.last())
                    if blk >= 2:
                        dve.wait_ge(pool_done, e.at("pool", ("state", blk - 2)))
                    rate = s5v[:, 5, blk:blk + 1].to_broadcast([P, T])
                    for i in range(2):
                        e.step(dve.tensor_tensor_scan(z_st[:, k, i, :], rate, z_in[:, k, i, :], 0.0, ALU.mult, ALU.add).then_inc(dve_done, 1), ("z", blk))
                y_part(3)

                dve.wait_ge(act_done, e.at("act", "mla_sq"))
                e.step(ts_(mst[:, 1, 0:2], mst[:, 0, 0:2], 1.0 / QR, EPS, ALU.mult, ALU.add).then_inc(dve_done, 1))
                e.step(ts_(mst[:, 1, 2:4], mst[:, 0, 2:4], 1.0 / KR, EPS, ALU.mult, ALU.add).then_inc(dve_done, 1), "mla_ms")
                dve.wait_ge(act_done, e.at("act", "mla_rt"))
                e.step(dve.reciprocal(mst[:, 1, :], mst[:, 2, :]).then_inc(dve_done, 1))
                dve.wait_ge(dve_done, e.last())
                for tt in range(TT):
                    e.step(ts_(mlan[:, tt, :], ql[:, tt, :], mst[:, 1, tt:tt + 1], None, ALU.mult).then_inc(dve_done, 1), "mla_xn")
                for tt in range(TT):
                    e.step(ts_(kvl[:, tt, :], kvl[:, tt, :], mst[:, 1, 2 + tt:3 + tt], None, ALU.mult).then_inc(dve_done, 1), "mla_kn")
                def glu_product(u):
                    for j in range(2):
                        m = 4 * (u - 2) + 2 * j
                        dve.wait_ge(pe_done, e.at("pe", ("group", ("gl", u, j))))
                        b = banks[e.bank(("gl", u, j))]
                        dve.wait_ge(pool_done, e.at("pool", ("sg", u - 2, j)))
                        e.evacuated(("gl", u, j), tt_(merged[:, m:m + 2, :], b[:, :].rearrange("p (a b) -> p a b", a=2),
                                                 sgl[:, m:m + 2, :], ALU.mult).then_inc(bank_evac[e.bank(("gl", u, j))], 1))

                glu_product(2)
                for key, dst, k0, gain in ((("qlT", 1), qlT, 2, V2["q"]), ("kvT", kvT, 0, V2["kv"])):
                    dve.wait_ge(pe_done, e.at("pe", ("group", key)))
                    b = banks[e.bank(key)]
                    for k in range(k0, k0 + 2):
                        src = b[:, T * (k - k0):T * (k - k0 + 1)]
                        e.evacuated(key, ts_(dst[:, k, :], src, vt[:, gain + k:gain + k + 1], None, ALU.mult).then_inc(bank_evac[e.bank(key)], 1))
                cos2, sin2 = (t[:, 96:128].rearrange("p (t c) -> p t c", t=TT) for t in (cos_t, sin_t))
                rt = [m_tmp[:, i, :, :].rearrange("p (a b) c -> p a b c", a=TT) for i in range(4)]
                rk = [m_tmp[:, i, 0:TT, :].unsqueeze(2) for i in range(4)]
                for s_, v_ in e.evacuations(("kr", 0)):
                    dve.wait_ge(s_, v_)
                rope(krp.unsqueeze(2), cos2, sin2, ROPE // 2, rk, None)
                e.step(dve.tensor_copy(m_k[:, :, :, NOPE:QK], bc(krp, 2, [TT, MH, ROPE])).then_inc(dve_done, 1))
                for c in range(2):
                    for tt in range(TT):
                        dve.wait_ge(pe_done, e.at("pe", ("group", ("ukv", c, tt))))
                        b = banks[e.bank(("ukv", c, tt))]
                        dve.wait_ge(bank_evac[e.bank(("ukv", c, tt))], e.evac_value(("ukv", c, tt)) - 1)
                        e.evacuated(("ukv", c, tt), dve.tensor_copy(
                            m_v[:, tt, 4 * c:4 * c + 4, :], b[:, :].rearrange("p (h d) -> p h d", h=4)[:, :, NOPE:]).then_inc(bank_evac[e.bank(("ukv", c, tt))], 1))
                for s_, v_ in e.evacuations(*[("uq", u, tt) for u in range(2) for tt in range(TT)]):
                    dve.wait_ge(s_, v_)
                rope(m_q[:, :, :, NOPE:QK], cos2, sin2, ROPE // 2, rt, "mq_roped")
                glu_product(3)
                for s_, v_ in e.evacuations(*[("ukv", c, tt) for c in range(2) for tt in range(TT)]):
                    dve.wait_ge(s_, v_)
                e.step(dve.tensor_copy(m_tmp[:, 0, 0, 0:1], krp[:, 0, 0:1]).then_inc(dve_done, 1), "mk_roped")
                for j in range(4):
                    evac(("mkT", j), m_kT[0:QK, 2 * j:2 * j + 2, :], 512, p=QK)

                def l_scores(h):
                    if h >= 3:
                        dve.wait_ge(pe_done, e.at("pe", ("group", ("lp", h - 3))))
                    e.step(causal_max(("ls", h), m_sc[:, h % 3, 0:384], h % 3, 0, QK ** -0.5).then_inc(dve_done, 1), ("la", "max", h))

                def l_sums(h):
                    dve.wait_ge(act_done, e.at("act", ("la", "exp", h)))
                    e.step(dve.reciprocal(a_rec[:, h % 3, 0:2], a_sum[:, h % 3, 0:2]).then_inc(dve_done, 1), ("la", "rec", h))

                def l_outs(h):
                    if h % 2:
                        evac(("lo", h // 2), mT[:, h // 2, :], T)

                attention_dve("la", MH, l_scores, l_sums, l_outs)

                dve.wait_ge(act_done, e.at("act", "lb_exp"))
                e.step(ts_(lbt[:, 0, :], low[:, :], -1.0, 1.0, ALU.mult, ALU.add).then_inc(dve_done, 1))
                dve.wait_ge(dve_done, e.last())
                for s_, v_ in e.evacuations(("hf", 0), ("hf", 1)):
                    dve.wait_ge(s_, v_)
                for h in range(HH):
                    e.step(ts_(hb[:, h, :], hb[:, h, :], lbt[:, 0, h:h + 1], low[:, h:h + 1], ALU.mult, ALU.add).then_inc(dve_done, 1))
                dve.wait_ge(dve_done, e.last())
                e.step(ts_(hk[:, :, :], hb[:, :, :], -1.0, 1.0, ALU.mult, ALU.add).then_inc(dve_done, 1), "hk")
                dve.wait_ge(dve_done, e.last())
                e.step(ts_(hb[:, :, :], hb[:, :, :], 2.0 ** -63, None, ALU.max).then_inc(dve_done, 1), "hf")
                dve.wait_ge(dve_done, e.last())
                dve.wait_ge(act_done, e.at("act", "lnf"))
                for h in range(HH):
                    e.step(dve.tensor_tensor_scan(hb[:, h, :], ones[:, :], hE[:, h, :], 0.0, ALU.mult, ALU.add).then_inc(dve_done, 1))
                dve.wait_ge(dve_done, e.last())
                dve.wait_ge(pool_done, e.at("pool", "h_init"))

                def take_level(n, L):
                    if L == P:
                        dve.wait_ge(pe_done, e.at("pe", ("group", ("hl", L))))
                        b = banks[e.bank(("hl", L))]
                        e.evacuated(("hl", L), dve.tensor_copy(hA[:, :, 2, :], b[:, :].rearrange("p (h t) -> p h t", h=HH)).then_inc(bank_evac[e.bank(("hl", L))], 1))
                        return
                    for half in range(2):
                        b = banks[e.bank(("hl", L, half))]
                        for i in range(2):
                            ins = dve.copy_predicated(
                                hA[:, 2 * half + i, 0:2, :], bc(level_mask[:, n, :], 1, [2, P]),
                                b[:, T * i:T * (i + 1)].rearrange("p (b c) -> p b c", b=2))
                            if i:
                                e.evacuated(("hl", L, half), ins.then_inc(bank_evac[e.bank(("hl", L, half))], 1))

                for s_, v_ in e.evacuations(("hq", 0), ("hq", 1)):
                    dve.wait_ge(s_, v_)
                for n, L in enumerate(LEVELS, 1):
                    ns = HH * T // (2 * L)
                    v = [t.rearrange("p h t -> p (h t)").rearrange("p (n l) -> p n l", n=ns)
                         for t in (hb, hE, hq, hk, hQ[:, n % 2], hKp[:, n % 2])]
                    ref = v[0][:, :, L - 1:L].to_broadcast([P, ns, L])
                    dve.wait_ge(pe_done, e.at("pe", ("group", ("hl", L // 2 if n > 1 else 0, 1))))
                    e.step(tt_(v[1][:, :, L:2 * L], v[0][:, :, L:2 * L], ref, ALU.subtract).then_inc(dve_done, 1))
                    e.step(tt_(v[1][:, :, 0:L], ref, v[0][:, :, 0:L], ALU.subtract).then_inc(dve_done, 1), ("sub", L))
                    take_level(n - 1, L // 2 if n > 1 else 0)
                    dve.wait_ge(act_done, e.at("act", ("hexp", L)))
                    e.step(tt_(v[4][:, :, L:2 * L], v[2][:, :, L:2 * L], v[1][:, :, L:2 * L], ALU.mult).then_inc(dve_done, 1))
                    e.step(tt_(v[5][:, :, 0:L], v[3][:, :, 0:L], v[1][:, :, 0:L], ALU.mult).then_inc(dve_done, 1), ("level", L))
                    dve.wait_ge(dve_done, e.last())
                    if n < len(BETWEEN_LEVELS) and BETWEEN_LEVELS[n][0] == "mo2":
                        i = BETWEEN_LEVELS[n][1]
                        product("mo2", i // 2, i % 2, 1)
                take_level(len(LEVELS), P)
                for tt in range(TT):
                    evac(("ho", tt), ho[:, tt, :, :].rearrange("p h d -> p (h d)"), 512)
                for s_, v_ in e.evacuations(("ho", 0), ("ho", 1)):
                    dve.wait_ge(s_, v_)
                of, sf, gf = (t.rearrange("p t h d -> p (t h d)").rearrange("p (n d) -> p n d", d=HK)
                              for t in (ho, hsq, hg))
                dve.wait_ge(pool_done, e.at("pool", ("mg", "mo2", 3)))
                e.step(tt_(sf, of, of, ALU.mult).then_inc(dve_done, 1))
                dve.wait_ge(dve_done, e.last())
                e.step(dve.tensor_reduce(hs_a[:, 0:8], sf, AX.X, ALU.add).then_inc(dve_done, 1))
                dve.wait_ge(dve_done, e.last())
                e.step(ts_(hs_b[:, 0:8], hs_a[:, 0:8], 1.0 / HK, EPS, ALU.mult, ALU.add).then_inc(dve_done, 1), "hg_ms")
                dve.wait_ge(act_done, e.at("act", "hg_rt"))
                e.step(dve.reciprocal(hs_a[:, 0:8], hs_c[:, 0:8]).then_inc(dve_done, 1))
                dve.wait_ge(dve_done, e.last())
                e.step(tt_(of, of, bc(hs_a[:, 0:8], 2, [8, HK]), ALU.mult).then_inc(dve_done, 1))
                dve.wait_ge(dve_done, e.last())
                for s_, v_ in e.evacuations(("hg", 0), ("hg", 1)):
                    dve.wait_ge(s_, v_)
                e.step(tt_(of, of, gf, ALU.mult).then_inc(dve_done, 1), "hg_out")
                e.step(tt_(lbt[:, 0, :], lbt[:, 2, :], lbt[:, 3, :], ALU.add).then_inc(dve_done, 1))
                dve.wait_ge(dve_done, e.last())
                e.step(dve.reciprocal(lbt[:, 1, :], lbt[:, 0, :]).then_inc(dve_done, 1))
                dve.wait_ge(dve_done, e.last())
                e.step(tt_(lbt[:, 3, :], lbt[:, 3, :], lbt[:, 1, :], ALU.mult).then_inc(dve_done, 1))
                dve.wait_ge(dve_done, e.last())
                e.step(tt_(low[:, :], low[:, :], lbt[:, 3, :], ALU.add).then_inc(dve_done, 1))
                for u in range(2):
                    for j in range(2):
                        product("ho2", u, j, 2)
                for j in range(4):
                    add_x("wout", j)
                for s_, v_ in e.evacuations(*[("wout", j) for j in range(4)]):
                    dve.wait_ge(s_, v_)
                norm_dve("n3", 4)
                norm_evac_dve("n3", V2["cross"])

                def x_scores(h):
                    k = h % 3
                    dve.wait_ge(pe_done, e.at("pe", ("group", ("xs", h))))
                    b = banks[e.bank(("xs", h))]
                    if h >= 3:
                        for s_, v_ in e.evacuations(("xs", h - 3)):
                            dve.wait_ge(s_, v_)
                    e.evacuated(("xs", h), dve.tensor_reduce(a_rec[:, k, 2:4], b[:, :].rearrange("p (t n) -> p t n", t=TT),
                                                        AX.X, ALU.max).then_inc(bank_evac[e.bank(("xs", h))], 1))
                    dve.wait_ge(bank_evac[e.bank(("xs", h))], e.evac_value(("xs", h)) - 1)
                    e.step(ts_(a_max[:, k, 0:2], a_rec[:, k, 2:4], -(XK ** -0.5), None, ALU.mult).then_inc(dve_done, 1), ("xa", "max", h))

                def x_sums(h):
                    for s_, v_ in e.evacuations(("xs", h)):
                        dve.wait_ge(s_, v_)
                    e.step(dve.reciprocal(a_rec[:, h % 3, 0:2], a_sum[:, h % 3, 0:2]).then_inc(dve_done, 1), ("xa", "rec", h))

                attention_dve("xa", XH, x_scores, x_sums, lambda h: evac(("xo", h), xoT[:, h, :], T))

                def ffn_low(c):
                    dve.wait_ge(act_done, e.at("act", ("high", c)))
                    e.step(tt_(w_low[:, c % 2, :], ring[:, (ffn_first + c) % RING, :], w_high[:, c % 2, :].bitcast(F32),
                               ALU.subtract).then_inc(dve_done, 1), ("low", c))

                ffn_low(0)
                ffn_low(1)
                for u in range(2):
                    for tt in range(TT):
                        xs = x[:, tt, 512 * u:512 * (u + 1)]
                        dve.wait_ge(pe_done, e.at("pe", ("group", ("xw", u, tt))))
                        b = banks[e.bank(("xw", u, tt))]
                        e.evacuated(("xw", u, tt), tt_(xs, xs, b[:, :], ALU.add).then_inc(bank_evac[e.bank(("xw", u, tt))], 1))
                for s_, v_ in e.evacuations(*[("xw", u, tt) for u in range(2) for tt in range(TT)]):
                    dve.wait_ge(s_, v_)
                norm_dve("n4", 2)
                norm_low("n4", V2["ffn"], h_high, h_low)
                for i in range(n_down):
                    ffn_low(2 * i + 2)
                    for s_, v_ in e.evacuations(("fg", i)):
                        dve.wait_ge(s_, v_)
                    dve.wait_ge(pe_done, e.at("pe", ("group", ("fu", i))))
                    b = banks[e.bank(("fu", i))]
                    e.evacuated(("fu", i), tt_(f_tmp[:, i % 4, :], b[:, :], f_tmp[:, i % 4, :],
                                          ALU.mult).then_inc(bank_evac[e.bank(("fu", i))], 1))
                    ffn_low(2 * i + 3)
                    dve.wait_ge(act_done, e.at("act", ("gu_high", i)))
                    gh, gl = (t[:, 2 * i:2 * i + 2, :].rearrange("p a b -> p (a b)") for t in (gu_high, gu_low))
                    e.step(tt_(gl, f_tmp[:, i % 4, :], gh.bitcast(F32), ALU.subtract).then_inc(dve_done, 1), ("gu", i))
                for c in range(2 * n_down + 2, ffn_units):
                    ffn_low(c)
                for tt in range(TT):
                    for c in range(2):
                        xs = x[:, tt, 512 * c:512 * (c + 1)]
                        dve.wait_ge(pe_done, e.at("pe", ("group", ("fd", tt, c))))
                        b = banks[e.bank(("fd", tt, c))]
                        e.evacuated(("fd", tt, c), tt_(xs, xs, b[:, :], ALU.add).then_inc(bank_evac[e.bank(("fd", tt, c))], 1))
                for s_, v_ in e.evacuations(*[("fd", tt, c) for tt in range(TT) for c in range(2)]):
                    dve.wait_ge(s_, v_)

            def product(key, u, j, branch):
                m, k = 4 * u + 2 * j, j % 2
                dve.wait_ge(pe_done, e.at("pe", ("group", (key, u, j))))
                b = banks[e.bank((key, u, j))]
                if u == 0 and branch == 1:
                    if j == 0:
                        dve.wait_ge(pool_done, e.at("pool", "h_init"))
                else:
                    dve.wait_ge(pool_done, e.at("pool", ("mg", key, 2 * u + j - 2) if u else ("mg", "mo2", 2 + j)))
                e.evacuated((key, u, j), tt_(m_tmp2[:, k, :], b[:, :], gates[:, 8 * branch + m:8 * branch + m + 2, :]
                                        .rearrange("p a b -> p (a b)"), ALU.mult).then_inc(bank_evac[e.bank((key, u, j))], 1))

            in_layers(e, dve, layer)
            norm_dve("nf")
            dve.wait_ge(out_stored, 16)
            for tt in range(TT):
                e.step(ts_(xn[:, tt, :], x[:, tt, :], st_b[:, tt:tt + 1], None, ALU.mult).then_inc(dve_done, 1))
                dve.wait_ge(dve_done, e.last())
                e.step(tt_(xn[:, tt, :], xn[:, tt, :], nfin, ALU.mult).then_inc(dve_done, 1), "final")

        @block.gpsimd
        def _(pool):
            e = Hand(prog, "pool", bank_evac)

            def select(out, pattern, base, cm, fill, op=ALU.is_ge):
                e.step(pool.affine_select(out=out, in_=out, compare_op=op, fill=fill, base=base,
                                             pattern=pattern, channel_multiplier=cm).then_inc(pool_done, 1))
                pool.wait_ge(pool_done, e.last())

            e.step(pool.memset(rows[:, :], 0.0).then_inc(pool_done, 1), "rows_clear")
            e.step(pool.memset(ident[:, :], 0.0).then_inc(pool_done, 1))
            pool.wait_ge(pool_done, e.last())
            select(ident[:, :], [[-1, P]], 0, 1, 1.0, ALU.not_equal)
            e.line.mark("ident", False)
            e.step(pool.iota(pos_i[:, 0:2], [[P, TT]], base=0, channel_multiplier=1).then_inc(pool_done, 1))
            e.step(pool.iota(pos_i[:, 2:3], [[0, 1]], base=CL - 1, channel_multiplier=CS).then_inc(pool_done, 1))
            e.step(pool.iota(chm_i[:, 0:1], [[0, 1]], base=0, channel_multiplier=1).then_inc(pool_done, 1))
            for n, half in ((0, HD // 2), (32, ROPE // 2)):
                f = np.float32(10000.0) ** (-np.arange(half, dtype=np.float32) / np.float32(half))
                for i in range(half):
                    e.step(pool.memset(freqs[:, n + i:n + i + 1], float(f[i])).then_inc(pool_done, 1))
            e.step(pool.memset(ones[:, :], 1.0).then_inc(pool_done, 1))
            e.step(pool.memset(causal3[:, :, :], 0.0).then_inc(pool_done, 1))
            e.step(pool.memset(cmp_neg, 0.0).then_inc(pool_done, 1))
            e.step(pool.memset(cmp_on, 1.0).then_inc(pool_done, 1))
            e.step(pool.memset(kcT, 0.0).then_inc(pool_done, 1))
            e.step(pool.memset(vcf, 0.0).then_inc(pool_done, 1))
            pool.wait_ge(pool_done, e.last())
            for i in (0, 2):
                select(causal3[:, i, :], [[-1, P]], 0, 1, NEG)
            for m, fill in ((cmp_neg, NEG), (cmp_on, 0.0)):
                select(m, [[P, TT], [-CS, NCP]], -(CL - 1), 1, fill)
                e.step(pool.memset(m[:, :, NCMP:], fill).then_inc(pool_done, 1))
                pool.wait_ge(pool_done, e.last())
            e.step(pool.memset(level_mask[:, :, :], 0).then_inc(pool_done, 1))
            pool.wait_ge(pool_done, e.last())
            for n, L in enumerate([0] + LEVELS[:-1]):
                if L == 0:
                    select(level_mask[:, 0, :], [[-1, P]], 0, 1, 1.0, ALU.not_equal)
                    continue
                ns = P // (2 * L)
                odd = level_mask[:, n, :].rearrange("p (n l) -> p n l", n=ns)[:, :, L:2 * L]
                e.step(pool.memset(odd, 1).then_inc(pool_done, 1))
                pool.wait_ge(pool_done, e.last())
                select(odd, [[-2 * L, ns], [0, L]], 0, 1, 0.0)
                select(odd, [[2 * L, ns], [0, L]], L - 1, -1, 0.0)
            e.line.mark("constants", False)

            def scaled(out, src, col):
                return pool.tensor_tensor(out, src, col.to_broadcast([P, src.shape[1]]), ALU.mult)

            def normalise(s, slot, c0, norm, mark):
                for tt, (a, b) in enumerate(((0, P), (P, 3 * P))):
                    e.step(scaled(s[:, a:b], s[:, a:b], norm[:, slot, c0 + tt:c0 + tt + 1]).then_inc(pool_done, 1), mark)

            def whole_input(n):
                for s_, v_ in e.evacuations(*[("nT", n, j) for j in range(KD // 2)]):
                    pool.wait_ge(s_, v_)
                e.step(pool.tensor_tensor(hT[:, :, :], in_high[:, :, :].bitcast(F32), in_low[:, :, :].bitcast(F32),
                                          ALU.add).then_inc(pool_done, 1), ("hT", n))

            whole_input("n0")
            for h in range(H):
                pool.wait_ge(dve_done, e.at("dve", ("ma", "rec", h)))
                normalise(sc[:, h % 3, 0:384], h % 3, 0, a_rec, ("ma", "norm", h))
            whole_input("n1")
            for s in range(2):
                for s_, v_ in e.evacuations(("nk", s)):
                    pool.wait_ge(s_, v_)
                e.step(pool.tensor_copy(dup[:, s], bc(kvr[:, s], 2, [TT * KV, 2, HD])).then_inc(pool_done, 1), ("dup", s))
            for a, n in enumerate(("ks", "kw")):
                pool.wait_ge(dve_done, e.at("dve", ("roped", n)))
                pool.wait_ge(pe_done, e.at("pe", ("group", ("cx", a, 1))))
                e.step(pool.tensor_copy(dup[:, a], bc(kvr[:, 2 + 2 * a], 2, [TT * KV, 2, HD])).then_inc(pool_done, 1), ("dup", 2 + a))
            for h in range(H):
                k = h % 3
                pool.wait_ge(dve_done, e.at("dve", ("na", "rec", h)))
                c = sc[:, k, 768:800].rearrange("p (t n) -> p t n", t=TT)
                e.step(pool.tensor_tensor(c, c, cmp_on, ALU.mult).then_inc(pool_done, 1))
                pool.wait_ge(pool_done, e.last())
                for tt in range(TT):
                    ct = sc[:, k, 768 + NCP * tt:768 + NCP * (tt + 1)]
                    e.step(pool.tensor_scalar(ct, ct, a_nrm[:, k, tt:tt + 1], None, ALU.mult).then_inc(pool_done, 1))
                for a in range(2):
                    normalise(sc[:, k, 384 * a:384 * (a + 1)], k, 2 + 2 * a, a_nrm, ("na", "norm", h))
            pool.wait_ge(dve_done, e.at("dve", ("x", 1)))

            def layer(l):
                e.l = l
                pool.wait_ge(dve_done, e.at("dve", "s_cos"))
                e.step(pool.tensor_tensor(e_re[:, :, 0:1], ones[:, 0:SB].unsqueeze(2), ones[:, 0:SB].unsqueeze(2), ALU.mult).then_inc(pool_done, 1))
                e.step(pool.tensor_tensor(e_im[:, :, 0:1], causal3[:, 1, 0:SB].unsqueeze(2),
                                         causal3[:, 1, 0:SB].unsqueeze(2), ALU.add).then_inc(pool_done, 1))
                e.step(pool.tensor_copy(e_re[:, :, 1:2], s5v[:, 8, :].unsqueeze(2)).then_inc(pool_done, 1))
                e.step(pool.tensor_copy(e_im[:, :, 1:2], s5v[:, 6, :].unsqueeze(2)).then_inc(pool_done, 1))
                pool.wait_ge(pool_done, e.last())
                n = 1
                while n < T:
                    cn, sn_ = (t[:, :, n:n + 1].to_broadcast([P, SB, n]) for t in (e_re, e_im))
                    c1, s1 = e_re[:, :, 1:n + 1], e_im[:, :, 1:n + 1]
                    c2, s2 = e_re[:, :, n + 1:2 * n + 1], e_im[:, :, n + 1:2 * n + 1]
                    tm = e_tmp[:, :, 0:n]
                    if n in SHARED_DOUBLINGS:
                        if n != SHARED_DOUBLINGS[0]:
                            pool.wait_ge(dve_done, e.at("dve", ("re", n // 2)))
                    else:
                        e.step(pool.tensor_tensor(c2, c1, cn, ALU.mult).then_inc(pool_done, 1))
                        e.step(pool.tensor_tensor(tm, s1, sn_, ALU.mult).then_inc(pool_done, 1))
                        pool.wait_ge(pool_done, e.last())
                        e.step(pool.tensor_tensor(c2, c2, tm, ALU.subtract).then_inc(pool_done, 1))
                        pool.wait_ge(pool_done, e.last())
                    e.step(pool.tensor_tensor(s2, s1, cn, ALU.mult).then_inc(pool_done, 1))
                    e.step(pool.tensor_tensor(tm, c1, sn_, ALU.mult).then_inc(pool_done, 1))
                    pool.wait_ge(pool_done, e.last())
                    e.step(pool.tensor_tensor(s2, s2, tm, ALU.add).then_inc(pool_done, 1), ("doubled", n))
                    pool.wait_ge(pool_done, e.last())
                    n *= 2
                for blk in range(SB):
                    k = blk % 2
                    c, s = e_re[:, blk, 0:T], e_im[:, blk, 0:T]
                    pool.wait_ge(dve_done, e.at("dve", ("z", blk)))
                    zr, zi = z_st[:, k, 0, :], z_st[:, k, 1, :]
                    for i, (u, v) in enumerate(((zr, c), (zi, s), (zi, c), (zr, s))):
                        ins = pool.tensor_tensor(x_tm[:, i, :], u, v, ALU.mult)
                        e.step(ins.then_inc(pool_done, 1))
                    pool.wait_ge(pool_done, e.last())
                    if blk >= 2:
                        pool.wait_ge(pe_done, e.at("pe", ("s5_out", blk - 2)))
                    e.step(pool.tensor_tensor(x_st[:, k, 0, :], x_tm[:, 0, :], x_tm[:, 1, :], ALU.subtract).then_inc(pool_done, 1))
                    e.step(pool.tensor_tensor(x_st[:, k, 1, :], x_tm[:, 2, :], x_tm[:, 3, :], ALU.add).then_inc(pool_done, 1), ("state", blk))
                    pool.wait_ge(pool_done, e.last())
                for u in range(2):
                    for j in range(2):
                        m = 4 * u + 2 * j
                        for s_, v_ in e.evacuations(("gl", u, j)):
                            pool.wait_ge(s_, v_)
                        e.step(pool.tensor_tensor(sgl[:, m:m + 2, :], sgl[:, m:m + 2, :], gates[:, m:m + 2, :], ALU.mult).then_inc(pool_done, 1), ("sg", u, j))
                for h in range(MH):
                    pool.wait_ge(dve_done, e.at("dve", ("la", "rec", h)))
                    normalise(m_sc[:, h % 3, 0:384], h % 3, 0, a_rec, ("la", "norm", h))
                pool.wait_ge(pe_done, e.at("pe", ("group", ("lo", 3))))
                for buf, n in ((hQ, 2 * HH * T), (hKp, 2 * HH * T), (hA, HH * 3 * P)):
                    flat_buf = buf.rearrange("p a b c -> p (a b c)")
                    zeros = causal3[:, 1, 0:1].to_broadcast([P, n])
                    e.step(pool.tensor_tensor(flat_buf, zeros, zeros, ALU.add).then_inc(pool_done, 1), "h_init")

                def add_merged(key):
                    for u in range(2):
                        for j in range(2):
                            m = 4 * u + 2 * j
                            for s_, v_ in e.evacuations((key, u, j)):
                                pool.wait_ge(s_, v_)
                            mv = merged[:, m:m + 2, :].rearrange("p a b -> p (a b)")
                            e.step(pool.tensor_tensor(mv, mv, m_tmp2[:, j % 2, :], ALU.add).then_inc(pool_done, 1), ("mg", key, 2 * u + j))
                            pool.wait_ge(pool_done, e.last())

                for u in range(2, 4):
                    for s_, v_ in e.evacuations(("gl", u, 0), ("gl", u, 1)):
                        pool.wait_ge(s_, v_)
                add_merged("mo2")
                pool.wait_ge(dve_done, e.at("dve", ("level", P)))
                for k in range(KD):
                    e.step(scaled(memT[:, k, :], memn[:, k, :], vt[:, V2["mem"] + k:V2["mem"] + k + 1]).then_inc(pool_done, 1), "memT")
                add_merged("ho2")
                for h in range(XH):
                    k = h % 3
                    pool.wait_ge(dve_done, e.at("dve", ("xa", "rec", h)))
                    for tt in range(TT):
                        s = x_sc[:, k, T * tt:T * (tt + 1)]
                        e.step(scaled(s, s, a_rec[:, k, tt:tt + 1]).then_inc(pool_done, 1), ("xa", "norm", h))

            in_layers(e, pool, layer)

        @block.sync
        def _(sp):
            e = Hand(prog, "sp", bank_evac)

            def start(dst, src, **how):
                sp.dma_start(dst, src, **how).then_inc(start_ready, 16)
                loads.append(1)

            def first(dst, src):
                sp.dma_start(dst, src).then_inc(first_ready, 16)
                loads.append(1)

            def param(dst, src):
                sp.dma_start(dst, src).then_inc(params_ready, 16)
                loads.append(1)

            def row_view(v):
                return v.rearrange("(r c) -> r c", c=P)

            def load_unit(plan, n, before):
                if plan[n] is None:
                    return
                if before is not None:
                    if before[0] == "unit" and before[1] and before[2] in first_split:
                        sp.wait_ge(dve_done, e.at("dve", ("first_low", first_split.index(before[2]))))
                    elif before[0] == "unit" and not before[1] and is_split(before[2]):
                        sp.wait_ge(dve_done, e.at("dve", ("low", before[2] - ffn_first)))
                    else:
                        sp.wait_ge(pe_done, e.at("pe", before))
                _, (nk, nc_), src = plan[n]
                s = n % RING
                sp.dma_start(ring[:, s, 0:nk * nc_].rearrange("p (k n) -> p k n", k=nk), src).then_inc(unit_ready[s], 16)

            loads = []
            first(x[:, :, :], A["x"][0].rearrange("(t p) d -> p t d", p=P))
            sp.wait_ge(pool_done, e.at("pool", "rows_clear"))
            first(rows[0:16, :], A["norm_gain"].rearrange("l (r c) -> (l r) c", c=P))
            first(rows[16:32, :], A["ple_gate_gain"].rearrange("l (r c) -> (l r) c", c=P))
            first(rows[32:64, :], A["nsa_cmp_pe"][0].rearrange("s (j i) d -> (s j) (i d)", i=2))
            assert len(loads) == FIRST_LOADS
            loads.clear()
            for n in range(RING):
                load_unit(plan1, n, None)
            start(mem_in, A["mem_2"][0].rearrange("(t p) d -> p t d", p=P))
            for i, (name, n) in enumerate((("moba_q_gain", 1), ("moba_k_gain", 1), ("nsa_q_gain", 1), ("nsa_k_gain", 3))):
                src = A[name].rearrange("a d -> a d") if n == 1 else A[name].rearrange("a b d -> a (b d)")
                start(gains[:, i:i + n, :].rearrange("p a b -> p (a b)"), src.to_broadcast([P, n * HD]))
            start(pos_i[:, 3:5], A["positions_2"][0].rearrange("(t p) -> p t", p=P),
                  allow_slow_non_contiguous=True)
            start(w2s, A["nsa_cmp_w2"][0].rearrange("s (k p) d -> p s k d", p=P))
            for i in range(2):
                start(p_in[:, i], A["p"][i, 0].rearrange("(t p) d -> p t d", p=P))
            assert len(loads) == START_LOADS
            def params(l):
                loads.clear()
                for c, n, v in ((V2["mix"], 8, "norm_mix_2"), (V2["cross"], 8, "norm_cross_2"), (V2["mem"], 8, "norm_mem_2"),
                                (V2["ffn"], 8, "norm_ffn_2"), (V2["q"], 4, "mla_q_norm_2"), (V2["kv"], 2, "mla_kv_norm_2"),
                                (V2["hgn"], 1, "hg_g_norm_2")):
                    param(rows[c:c + n, :], row_view(A[v][l]))
                for i in range(DEPTH):
                    param(rows[V2["lb0"] + 4 * i:V2["lb0"] + 4 * i + 4, :], row_view(A["hg_lb_2"][i]))
                param(rows[V2["skip"]:V2["skip"] + 4, :], A["ssm_d_2"][l].rearrange("(q g) c -> q (g c)", q=4))
                for c, v in ((V2["lam_re"], "ssm_lam_re_2"), (V2["lam_im"], "ssm_lam_im_2")):
                    param(rows[c:c + SB, :], A[v][l].rearrange("(b g) n -> b (g n)", g=2))
                param(lsr[96:112, :], A["ssm_log_step_2"][l].rearrange("(b g) -> b g", g=2))
                for i, v in enumerate(("ssm_b_re_2", "ssm_b_im_2")):
                    param(b_raw[:, i], A[v][l].rearrange("(b g) n c -> (g n) b c", g=2))
                for i, v in enumerate(("ssm_c_re_2", "ssm_c_im_2")):
                    param(c_raw[:, i], A[v][l].rearrange("(q g) c n -> (g c) q n", q=4))
                assert len(loads) == PARAM_LOADS

            early = last_unit(plan1) - 2
            for n in range(RING, len(plan1)):
                if n == early:
                    sp.wait_ge(pe_done, e.at("pe", ("group", ("no", KD - 1))))
                    params(0)
                load_unit(plan1, n, ("unit", True, n - RING))
            n_layer = len(plan2[0])
            late = n_layer - 4
            prev = lambda n: ("unit", True, len(plan1) + n - RING)
            for l in range(DEPTH):
                for n in range(n_layer):
                    if n >= RING:
                        e.l = l
                        load_unit(plan2[l], n, ("unit", False, n - RING))
                    elif l == 0:
                        load_unit(plan2[l], n, used(prev(n), plan1))
                    else:
                        e.l = l - 1
                        load_unit(plan2[l], n, used(("unit", False, n_layer + n - RING), plan2[0]))
                    if n == late and l + 1 < DEPTH:
                        e.l = l
                        for s_, v_ in e.evacuations(("fu", FF // 256 - 1)):
                            sp.wait_ge(s_, v_)
                        params(l + 1)
            e.l = DEPTH - 1
            sp.wait_ge(pe_done, e.at("pe", ("group", ("fu", FF // 256 - 1))))
            sp.dma_start(nfin, A["norm_final_2"].rearrange("(a d) -> a d", a=1).to_broadcast([P, D])).then_inc(out_stored, 16)
            sp.wait_ge(dve_done, e.at("dve", "final"))
            sp.dma_start(out.rearrange("a (t p) d -> p (a t) d", p=P), xn[:, :, :]).then_inc(out_stored, 16)
            sp.wait_ge(out_stored, 32)

        if known:
            for key, want in prog.evacs.items():
                if isinstance(key, tuple) and key[0] == "want":
                    assert prog.evacs.get(key[1], 0) == want, (key, prog.evacs.get(key[1]))

    return {"lines": {n: {"marks": v.marks, "layer": v.layer_now} for n, v in prog.lines.items()},
            "bank_layer": prog.bank_now, "groups": prog.groups}


_INS = ["x", "p", "norm_gain", "moba_w_in", "moba_q_gain", "moba_k_gain", "moba_w_out", "nsa_w_in", "nsa_q_gain",
        "nsa_k_gain", "nsa_cmp_pe", "nsa_cmp_w1", "nsa_cmp_w2", "nsa_w_out", "ple_w_proj", "ple_gate_gain",
        "ple_w_gate", "mem_2", "positions_2", "norm_mix_2", "w_in_2", "ssm_lam_re_2", "ssm_lam_im_2", "ssm_b_re_2",
        "ssm_b_im_2", "ssm_c_re_2", "ssm_c_im_2", "ssm_d_2", "ssm_log_step_2", "ssm_w_glu_2", "mla_q_norm_2",
        "mla_kv_norm_2", "mla_w_uq_2", "mla_w_ukv_2", "mla_w_o_2", "hg_lb_2", "hg_g_norm_2", "hg_w_o_2", "w_out_2",
        "norm_cross_2", "norm_mem_2", "x_w_q_2", "x_w_kv_2", "x_w_o_2", "norm_ffn_2", "ffn_w_gate_up_2",
        "ffn_w_down_2", "norm_final_2"]


def kernel(**inputs):
    import concourse.bacc as _bacc
    from concourse.bass_utils import run_bass_kernel_spmd as _run

    arrays = {f"in_{name}_dram": np.ascontiguousarray(inputs[name]) for name in _INS}
    known = None
    for _ in range(2):
        nc = _bacc.Bacc("TRN2", target_bir_lowering=False, num_devices=1)
        A = {}
        for name in _INS:
            a = arrays[f"in_{name}_dram"]
            A[name] = nc.dram_tensor(f"in_{name}_dram", a.shape, mybir.dt.from_np(a.dtype), kind="ExternalInput").ap()
        out = nc.dram_tensor("out_0_dram", (1, T, D), F32, kind="ExternalOutput").ap()
        known = build(nc, A, out, known)
    r = _run(nc, [arrays], core_ids=[0])
    return r.results[0]["out_0_dram"]
```
